# Optimizing a Trainium2 kernel written in Bass

```python
import math
import jax, jax.numpy as jnp
from jax import lax
import numpy as np

D_MODEL = 1024
BATCH = 1
SEQ = 256
DEPTH = 2

CHUNK = 64
Q_BLOCK = 128
HEAD_DIM = 64
N_DIFF_HEADS = D_MODEL // (2 * HEAD_DIM)
ROT_DIM = HEAD_DIM // 4
ROPE_THETA = 500000.0
CONV_WIDTH = 31
N_GROUPS = 4
EXPERTS_PER_GROUP = 8
N_EXPERTS = N_GROUPS * EXPERTS_PER_GROUP
EXPERT_TOPK = 2
D_EXPERT = D_MODEL // 2
N_MIXERS = 2
N_A = (DEPTH + 1) // 2
N_B = DEPTH // 2
EPS = 1e-6

kernel_name = "hybrid_diffattn_conformer_hmoe"

def rms_norm(x, g, eps=EPS):
    xf = x.astype(jnp.float32)
    y = xf * lax.rsqrt(jnp.mean(xf * xf, axis=-1, keepdims=True) + eps)
    return (y * g.astype(jnp.float32)).astype(x.dtype)

def layer_norm(x, g, b, eps=EPS):
    xf = x.astype(jnp.float32)
    mu = jnp.mean(xf, axis=-1, keepdims=True)
    xc = xf - mu
    var = jnp.mean(xc * xc, axis=-1, keepdims=True)
    y = xc * lax.rsqrt(var + eps) * g.astype(jnp.float32) + b.astype(jnp.float32)
    return y.astype(x.dtype)

def rope_tables(seq, dtype):
    pos = jnp.arange(seq, dtype=jnp.float32)
    inv_freq = ROPE_THETA ** (-jnp.arange(0, ROT_DIM, 2, dtype=jnp.float32) / ROT_DIM)
    ang = pos[:, None] * inv_freq[None, :]
    return jnp.cos(ang).astype(dtype), jnp.sin(ang).astype(dtype)

def partial_rope(x, cos, sin):
    c = cos[None, :, None, None, :]
    s = sin[None, :, None, None, :]
    half = ROT_DIM // 2
    x1 = x[..., :half]
    x2 = x[..., half:ROT_DIM]
    return jnp.concatenate([x1 * c - x2 * s, x2 * c + x1 * s, x[..., ROT_DIM:]], axis=-1)

def diff_attention(h, w_in, q_gain, k_gain, lq1, lk1, lq2, lk2, subln_g, w_out, lambda_init, cos, sin):
    B, S, D = h.shape
    H, DH = N_DIFF_HEADS, HEAD_DIM
    qkv = h @ w_in
    q = qkv[..., :D].reshape(B, S, H, 2, DH)
    k = qkv[..., D:2 * D].reshape(B, S, H, 2, DH)
    v = qkv[..., 2 * D:].reshape(B, S, H, 2 * DH)
    q = partial_rope(rms_norm(q, q_gain), cos, sin)
    k = partial_rope(rms_norm(k, k_gain), cos, sin)
    f32 = jnp.float32
    lam = (jnp.exp(jnp.sum(lq1.astype(f32) * lk1.astype(f32)))
           - jnp.exp(jnp.sum(lq2.astype(f32) * lk2.astype(f32))) + lambda_init)
    nb = S // Q_BLOCK
    q_blocks = jnp.moveaxis(q.reshape(B, nb, Q_BLOCK, H, 2, DH), 1, 0)
    key_chunk = jnp.arange(S) // CHUNK
    scale = DH ** -0.5

    def attend_block(args):
        qb, bi = args
        q_chunk = (bi * Q_BLOCK + jnp.arange(Q_BLOCK)) // CHUNK
        mask = key_chunk[None, :] <= q_chunk[:, None]
        s = jnp.einsum('bqhcd,bkhcd->bhcqk', qb, k).astype(f32) * scale
        s = jnp.where(mask, s, -jnp.inf)
        p = jax.nn.softmax(s, axis=-1)
        a = p[:, :, 0] - lam * p[:, :, 1]
        return jnp.einsum('bhqk,bkhe->bqhe', a.astype(v.dtype), v)

    o = lax.map(attend_block, (q_blocks, jnp.arange(nb)))
    o = jnp.moveaxis(o, 0, 1).reshape(B, S, H, 2 * DH)
    o = rms_norm(o, subln_g) * (1.0 - lambda_init)
    return o.reshape(B, S, D) @ w_out

def conformer_conv(h, w_in, b_in, dw_w, dw_b, ln_g, ln_b, w_out, b_out):
    D = h.shape[-1]
    a, g = jnp.split(h @ w_in + b_in, 2, axis=-1)
    u = a * jax.nn.sigmoid(g)
    u = lax.conv_general_dilated(
        u, dw_w[:, None, :].astype(u.dtype), window_strides=(1,),
        padding=[(CONV_WIDTH - 1, 0)],
        dimension_numbers=('NWC', 'WIO', 'NWC'),
        feature_group_count=D) + dw_b
    u = jax.nn.silu(layer_norm(u, ln_g, ln_b))
    return u @ w_out + b_out

def hier_moe(h, w_rg, b_rg, w_re, b_re, w_gate, w_up, w_down):
    B, S, D = h.shape
    t = h.reshape(B * S, D)
    f32 = jnp.float32
    g_prob = jax.nn.softmax((t @ w_rg + b_rg).astype(f32), axis=-1)
    g_p, g_idx = lax.top_k(g_prob, 1)
    e_all = (jnp.einsum('nd,gde->nge', t, w_re) + b_re).astype(f32)
    e_logits = jnp.einsum('nge,ng->ne', e_all, jax.nn.one_hot(g_idx[:, 0], N_GROUPS, dtype=f32))
    e_top, e_idx = lax.top_k(e_logits, EXPERT_TOPK)
    w = g_p * jax.nn.softmax(e_top, axis=-1)
    flat_id = g_idx * EXPERTS_PER_GROUP + e_idx
    combine = jnp.sum(jax.nn.one_hot(flat_id, N_EXPERTS, dtype=f32) * w[..., None], axis=1)
    combine = combine.astype(t.dtype)
    y = jnp.zeros_like(t)
    for e in range(N_EXPERTS):
        hid = jax.nn.silu(t @ w_gate[e]) * (t @ w_up[e])
        y = y + combine[:, e:e + 1] * (hid @ w_down[e])
    return y.reshape(B, S, D)

def setup_inputs(seed: int = 0) -> dict:
    key = jax.random.key(seed)
    ks = iter(jax.random.split(key, 40))
    D, DH, F, G, E, NE = D_MODEL, HEAD_DIM, D_EXPERT, N_GROUPS, EXPERTS_PER_GROUP, N_EXPERTS

    def nrm(shape, scale):
        return jax.random.normal(next(ks), shape, jnp.float32) * scale

    def gain(shape):
        return 1.0 + nrm(shape, 0.02)

    return {
        "x": nrm((BATCH, SEQ, D), 1.0),
        "attn_norm": gain((N_A, D)),
        "diff_w_in": nrm((N_A, D, 3 * D), D ** -0.5),
        "diff_q_gain": gain((N_A, DH)),
        "diff_k_gain": gain((N_A, DH)),
        "diff_lambda_q1": nrm((N_A, DH), 0.1),
        "diff_lambda_k1": nrm((N_A, DH), 0.1),
        "diff_lambda_q2": nrm((N_A, DH), 0.1),
        "diff_lambda_k2": nrm((N_A, DH), 0.1),
        "diff_subln": gain((N_A, 2 * DH)),
        "diff_w_out": nrm((N_A, D, D), D ** -0.5),
        "conv_norm": gain((N_B, D)),
        "conv_w_in": nrm((N_B, D, 2 * D), D ** -0.5),
        "conv_b_in": nrm((N_B, 2 * D), 0.02),
        "conv_dw_w": nrm((N_B, CONV_WIDTH, D), CONV_WIDTH ** -0.5),
        "conv_dw_b": nrm((N_B, D), 0.02),
        "conv_ln_g": gain((N_B, D)),
        "conv_ln_b": nrm((N_B, D), 0.02),
        "conv_w_out": nrm((N_B, D, D), D ** -0.5),
        "conv_b_out": nrm((N_B, D), 0.02),
        "ffn_norm": gain((DEPTH, D)),
        "router_group_w": nrm((DEPTH, D, G), D ** -0.5),
        "router_group_b": nrm((DEPTH, G), 0.01),
        "router_expert_w": nrm((DEPTH, G, D, E), D ** -0.5),
        "router_expert_b": nrm((DEPTH, G, E), 0.01),
        "moe_w_gate": nrm((DEPTH, NE, D, F), D ** -0.5),
        "moe_w_up": nrm((DEPTH, NE, D, F), D ** -0.5),
        "moe_w_down": nrm((DEPTH, NE, F, D), F ** -0.5),
    }

def reference(x, attn_norm, diff_w_in, diff_q_gain, diff_k_gain, diff_lambda_q1, diff_lambda_k1,
              diff_lambda_q2, diff_lambda_k2, diff_subln, diff_w_out,
              conv_norm, conv_w_in, conv_b_in, conv_dw_w, conv_dw_b, conv_ln_g, conv_ln_b,
              conv_w_out, conv_b_out,
              ffn_norm, router_group_w, router_group_b, router_expert_w, router_expert_b,
              moe_w_gate, moe_w_up, moe_w_down):
    cos, sin = rope_tables(x.shape[1], x.dtype)
    for i in range(DEPTH):
        j = i // N_MIXERS
        if i % N_MIXERS == 0:
            lambda_init = 0.8 - 0.6 * math.exp(-0.3 * i)
            x = x + diff_attention(
                rms_norm(x, attn_norm[j]), diff_w_in[j], diff_q_gain[j], diff_k_gain[j],
                diff_lambda_q1[j], diff_lambda_k1[j], diff_lambda_q2[j], diff_lambda_k2[j],
                diff_subln[j], diff_w_out[j], lambda_init, cos, sin)
        else:
            x = x + conformer_conv(
                rms_norm(x, conv_norm[j]), conv_w_in[j], conv_b_in[j], conv_dw_w[j], conv_dw_b[j],
                conv_ln_g[j], conv_ln_b[j], conv_w_out[j], conv_b_out[j])
        x = x + hier_moe(rms_norm(x, ffn_norm[i]), router_group_w[i], router_group_b[i],
                         router_expert_w[i], router_expert_b[i],
                         moe_w_gate[i], moe_w_up[i], moe_w_down[i])
    return x


_drawn_inputs = setup_inputs


def setup_inputs(seed=0):
    import zlib

    import numpy as np

    out = dict(_drawn_inputs(seed))
    spreads = {}
    factors = {'diff_lambda_q1': 8.0,
     'conv_norm': 3.739,
     'conv_b_in': 3.38,
     'conv_ln_g': 3.241,
     'conv_ln_b': 5.036,
     'conv_dw_b': 4.77,
     'conv_b_out': 4.198,
     'router_group_b': 2.736,
     'router_expert_b': 3.315}
    for name, (base, spread) in spreads.items():
        noise = np.random.default_rng([zlib.crc32(name.encode()), seed]).standard_normal(out[name].shape)
        drawn = base * np.exp(spread * noise) if base else spread * noise
        out[name] = __import__('jax').numpy.asarray(drawn.astype(out[name].dtype))
    for name, factor in factors.items():
        out[name] = (out[name] * factor).astype(out[name].dtype)
    return out
```

```python
from contextlib import ExitStack

import concourse.bass as bass
from concourse import mybir

P = 128
T = 256
NT = T // P
D = 1024
KC = D // P
BANK = 512
HEADS = 8
DH = 64
ROT = DH // 8
TAPS = 31
GROUPS = 4
PER_GROUP = 8
EXPERTS = GROUPS * PER_GROUP
F = 512
FC = F // P
SLOTS = 64
FRONT = 2
PADDED = EXPERTS + 8
EPS = 1e-6
LAMBDA_INIT = 0.2
BIG = 1e30
TRIO = 3
PE_CONV = (5, 6, 7)

SCRATCH = 8320
RING = 9
ATT_BASE = 0
MOE_PIECES = 3 * EXPERTS
MOE_BASE = (8, 8 + MOE_PIECES + 6)
CONV_BASE = 8 + MOE_PIECES

C_IDENT, C_BEFORE, C_ONES, C_IOTA, C_REV, C_EARLY, C_HIDE, C_COS, C_SIN, C_END = (
    0, 128, 256, 384, 448, 480, 608, 672, 688, 704)

IN_ORDER = (0, 2, 4, 1, 3, 5)
ROUNDS = {6: (0,), 7: (1, 2), 8: (3,), 9: (4, 5), 10: (6,), 11: (7,)}
UNITS = 16
LAG = 3
NORM_OUT = {8: 0, 10: 1, 15: 2}

PARAM_DMAS = 2 * 7
PHASES = ("att", "moe0", "conv", "moe1")


def build(nc, x_in, consts_in, p, out):
    fp32 = mybir.dt.float32
    i32 = mybir.dt.int32
    ALU = mybir.AluOpType
    ACT = mybir.ActivationFunctionType
    AX = mybir.AxisListType.X

    ctx = ExitStack()
    with ctx:
        def sb(name, shape, dt=fp32):
            return ctx.enter_context(nc.sbuf_tensor(name, shape, dt))

        def sem(name):
            return ctx.enter_context(nc.semaphore(name))

        ring = [sb(f"ring{i}", [P, 4096]) for i in range(RING)]
        x = sb("x", [P, NT, D])
        h = sb("h", [P, NT, KC, P])
        hT = sb("hT", [P, KC, T])
        con = sb("con", [P, C_END])
        norm_gain = sb("norm_gain", [P, 4, KC])
        router_w = sb("router_w", [P, 2, KC, GROUPS + EXPERTS])
        router_b = sb("router_b", [P, 2, GROUPS + EXPERTS])
        stat = sb("stat", [P, 144])
        flag_i = sb("flag_i", [P, 2], i32)
        scratch = sb("scratch", [P, SCRATCH])
        psum = ctx.enter_context(nc.psum_tensor("psum", [P, 8, BANK], fp32))

        ident = con[:, C_IDENT:C_IDENT + P]
        before = con[:, C_BEFORE:C_BEFORE + P]
        ones = con[:, C_ONES:C_ONES + P]
        iota = con[:, C_IOTA:C_IOTA + SLOTS]
        rev = con[:, C_REV:C_REV + EXPERTS]
        early = con[:, C_EARLY:C_EARLY + P]
        hide = con[:, C_HIDE:C_HIDE + 64]

        def carve(spec):
            at, views = 0, {}
            for name, *shape in spec:
                n = 1
                for s in shape:
                    n *= s
                v = scratch[:, at:at + n]
                at += n
                if len(shape) == 2:
                    v = v.rearrange("q (a b) -> q a b", a=shape[0])
                elif len(shape) == 3:
                    v = v.rearrange("q (a b c) -> q a b c", a=shape[0], b=shape[1])
                elif len(shape) == 4:
                    v = v.rearrange("q (a b c d) -> q a b c d", a=shape[0], b=shape[1], c=shape[2])
                views[name] = v
            assert at <= SCRATCH, at
            return views

        att = carve([("qk", NT, 2 * D), ("v", NT, D), ("probs", 3, 2, T),
                     ("pT", 2, P), ("junk", P), ("gains", 2, DH), ("subln", P)])
        o_rows = h[:].rearrange("q t c k -> q t (c k)")
        att["sq"] = o_rows[:, 0, 512:1024]
        att["tmp"] = o_rows[:, 1, 512:768].rearrange("q (a b) -> q a b", a=4)
        att["lam"] = att["probs"][:, 2].rearrange("q a b -> q (a b)")[:, 0:4 * DH].rearrange("q (a b) -> q a b", a=4)
        conv = carve([("u", KC, T + TAPS - 1), ("cv", KC, T), ("sig", 2, 2 * T), ("diag", 4, P),
                      ("cols", 40), ("taps", TAPS, KC), ("mean", T), ("rstd", T),
                      ("pad", 24), ("rows", 3, P), ("b_out", D)])
        conv["sq"] = h[:].rearrange("q t c k -> q (t c k)").rearrange("q (a b) -> q a b", a=KC)
        moe = carve([("xg", KC, 2, TRIO * SLOTS), ("sel", NT, 2, TRIO * SLOTS), ("selw", NT, 2, SLOTS),
                     ("silu", T), ("hid", T), ("hidT", 2, P), ("combT", T), ("outs", D),
                     ("logit", NT, 36), ("ml", NT, EXPERTS), ("one", NT, EXPERTS), ("two", NT, EXPERTS),
                     ("t32", NT, EXPERTS), ("posm", NT, PADDED), ("comb", NT, PADDED),
                     ("late", NT, EXPERTS)])
        zero = moe["outs"][:, 0:BANK]
        ovf = carve([("wg", KC, P), ("wu", KC, P), ("wd", D), ("silu", T), ("hid", T)])

        st, at = {}, 0
        for name, n, cols in (("ss", 2, 0), ("ms", 2, 0), ("rstd", 2, 0), ("qms", 8, 0), ("qrstd", 8, 0),
                              ("nm", 6, 0), ("den", 6, 0), ("oss", 16, 0), ("oms", 16, 0), ("orstd", 16, 0),
                              ("lam_s", 2, 0), ("lam_e", 2, 0), ("neglam", 1, 0), ("mx", 2, 0), ("ge", 8, GROUPS),
                              ("pick", 8, GROUPS), ("gp", 2, 0), ("m1", 2, 0), ("m2", 2, 0), ("dm", 2, 0),
                              ("e2", 2, 0)):
            st[name] = stat[:, at:at + n] if not cols else stat[:, at:at + n].rearrange("q (a b) -> q a b", b=cols)
            at += n

        arrived = [sem(f"arrived{i}") for i in range(RING)]
        piece_used = sem("piece_used")
        x_loaded = sem("x_loaded")
        consts_loaded = sem("consts_loaded")
        att_params_loaded = sem("att_params_loaded")
        lambda_params_loaded = sem("lambda_params_loaded")
        params_loaded = sem("params_loaded")
        conv_params_loaded = sem("conv_params_loaded")
        out_stored = sem("out_stored")
        dve_step = sem("dve_step")
        x_ready = [None] + [sem(f"x_ready_{n}") for n in PHASES[1:]] + [sem("x_final")]
        squares = [sem(f"squares_{n}") for n in PHASES]
        inv_ms = [sem(f"inv_ms_{n}") for n in PHASES]
        rstd_ready = [sem(f"rstd_{n}") for n in PHASES]
        rows_ready = [sem(f"rows_{n}") for n in PHASES]
        rows_turned = [sem(f"rows_turned_{n}") for n in PHASES]
        hT_ready = [sem(f"hT_ready_{n}") for n in PHASES]
        hT_other = [sem(f"hT_other_{n}") for n in PHASES]
        gains_loaded = sem("gains_loaded")
        A = {n: sem("att_" + n) for n in (
            "qkv", "qkv_out", "ms", "rstd", "rotated", "turned", "turned_out", "scores", "max", "neg_max",
            "exp", "mixed", "probs_turned", "pT_ready", "pv", "o_ready", "o_ms", "o_rstd", "o_normed", "o_turned",
            "oT_ready", "lam_sum", "lam_exp")}
        C = {n: sem("conv_" + n) for n in (
            "params_turned", "params", "pads", "glu", "sig", "u_ready", "diag", "diag_used",
            "pe_conv_out", "dve_conv", "sum", "centred", "squared", "var", "inv", "rstd", "scaled", "act")}
        M = [{n: sem(f"moe{l}_" + n) for n in (
            "logits", "group_in", "group_exp", "top_in", "top_exp", "picked", "pos", "sel", "pair", "selw", "flag",
            "first_gathered", "first_dve", "first_act",
            "gathered", "xg", "silu", "hid", "hid_turned", "hidT", "comb_turned", "combT", "outs",
            "combined", "zero", "ov_loaded", "ov_freed", "ov_gu", "ov_silu", "ov_hid", "ov_down",
            "ov_added")} for l in range(2)]

        block = ctx.enter_context(nc.Block())

        def unit(u):
            return u % 8 // 4, 4 * (u // 8) + u % 4

        def turned_product(n):
            return None if n // 2 % 3 == 2 else n - 2 * (n // 6)

        def first_rows(k):
            n, c = k // KC, k % KC
            at = (1 - n) * 2 * SLOTS
            return moe["xg"][:, c, n, at:TRIO * SLOTS], psum[:, 5 + k % 3, 0:TRIO * SLOTS - at]

        def gate_at(l, e):
            return MOE_BASE[l] if isinstance(e, int) and e == 0 else 3 * e + (MOE_BASE[l] - 1)

        def up_at(l, e):
            return gate_at(l, e) + 1

        def down_at(l, e):
            return 3 * e + (MOE_BASE[l] + 4) if not (isinstance(e, int) and e == EXPERTS - 1) else MOE_BASE[l] + 95

        @block.sync
        def _(sp):
            def load(place, src, slot=None, lap=None):
                slot = place % RING if slot is None else slot
                if not isinstance(place, int) or place >= RING:
                    sp.wait_ge(piece_used, place - RING + 1)
                sp.dma_start(ring[slot][:], src).then_inc(arrived[slot], 16)

            def columns(w, n):
                return w[:, n * 512:(n + 1) * 512].rearrange("(p c) f -> p c f", c=KC)

            def rows(w, half):
                return w[half * 512:(half + 1) * 512, :].rearrange("(c p) f -> p c f", p=P)

            def up_src(w, l, e):
                return w[l, bass.ds(e, 1)].rearrange("o (p c) f -> p (o c f)", c=KC)

            def down_src(l, e):
                return p["moe_w_down"][l, bass.ds(e, 1)].rearrange("o (c p) f -> p (o c) f", p=P)

            def load_moe(l):
                base = MOE_BASE[l]
                load(base, up_src(p["moe_w_gate"], l, 0))
                load(base + 1, up_src(p["moe_w_up"], l, 0))
                with sp.Fori(0, 5) as i:
                    for k in range(6):
                        at = base + 2 + 3 * k
                        load(18 * i + at, up_src(p["moe_w_gate"], l, 6 * i + k + 1), at % RING)
                        load(18 * i + at + 1, up_src(p["moe_w_up"], l, 6 * i + k + 1), (at + 1) % RING)
                        load(18 * i + at + 2, down_src(l, 6 * i + k), (at + 2) % RING)
                at = base + 92
                load(at, up_src(p["moe_w_gate"], l, EXPERTS - 1))
                load(at + 1, up_src(p["moe_w_up"], l, EXPERTS - 1))
                load(at + 2, down_src(l, EXPERTS - 2))
                load(at + 3, down_src(l, EXPERTS - 1))

            sp.dma_start(x[:], x_in[0].rearrange("(t p) d -> p t d", p=P)).then_inc(x_loaded, 16)
            sp.dma_start(norm_gain[:, 0, :], p["attn_norm"].rearrange("o (q c) -> q (o c)", c=KC)).then_inc(
                gains_loaded, 16)
            sp.dma_start(con[:], consts_in).then_inc(consts_loaded, 16)
            for n, name in enumerate(("diff_q_gain", "diff_k_gain")):
                sp.dma_start(att["gains"][:, n, :], p[name][0].partition_broadcast(P)).then_inc(att_params_loaded, 16)
            w = p["diff_w_in"][0]
            for n in range(6):
                load(ATT_BASE + n, columns(w, IN_ORDER[n]))
            sp.dma_start(att["subln"], p["diff_subln"][0].partition_broadcast(P)).then_inc(lambda_params_loaded, 16)
            for n, name in enumerate(("q1", "k1", "q2", "k2")):
                sp.dma_start(att["lam"][:, n, :], p["diff_lambda_" + name][0].partition_broadcast(P)).then_inc(
                    lambda_params_loaded, 16)
            for half in range(2):
                load(ATT_BASE + 6 + half, rows(p["diff_w_out"][0], half))
            sp.dma_start(norm_gain[:, 2, :], p["conv_norm"].rearrange("o (q c) -> q (o c)", c=KC)).then_inc(
                gains_loaded, 16)
            for l in range(2):
                sp.dma_start(norm_gain[:, 2 * l + 1, :], p["ffn_norm"][l].rearrange("(q c) -> q c", c=KC)).then_inc(
                    gains_loaded, 16)
                sp.dma_start(router_w[:, l, :, 0:GROUPS], p["router_group_w"][l].rearrange(
                    "(q c) g -> q c g", c=KC)).then_inc(params_loaded, 16)
                for g in range(GROUPS):
                    at = GROUPS + g * PER_GROUP
                    sp.dma_start(router_w[:, l, :, at:at + PER_GROUP], p["router_expert_w"][l, g].rearrange(
                        "(q c) e -> q c e", c=KC)).then_inc(params_loaded, 16)
                sp.dma_start(router_b[:, l, 0:GROUPS], p["router_group_b"][l].partition_broadcast(P)).then_inc(
                    params_loaded, 16)
                sp.dma_start(router_b[:, l, GROUPS:], p["router_expert_b"][l].rearrange(
                    "g e -> (g e)").partition_broadcast(P)).then_inc(params_loaded, 16)
            load_moe(0)
            for n, c in enumerate((0, 2, 1, 3)):
                load(CONV_BASE + n, columns(p["conv_w_in"][0], c))
            for half in range(2):
                load(CONV_BASE + 4 + half, rows(p["conv_w_out"][0], half))
            load_moe(1)
            sp.wait_ge(x_ready[4], 4)
            for t in range(NT):
                sp.dma_start(out[0, t * P:(t + 1) * P, :], x[:, t, :]).then_inc(out_stored, 16)
            sp.wait_ge(out_stored, 16 * NT)

        def has_arrived(eng, place, slot=None, lap=0):
            eng.wait_ge(arrived[place % RING], 16 * (place // RING + lap + 1))

        @block.tensor
        def _(pe):
            def turn_rows(ph):
                for r in range(4):
                    t, half = r // 2, r % 2
                    if half == 0:
                        pe.wait_ge(rows_ready[ph], t + 1)
                    for j in range(4):
                        mm = pe.transpose(psum[:, 4 + r, j * P:(j + 1) * P], h[:, t, 4 * half + j, :], ident)
                    mm.then_inc(rows_turned[ph], 1)

            def all_turned(ph, t):
                pe.wait_ge(hT_ready[ph], t + 1)
                pe.wait_ge(hT_other[ph], t + 1)

            def attention():
                turn_rows(0)

                bank6 = [hT_ready[0], 2]

                def turn(blocks, signal, reader, count):
                    pe.wait_ge(*bank6)
                    for j, block in enumerate(blocks):
                        mm = pe.transpose(psum[:, 6, j * P:(j + 1) * P], block, ident)
                    mm.then_inc(signal, 1)
                    bank6[:] = [reader, count]

                def turn_heads(n):
                    r, t, at = turned_product(n), n % 2, IN_ORDER[n // 2] * 512
                    pe.wait_ge(A["rotated"], r + 1)
                    turn([att["qk"][:, t, at + j * P:at + (j + 1) * P] for j in range(4)], A["turned"],
                         A["turned_out"], r + 1)

                def scores(u):
                    t, hd = unit(u)
                    pe.wait_ge(A["turned_out"], 4 + 4 * (u // 8))
                    if u >= 2:
                        pe.wait_ge(A["exp"], 2 * u - 2)
                    nk = (t + 1) * P
                    for c in range(2):
                        half, bank = slice(c * DH, (c + 1) * DH), 2 + 2 * (u % 2) + c
                        pe.matmul(psum[:, bank, 0:nk], att["qk"][half, t, hd * P:(hd + 1) * P],
                                  att["qk"][half, 0:t + 1, D + hd * P:D + (hd + 1) * P], start=True, stop=False)
                        mm = pe.matmul(psum[:, bank, nk - 64:nk], early[half, :], hide[half, :], start=False, stop=True)
                    mm.then_inc(A["scores"], 1)

                def turn_probs(u):
                    t, hd = unit(u)
                    pe.wait_ge(A["mixed"], u + 1)
                    turn([att["probs"][:, u % 3, 0, k * P:(k + 1) * P] for k in range(t + 1)], A["probs_turned"],
                         A["pT_ready"], u + 1)

                def values(u):
                    t, hd = unit(u)
                    pe.wait_ge(A["pT_ready"], u + 1)
                    pe.wait_ge(A["qkv_out"], 6 + 6 * (u // 8))
                    if u >= 1:
                        pe.wait_ge(A["o_ready"], 2 * u)
                    for k in range(t + 1):
                        mm = pe.matmul(psum[:, 7, 0:P], att["pT"][:, k, :], att["v"][:, k, hd * P:(hd + 1) * P],
                                       start=(k == 0), stop=(k == t))
                    mm.then_inc(A["pv"], 1)

                def turn_out(b):
                    pe.wait_ge(A["o_normed"], b + 1)
                    turn([o_rows[:, b % 2, (4 * (b // 2) + j) * P:(4 * (b // 2) + j + 1) * P] for j in range(4)],
                         A["o_turned"], A["oT_ready"], b + 1)

                def round_of(j):
                    if j < UNITS:
                        scores(j)
                    if LAG <= j < UNITS + LAG:
                        values(j - LAG)
                    if 2 <= j < UNITS + 2:
                        turn_probs(j - 2)
                    if j - 1 in NORM_OUT:
                        turn_out(NORM_OUT[j - 1])

                for n in range(12):
                    if n < 2:
                        all_turned(0, n)
                    if n % 2 == 0:
                        has_arrived(pe, ATT_BASE + n // 2)
                    if n >= 2:
                        pe.wait_ge(A["qkv_out"], n - 1)
                    w = ring[(ATT_BASE + n // 2) % RING][:].rearrange("q (c f) -> q c f", c=KC)
                    for c in range(KC):
                        mm = pe.matmul(psum[:, n % 2, :], hT[:, c, (n % 2) * P:(n % 2 + 1) * P], w[:, c, :],
                                       start=(c == 0), stop=(c == KC - 1))
                    mm.then_inc(A["qkv"] if n % 2 == 0 else piece_used, 1)
                    if n >= 2 and turned_product(n - 2) is not None:
                        turn_heads(n - 2)
                    for j in ROUNDS.get(n, ()):
                        round_of(j)
                for j in range(8, UNITS + LAG):
                    round_of(j)
                pe.wait_ge(A["exp"], 2 * UNITS)
                pe.wait_ge(A["qkv_out"], 12)
                for half in range(2):
                    has_arrived(pe, ATT_BASE + 6 + half)
                    if half == 1:
                        turn_out(3)
                    pe.wait_ge(A["oT_ready"], 2 * half + 2)
                    w = ring[(ATT_BASE + 6 + half) % RING][:].rearrange("q (c f) -> q c f", c=4)
                    for c in range(4):
                        for t in range(NT):
                            for n in range(2):
                                mm = pe.matmul(psum[:, 2 * t + n, :], att["qk"][:, t, (4 * half + c) * P:(4 * half + c + 1) * P],
                                               w[:, c, n * 512:(n + 1) * 512], start=(half + c == 0),
                                               stop=(half == 1 and c == 3))
                    mm.then_inc(piece_used, 1)

            def convolution():
                turn_rows(2)
                all_turned(2, 1)
                pe.wait_ge(conv_params_loaded, 16 * 6)
                pe.transpose(psum[:, 4, 0:40], conv["rows"][0:40, 0, :], ident[0:40, 0:40])
                for b in range(2):
                    mm = pe.transpose(psum[:, 4, 40 + 124 * b:164 + 124 * b], conv["rows"][0:124, 1 + b, :],
                                      ident[0:124, 0:124])
                mm.then_inc(C["params_turned"], 1)
                for n in range(4):
                    has_arrived(pe, CONV_BASE + n)
                    if n == 2:
                        pe.wait_ge(C["params"], 1)
                    w = ring[(CONV_BASE + n) % RING][:].rearrange("q (c f) -> q c f", c=KC)
                    for j in range(4):
                        bank = 4 * (n // 2) + 2 * (n % 2) + j // 2
                        for c in range(KC):
                            mm = pe.matmul(psum[:, bank, (j % 2) * T:(j % 2 + 1) * T], w[:, c, j * P:(j + 1) * P],
                                           hT[:, c, :], start=(c == 0), stop=(c == KC - 1))
                        if j == 1:
                            mm.then_inc(C["glu"], 1)
                    mm.then_inc(piece_used, 1)
                for i, j in enumerate(PE_CONV):
                    pe.wait_ge(C["u_ready"], j // 2 + 1)
                    for tap in range(TAPS):
                        n = i * TAPS + tap
                        pe.wait_ge(C["diag"], n + 1)
                        pe.matmul(psum[:, i, 0:T], conv["diag"][:, n % 4, :], conv["u"][:, j, tap:tap + T],
                                  start=(tap == 0), stop=(tap == TAPS - 1)).then_inc(C["diag_used"], 1)
                pe.wait_ge(C["dve_conv"], 1)
                for j in range(KC):
                    if j in PE_CONV:
                        pe.wait_ge(C["pe_conv_out"], PE_CONV.index(j) + 1)
                    mm = pe.matmul(psum[:, 4, 0:T], ones, conv["cv"][:, j, :], start=(j == 0), stop=(j == KC - 1))
                mm.then_inc(C["sum"], 1)
                for j in range(KC):
                    pe.wait_ge(C["squared"], j + 1)
                    mm = pe.matmul(psum[:, 5, 0:T], ones, conv["sq"][:, j, :], start=(j == 0), stop=(j == KC - 1))
                mm.then_inc(C["var"], 1)
                for half in range(2):
                    has_arrived(pe, CONV_BASE + 4 + half)
                    w = ring[(CONV_BASE + 4 + half) % RING][:].rearrange("q (c f) -> q c f", c=4)
                    for c in range(4):
                        pe.wait_ge(C["act"], 4 * half + c + 1)
                        for t in range(NT):
                            for n in range(2):
                                mm = pe.matmul(psum[:, 2 * t + n, :], conv["sq"][:, 4 * half + c, t * P:(t + 1) * P],
                                               w[:, c, n * 512:(n + 1) * 512], start=(half + c == 0),
                                               stop=(half == 1 and c == 3))
                    mm.then_inc(piece_used, 1)

            def experts(l):
                m, base = M[l], MOE_BASE[l]
                turn_rows(2 * l + 1)
                if l == 0:
                    pe.wait_ge(params_loaded, PARAM_DMAS * 16)
                for t in range(NT):
                    all_turned(2 * l + 1, 1)
                    for c in range(KC):
                        mm = pe.matmul(psum[:, 4, 64 * t:64 * t + 36], hT[:, c, t * P:(t + 1) * P], router_w[:, l, c, :],
                                       start=(c == 0), stop=(c == KC - 1))
                mm.then_inc(m["logits"], 1)
                pe.wait_ge(m["zero"], 1)
                for b in range(4):
                    pe.matmul(psum[:, b, :], zero[:, 0:P], zero, start=True, stop=False,
                              skip_group_check=True)
                pe.wait_ge(m["picked"], 1)
                picked = moe["t32"]
                pe.matmul(psum[:, 5, 0:32], before, picked[:, 0, :], start=True, stop=True)
                pe.matmul(psum[:, 5, 32:64], ones, picked[:, 0, :], start=True, stop=False)
                pe.matmul(psum[:, 5, 32:64], before, picked[:, 1, :], start=False, stop=True)
                pe.matmul(psum[:, 5, 64:96], ones, picked[:, 0, :], start=True, stop=False)
                pe.matmul(psum[:, 5, 64:96], ones, picked[:, 1, :], start=False, stop=True).then_inc(m["pos"], 1)

                def gather(q, buf, c):
                    pe.wait_ge(m["xg"], 8 * q + (c - 15))
                    for t in range(NT):
                        mm = pe.matmul(psum[:, 7, 0:TRIO * SLOTS], h[:, t, c, :], moe["sel"][:, t, buf, :],
                                       start=(t == 0), stop=(t == NT - 1))
                    mm.then_inc(m["gathered"], 1)

                def up(place, lap, buf, j, bankcol):
                    has_arrived(pe, place, lap=lap)
                    w = ring[place % RING][:].rearrange("q (c f) -> q c f", c=KC)
                    for c in range(KC):
                        for hf in range(2):
                            mm = pe.matmul(psum[hf * SLOTS:(hf + 1) * SLOTS, 4, bankcol:bankcol + 256],
                                           moe["xg"][:, c, buf, j * SLOTS:(j + 1) * SLOTS],
                                           w[:, c, hf * 256:(hf + 1) * 256], start=(c == 0), stop=(c == KC - 1))
                    mm.then_inc(piece_used, 1)

                def turn_hidden(e):
                    pe.wait_ge(m["hid"], e + 1)
                    for j in range(2):
                        mm = pe.transpose(psum[:, 6, j * P:(j + 1) * P], moe["hid"][:, j * P:(j + 1) * P], ident)
                    mm.then_inc(m["hid_turned"], 1)

                def turn_combine(pair):
                    pe.wait_ge(m["selw"], pair + 1)
                    pe.wait_ge(m["hidT"], 2 * pair + 2)
                    for t in range(NT):
                        mm = pe.transpose(psum[:, 6, 256 + t * P:256 + (t + 1) * P],
                                          moe["selw"][:, t].rearrange("q a b -> q (a b)"), ident)
                    mm.then_inc(m["comb_turned"], 1)

                def down(e, odd, place, lap):
                    has_arrived(pe, place, lap=lap)
                    pe.wait_ge(m["hidT"], e + 1)
                    if odd:
                        pe.wait_ge(m["outs"], 2 * e)
                    w = ring[place % RING][:].rearrange("q (c f) -> q c f", c=FC)
                    for f in range(FC):
                        for hf in range(2):
                            mm = pe.matmul(psum[hf * SLOTS:(hf + 1) * SLOTS, 5, :],
                                           moe["hidT"][:, f % 2, (f // 2) * SLOTS:(f // 2 + 1) * SLOTS],
                                           w[:, f, hf * 512:(hf + 1) * 512], start=(f == 0), stop=(f == FC - 1))
                    mm.then_inc(piece_used, 1)

                def combine(pair, last=False):
                    pe.wait_ge(m["combT"], pair + 1)
                    pe.wait_ge(m["outs"], 4 * pair + 4)
                    for t in range(NT):
                        for hf in range(2):
                            mm = pe.matmul(psum[:, 2 * hf + t, :], moe["combT"][:, t * P:(t + 1) * P],
                                           moe["outs"][:, hf * 512:(hf + 1) * 512], start=False, stop=last,
                                           skip_group_check=True)
                    mm.then_inc(m["combined"], 1)

                def step(i, k):
                    e, q, buf, j = 6 * i + (k + 1), 2 * i + (1 + k // TRIO), (1 + k // TRIO) % 2, k % TRIO
                    at, lap = base + 2 + 3 * k, 2 * i
                    if j == 0:
                        pe.wait_ge(m["xg"], 8 * q - 7)
                        pe.wait_ge(m["sel"], q + 2)
                    pe.wait_ge(m["hid"], e)
                    up(at, lap, buf, j, 0)
                    gather(q + 1, 1 - buf, 3 * j)
                    turn_hidden(e - 1)
                    up(at + 1, lap, buf, j, 256)
                    gather(q + 1, 1 - buf, 3 * j + 1)
                    odd, pair = k % 2 == 1, 3 * i + k // 2
                    if odd:
                        turn_combine(pair)
                    down(e - 1, odd, at + 2, lap)
                    if 3 * j + 2 < KC:
                        gather(q + 1, 1 - buf, 3 * j + 2)
                    if odd:
                        combine(pair)

                def first_gather(n, c):
                    at, at_end = ((2 * SLOTS, TRIO * SLOTS), (0, TRIO * SLOTS))[n]
                    k = KC * n + c
                    if k >= 3:
                        pe.wait_ge(m["first_act" if k % 2 == 0 else "first_dve"], (k - 3) // 2 + 1)
                    for t in range(NT):
                        mm = pe.matmul(psum[:, 5 + k % 3, 0:at_end - at], h[:, t, c, :],
                                       moe["sel"][:, t, n, at:at_end], start=(t == 0), stop=(t == NT - 1))
                    mm.then_inc(m["first_gathered"], 1)

                pe.wait_ge(m["sel"], 2)
                for c in range(KC):
                    first_gather(0, c)
                pe.wait_ge(m["first_act"], 4)
                pe.wait_ge(m["first_dve"], 4)
                up(base, 0, 0, 2, 0)
                for c in range(4):
                    first_gather(1, c)
                up(base + 1, 0, 0, 2, 256)
                for c in range(4, KC):
                    first_gather(1, c)
                pe.wait_ge(m["first_act"], 7)
                with pe.Fori(0, 5) as i:
                    for k in range(6):
                        step(i, k)
                e, at = EXPERTS - 1, base + 92
                pe.wait_ge(m["xg"], 8 * 11 - 7)
                pe.wait_ge(m["hid"], e)
                up(at, 0, 1, 0, 0)
                turn_hidden(e - 1)
                up(at + 1, 0, 1, 0, 256)
                down(e - 1, False, at + 2, 0)
                turn_hidden(e)
                turn_combine(EXPERTS // 2 - 1)
                down(e, True, at + 3, 0)
                combine(EXPERTS // 2 - 1, last=True)

                pe.wait_ge(m["flag"], 1)
                late = pe.value_load(flag_i[0:1, l:l + 1], min_val=0, max_val=T)
                with pe.If(late > SLOTS):
                    with pe.Fori(0, EXPERTS) as e:
                        pe.wait_ge(m["ov_added"], 4 * e + 1)
                        for f in range(FC):
                            pe.wait_ge(m["ov_loaded"], 48 * (FC * e + f + 1))
                            for bank, wt in ((4, "wg"), (5, "wu")):
                                for c in range(KC):
                                    mm = pe.matmul(psum[:, bank, 0:T], ovf[wt][:, c, :], hT[:, c, :], start=(c == 0),
                                                   stop=(c == KC - 1))
                            mm.then_inc(m["ov_gu"], 1)
                            pe.wait_ge(m["ov_hid"], FC * e + f + 1)
                            for t in range(NT):
                                for n in range(2):
                                    mm = pe.matmul(psum[:, 2 * t + n, :], ovf["hid"][:, t * P:(t + 1) * P],
                                                   ovf["wd"][:, n * 512:(n + 1) * 512], start=(f == 0),
                                                   stop=(f == FC - 1))
                            mm.then_inc(m["ov_freed"], 1)

            pe.wait_ge(consts_loaded, 16)
            attention()
            experts(0)
            convolution()
            experts(1)

        @block.scalar
        def _(act):
            def norm(ph):
                for t in range(NT):
                    if ph > 0:
                        act.wait_ge(x_ready[ph], 2 * (t + 1))
                    elif t == 0:
                        act.wait_ge(x_loaded, 16)
                    nc.scalar.activation(h[:, t].rearrange("q c k -> q (c k)"), x[:, t, :], ACT.Square,
                                         accum_out=st["ss"][:, t:t + 1]).then_inc(squares[ph], 1)
                    act.wait_ge(inv_ms[ph], t + 1)
                    nc.scalar.activation(st["rstd"][:, t:t + 1], st["ms"][:, t:t + 1], ACT.Sqrt).then_inc(
                        rstd_ready[ph], 1)
                for t in range(NT):
                    if t == 0:
                        act.wait_ge(gains_loaded, 16 * (1 if ph == 0 else 4))
                    act.wait_ge(rows_turned[ph], 2 * t + 2)
                    for j in range(4):
                        ins = nc.scalar.activation(hT[:, 4 + j, t * P:(t + 1) * P], psum[:, 5 + 2 * t, j * P:(j + 1) * P],
                                                   ACT.Copy, scale=norm_gain[:, ph, 4 + j:5 + j])
                    ins.then_inc(hT_other[ph], 1)

            def attention():
                norm(0)

                def exps(u):
                    t, hd = unit(u)
                    act.wait_ge(A["neg_max"], u + 1)
                    if u >= 3:
                        act.wait_ge(A["probs_turned"], u - 2)
                    nk = (t + 1) * P
                    for c in range(2):
                        at = 2 * (u % 3) + c
                        nc.scalar.activation(att["probs"][:, u % 3, c, 0:nk], psum[:, 2 + 2 * (u % 2) + c, 0:nk],
                                             ACT.Exp, bias=st["nm"][:, at:at + 1], scale=DH ** -0.5,
                                             accum_out=st["den"][:, at:at + 1]).then_inc(A["exp"], 1)

                def outputs(u):
                    t, hd = unit(u)
                    act.wait_ge(A["pv"], u + 1)
                    nc.scalar.activation(o_rows[:, t, hd * P:(hd + 1) * P], psum[:, 7, 0:P], ACT.Copy).then_inc(
                        A["o_ready"], 1)
                    if u >= 1:
                        act.wait_ge(A["o_ready"], 2 * u)
                    nc.scalar.activation(att["junk"], psum[:, 7, 0:P], ACT.Square,
                                         accum_out=st["oss"][:, u:u + 1]).then_inc(A["o_ready"], 1)

                def probs_out(u):
                    t, hd = unit(u)
                    act.wait_ge(A["probs_turned"], u + 1)
                    nc.scalar.activation(att["pT"][:, 0:t + 1, :].rearrange("q a b -> q (a b)"),
                                         psum[:, 6, 0:(t + 1) * P], ACT.Copy).then_inc(A["pT_ready"], 1)

                def norm_out(b):
                    act.wait_ge(A["o_ms"], b + 1)
                    sl = slice(4 * b, 4 * b + 4)
                    nc.scalar.activation(st["orstd"][:, sl], st["oms"][:, sl], ACT.Sqrt).then_inc(A["o_rstd"], 1)

                def turned_out(b):
                    act.wait_ge(A["o_turned"], b + 1)
                    nc.scalar.activation(att["qk"][:, b % 2, 512 * (b // 2):512 * (b // 2 + 1)], psum[:, 6, :],
                                         ACT.Copy).then_inc(A["oT_ready"], 1)

                def round_of(j):
                    if j < UNITS:
                        exps(j)
                    if LAG <= j < UNITS + LAG:
                        outputs(j - LAG)
                    if 2 <= j < UNITS + 2:
                        probs_out(j - 2)
                    if j in NORM_OUT:
                        norm_out(NORM_OUT[j])
                    if j - 1 in NORM_OUT:
                        turned_out(NORM_OUT[j - 1])

                for n in range(12):
                    if n % 2 == 0:
                        act.wait_ge(A["qkv"], n // 2 + 1)
                    else:
                        act.wait_ge(piece_used, ATT_BASE + n // 2 + 1)
                    at = IN_ORDER[n // 2] * 512
                    dst = att["qk"][:, n % 2, at:at + 512] if at < 2 * D else att["v"][:, n % 2, at - 2 * D:at - 2 * D + 512]
                    nc.scalar.activation(dst, psum[:, n % 2, :], ACT.Copy).then_inc(A["qkv_out"], 1)
                    if n >= 2 and turned_product(n - 2) is not None:
                        act.wait_ge(A["turned"], turned_product(n - 2) + 1)
                        at = IN_ORDER[(n - 2) // 2] * 512
                        nc.scalar.activation(att["qk"][:, n % 2, at:at + 512], psum[:, 6, :], ACT.Copy).then_inc(
                            A["turned_out"], 1)
                    for j in ROUNDS.get(n, ()):
                        round_of(j)
                    if turned_product(n) is not None:
                        act.wait_ge(A["ms"], turned_product(n) + 1)
                        nc.scalar.activation(st["qrstd"], st["qms"], ACT.Sqrt).then_inc(A["rstd"], 1)
                    if n == 5:
                        act.wait_ge(A["lam_sum"], 1)
                        nc.scalar.activation(st["lam_e"], st["lam_s"], ACT.Exp).then_inc(A["lam_exp"], 1)
                for j in range(8, UNITS + LAG):
                    round_of(j)
                norm_out(3)
                turned_out(3)

            def convolution():
                norm(2)
                for b in range(4):
                    piece = CONV_BASE + 2 * (b // 2) + 1
                    if b == 0:
                        act.wait_ge(C["params"], 1)
                    if b % 2 == 0:
                        act.wait_ge(C["glu"], piece - CONV_BASE + 1)
                    else:
                        act.wait_ge(piece_used, piece + 1)
                    if b >= 2:
                        act.wait_ge(C["u_ready"], b - 1)
                    for jj in range(2):
                        j = 2 * b + jj
                        nc.scalar.activation(conv["sig"][:, b % 2, jj * T:(jj + 1) * T],
                                             psum[:, 4 * (b // 2) + 2 + b % 2, jj * T:(jj + 1) * T], ACT.Sigmoid,
                                             bias=conv["cols"][:, 8 + j:9 + j]).then_inc(C["sig"], 1)

                def diagonals(i, j):
                    for tap in range(TAPS):
                        n = i * TAPS + tap
                        if n >= 4:
                            act.wait_ge(C["diag_used"], n - 3)
                        nc.scalar.activation(conv["diag"][:, n % 4, :], ident, ACT.Copy,
                                             scale=conv["taps"][:, tap, j:j + 1]).then_inc(C["diag"], 1)

                def taps_out(i, j):
                    act.wait_ge(C["diag_used"], (i + 1) * TAPS)
                    nc.scalar.activation(conv["cv"][:, j, :], psum[:, i, 0:T], ACT.Identity,
                                         bias=conv["cols"][:, 16 + j:17 + j]).then_inc(C["pe_conv_out"], 1)

                for i, j in enumerate(PE_CONV):
                    diagonals(i, j)
                    if i >= 1:
                        taps_out(i - 1, PE_CONV[i - 1])
                taps_out(len(PE_CONV) - 1, PE_CONV[-1])
                for j in range(KC):
                    act.wait_ge(C["centred"], j + 1)
                    nc.scalar.activation(conv["sq"][:, j, :], conv["cv"][:, j, :], ACT.Square).then_inc(C["squared"], 1)
                act.wait_ge(C["inv"], 1)
                nc.scalar.activation(conv["rstd"], conv["mean"], ACT.Sqrt).then_inc(C["rstd"], 1)
                for j in range(KC):
                    act.wait_ge(C["scaled"], j + 1)
                    nc.scalar.activation(conv["sq"][:, j, :], conv["cv"][:, j, :], ACT.Silu,
                                         scale=conv["cols"][:, 24 + j:25 + j],
                                         bias=conv["cols"][:, 32 + j:33 + j]).then_inc(C["act"], 1)

            def experts(l):
                m = M[l]
                norm(2 * l + 1)
                act.wait_ge(m["group_in"], 1)
                nc.scalar.activation(st["ge"], st["ge"], ACT.Exp).then_inc(m["group_exp"], 1)
                act.wait_ge(m["top_in"], 1)
                nc.scalar.activation(st["e2"], st["dm"], ACT.Exp).then_inc(m["top_exp"], 1)

                def silu(e):
                    act.wait_ge(piece_used, up_at(l, e) + 1)
                    nc.scalar.activation(moe["silu"], psum[:, 4, 0:256], ACT.Silu).then_inc(m["silu"], 1)

                def hidden_out(e):
                    act.wait_ge(m["hid_turned"], e + 1)
                    nc.scalar.activation(moe["hidT"].rearrange("q a b -> q (a b)"), psum[:, 6, 0:256],
                                         ACT.Copy).then_inc(m["hidT"], 1)

                def down_out(e, odd):
                    act.wait_ge(piece_used, down_at(l, e) + 1)
                    for hf in range(2):
                        nc.scalar.activation(moe["outs"][odd * SLOTS:(odd + 1) * SLOTS, hf * 512:(hf + 1) * 512],
                                             psum[hf * SLOTS:(hf + 1) * SLOTS, 5, :], ACT.Copy).then_inc(m["outs"], 1)

                def first_rows_in(k):
                    act.wait_ge(m["first_gathered"], k + 1)
                    dst, bank = first_rows(k)
                    nc.scalar.activation(dst, bank, ACT.Copy, scale=norm_gain[:, 2 * l + 1, k % KC:k % KC + 1]).then_inc(
                        m["first_act"], 1)

                for k in (1, 3, 5, 7, 9, 11):
                    first_rows_in(k)
                silu(0)
                first_rows_in(13)
                with act.Fori(0, 5) as i:
                    for k in range(6):
                        hidden_out(6 * i + k)
                        silu(6 * i + (k + 1))
                        down_out(6 * i + k, k % 2)
                hidden_out(EXPERTS - 2)
                silu(EXPERTS - 1)
                down_out(EXPERTS - 2, 0)
                hidden_out(EXPERTS - 1)
                down_out(EXPERTS - 1, 1)

                act.wait_ge(m["flag"], 1)
                late = act.value_load(flag_i[0:1, l:l + 1], min_val=0, max_val=T)
                with act.If(late > SLOTS):
                    with act.Fori(0, EXPERTS) as e:
                        for f in range(FC):
                            act.wait_ge(m["ov_gu"], FC * e + f + 1)
                            nc.scalar.activation(ovf["silu"], psum[:, 4, 0:T], ACT.Silu).then_inc(m["ov_silu"], 1)

            attention()
            experts(0)
            convolution()
            experts(1)

        @block.vector
        def _(dve):
            done = [0]
            V = nc.vector

            def link(ins):
                done[0] += 1
                ins.then_inc(dve_step, 1)
                dve.wait_ge(dve_step, done[0])

            def wide(ap, axis, shape):
                return ap.unsqueeze(axis).to_broadcast(shape)

            def norm(ph):
                for t in range(NT):
                    ms = st["ms"][:, t:t + 1]
                    dve.wait_ge(squares[ph], t + 1)
                    link(V.tensor_scalar(ms, st["ss"][:, t:t + 1], 1.0 / D, EPS, ALU.mult, ALU.add))
                    V.reciprocal(ms, ms).then_inc(inv_ms[ph], 1)
                    dve.wait_ge(rstd_ready[ph], t + 1)
                    V.tensor_scalar(h[:, t].rearrange("q c k -> q k c"), x[:, t, :].rearrange("q (k c) -> q k c", c=KC),
                                    st["rstd"][:, t:t + 1], None, ALU.mult).then_inc(rows_ready[ph], 1)
                dve.wait_ge(gains_loaded, 16 * (1 if ph == 0 else 4))
                for t in range(NT):
                    dve.wait_ge(rows_turned[ph], 2 * t + 1)
                    V.tensor_tensor(hT[:, 0:4, t * P:(t + 1) * P],
                                    psum[:, 4 + 2 * t, :].rearrange("q (a b) -> q a b", a=4),
                                    wide(norm_gain[:, ph, 0:4], 2, [P, 4, P]), ALU.mult).then_inc(hT_ready[ph], 1)

            def attention():
                norm(0)
                tmp = att["tmp"]
                dve.wait_ge(consts_loaded, 16)
                dve.wait_ge(att_params_loaded, 16 * 2)

                def norm_heads(n):
                    r, t, at = turned_product(n), n % 2, IN_ORDER[n // 2] * 512
                    q = att["qk"][:, t, at:at + 512]
                    q3 = q.rearrange("q (a b) -> q a b", a=8)
                    dve.wait_ge(A["qkv_out"], n + 1)
                    link(V.tensor_tensor(att["sq"], q, q, ALU.mult))
                    link(V.tensor_reduce(st["qms"], att["sq"].rearrange("q (a b) -> q a b", a=8), AX, ALU.add))
                    link(V.tensor_scalar(st["qms"], st["qms"], 1.0 / DH, EPS, ALU.mult, ALU.add))
                    V.reciprocal(st["qms"], st["qms"]).then_inc(A["ms"], 1)
                    link(V.tensor_tensor(q3, q3, wide(att["gains"][:, at // D, :], 1, [P, 8, DH]), ALU.mult))
                    dve.wait_ge(A["rstd"], r + 1)
                    link(V.tensor_tensor(q3, q3, wide(st["qrstd"], 2, [P, 8, DH]), ALU.mult))
                    x1, x2 = q3[:, :, 0:ROT], q3[:, :, ROT:2 * ROT]
                    cos = wide(con[:, C_COS + ROT * t:C_COS + ROT * (t + 1)], 1, [P, 8, ROT])
                    sin = wide(con[:, C_SIN + ROT * t:C_SIN + ROT * (t + 1)], 1, [P, 8, ROT])
                    a = [tmp[:, k, :].rearrange("q (a b) -> q a b", a=8) for k in range(4)]
                    V.tensor_tensor(a[0], x1, cos, ALU.mult)
                    V.tensor_tensor(a[1], x2, sin, ALU.mult)
                    V.tensor_tensor(a[2], x2, cos, ALU.mult)
                    link(V.tensor_tensor(a[3], x1, sin, ALU.mult))
                    V.tensor_tensor(x1, a[0], a[1], ALU.subtract)
                    V.tensor_tensor(x2, a[2], a[3], ALU.add).then_inc(A["rotated"], 1)
                    dve.wait_ge(A["rotated"], r + 1)

                def biggest(u):
                    t, hd = unit(u)
                    dve.wait_ge(A["scores"], u + 1)
                    nm = st["nm"][:, 2 * (u % 3):2 * (u % 3) + 2]
                    bank = 2 + 2 * (u % 2)
                    V.tensor_reduce(nm, psum[:, bank:bank + 2, 0:(t + 1) * P], AX, ALU.max).then_inc(A["max"], 1)
                    dve.wait_ge(A["max"], u + 1)
                    V.tensor_scalar(nm, nm, -DH ** -0.5, None, ALU.mult).then_inc(A["neg_max"], 1)

                def mix(u):
                    t, hd = unit(u)
                    nk = (t + 1) * P
                    den = st["den"][:, 2 * (u % 3):2 * (u % 3) + 2]
                    one, other = att["probs"][:, u % 3, 0, 0:nk], att["probs"][:, u % 3, 1, 0:nk]
                    dve.wait_ge(A["exp"], 2 * u + 2)
                    link(V.reciprocal(den, den))
                    link(V.tensor_scalar(other, other, den[:, 1:2], st["neglam"], ALU.mult, ALU.mult))
                    V.scalar_tensor_tensor(out=one, in0=one, scalar=den[:, 0:1], in1=other, op0=ALU.mult,
                                           op1=ALU.add).then_inc(A["mixed"], 1)

                def norm_out(b):
                    dve.wait_ge(A["o_ready"], 8 * (b + 1))
                    sl = slice(4 * b, 4 * b + 4)
                    link(V.tensor_scalar(st["oms"][:, sl], st["oss"][:, sl], 1.0 / P, EPS, ALU.mult, ALU.add))
                    V.reciprocal(st["oms"][:, sl], st["oms"][:, sl]).then_inc(A["o_ms"], 1)
                    o3 = o_rows[:, b % 2, 512 * (b // 2):512 * (b // 2 + 1)].rearrange("q (a b) -> q a b", a=4)
                    link(V.scalar_tensor_tensor(out=o3, in0=o3, scalar=1.0 - LAMBDA_INIT,
                                                in1=wide(att["subln"], 1, [P, 4, P]), op0=ALU.mult, op1=ALU.mult))
                    dve.wait_ge(A["o_rstd"], b + 1)
                    V.tensor_tensor(o3, o3, wide(st["orstd"][:, sl], 2, [P, 4, P]), ALU.mult).then_inc(A["o_normed"], 1)

                def round_of(j):
                    if j < UNITS:
                        biggest(j)
                    if 1 <= j < UNITS + 1:
                        mix(j - 1)
                    if j in NORM_OUT:
                        norm_out(NORM_OUT[j])

                for n in range(12):
                    for j in ROUNDS.get(n, ()):
                        round_of(j)
                    if turned_product(n) is not None:
                        norm_heads(n)
                    if n == 4:
                        dve.wait_ge(lambda_params_loaded, 16 * 5)
                        for c in range(2):
                            link(V.tensor_tensor(tmp[:, c, :], att["lam"][:, 2 * c, :], att["lam"][:, 2 * c + 1, :],
                                                 ALU.mult))
                        V.tensor_reduce(st["lam_s"], tmp[:, 0:2, :], AX, ALU.add).then_inc(A["lam_sum"], 1)
                        dve.wait_ge(A["lam_exp"], 1)
                        link(V.tensor_tensor(st["neglam"], st["lam_e"][:, 1:2], st["lam_e"][:, 0:1], ALU.subtract))
                        link(V.tensor_scalar(st["neglam"], st["neglam"], -LAMBDA_INIT, None, ALU.add))
                for j in range(8, UNITS + LAG):
                    round_of(j)
                norm_out(3)
                dve.wait_ge(piece_used, ATT_BASE + 8)
                for t in range(NT):
                    for n in range(2):
                        cols = slice(n * 512, (n + 1) * 512)
                        V.tensor_tensor(x[:, t, cols], x[:, t, cols], psum[:, 2 * t + n, :], ALU.add).then_inc(
                            x_ready[1], 1)

            def convolution():
                V.memset(conv["u"][:, :, 0:TAPS - 1], 0.0).then_inc(C["pads"], 1)
                norm(2)
                dve.wait_ge(C["params_turned"], 1)
                V.tensor_copy(conv["cols"], psum[:, 4, 0:40])
                V.tensor_copy(conv["taps"].rearrange("q a b -> q (a b)"), psum[:, 4, 40:288]).then_inc(C["params"], 1)
                dve.wait_ge(C["params"], 1)
                for t in range(NT):
                    V.tensor_tensor(x[:, t, :], x[:, t, :], conv["b_out"], ALU.add)

                def glu(b):
                    piece = CONV_BASE + 2 * (b // 2)
                    if b % 2 == 0:
                        dve.wait_ge(C["glu"], piece - CONV_BASE + 1)
                    else:
                        dve.wait_ge(piece_used, piece + 1)
                    dve.wait_ge(C["sig"], 2 * b + 2)
                    for jj in range(2):
                        j = 2 * b + jj
                        ins = V.scalar_tensor_tensor(
                            out=conv["u"][:, j, TAPS - 1:], in0=psum[:, 4 * (b // 2) + b % 2, jj * T:(jj + 1) * T],
                            scalar=conv["cols"][:, j:j + 1], in1=conv["sig"][:, b % 2, jj * T:(jj + 1) * T],
                            op0=ALU.add, op1=ALU.mult)
                    ins.then_inc(C["u_ready"], 1)
                    dve.wait_ge(C["u_ready"], b + 1)

                def taps(tiles, first=0, end=TAPS):
                    for tap in range(first, end):
                        for j in tiles:
                            src = conv["u"][:, j, tap:tap + T]
                            if tap == 0:
                                ins = V.tensor_scalar(conv["cv"][:, j, :], src, conv["taps"][:, 0, j:j + 1],
                                                      conv["cols"][:, 16 + j:17 + j], ALU.mult, ALU.add)
                            else:
                                ins = V.scalar_tensor_tensor(
                                    out=conv["cv"][:, j, :], in0=src, scalar=conv["taps"][:, tap, j:j + 1],
                                    in1=conv["cv"][:, j, :], op0=ALU.mult, op1=ALU.add)
                        link(ins)

                dve.wait_ge(C["pads"], 1)
                glu(0)
                taps((0, 1))
                glu(1)
                taps((2, 3), 0, 12)
                glu(2)
                glu(3)
                taps((2, 3), 12)
                taps((4,))
                V.memset(st["mx"], 0.0).then_inc(C["dve_conv"], 1)
                dve.wait_ge(C["sum"], 1)
                link(V.tensor_scalar(conv["mean"], psum[:, 4, 0:T], 1.0 / D, None, ALU.mult))
                for j in range(KC):
                    V.tensor_tensor(conv["cv"][:, j, :], conv["cv"][:, j, :], conv["mean"], ALU.subtract).then_inc(
                        C["centred"], 1)
                dve.wait_ge(C["var"], 1)
                dve.wait_ge(C["centred"], KC)
                link(V.tensor_scalar(conv["mean"], psum[:, 5, 0:T], 1.0 / D, EPS, ALU.mult, ALU.add))
                V.reciprocal(conv["mean"], conv["mean"]).then_inc(C["inv"], 1)
                dve.wait_ge(C["rstd"], 1)
                for j in range(KC):
                    V.tensor_tensor(conv["cv"][:, j, :], conv["cv"][:, j, :], conv["rstd"], ALU.mult).then_inc(
                        C["scaled"], 1)
                dve.wait_ge(piece_used, CONV_BASE + 6)
                for t in range(NT):
                    for n in range(2):
                        cols = slice(n * 512, (n + 1) * 512)
                        V.tensor_tensor(x[:, t, cols], x[:, t, cols], psum[:, 2 * t + n, :], ALU.add).then_inc(
                            x_ready[3], 1)

            def route(l):
                m = M[l]
                if l == 0:
                    dve.wait_ge(params_loaded, 16 * PARAM_DMAS)
                lg, ml, one, two, t32 = (moe[n] for n in ("logit", "ml", "one", "two", "t32"))
                dve.wait_ge(m["logits"], 1)
                link(V.tensor_tensor(lg, psum[:, 4, 0:128].rearrange("q (a b) -> q a b", a=2)[:, :, 0:36],
                                     wide(router_b[:, l, :], 1, [P, NT, 36]), ALU.add))
                gl = lg[:, :, 0:GROUPS]
                link(V.tensor_reduce(st["mx"], gl, AX, ALU.max))
                link(V.tensor_tensor(st["ge"], gl, wide(st["mx"], 2, [P, NT, GROUPS]), ALU.subtract))
                link(V.tensor_scalar(st["pick"], st["ge"], 0.0, None, ALU.is_equal))
                V.tensor_scalar(st["dm"], st["mx"], 0.0, None, ALU.mult).then_inc(m["group_in"], 1)
                rev4 = wide(rev[:, EXPERTS - GROUPS:EXPERTS], 1, [P, NT, GROUPS])
                link(V.tensor_tensor(st["pick"], st["pick"], rev4, ALU.mult))
                link(V.tensor_reduce(st["mx"], st["pick"], AX, ALU.max))
                link(V.tensor_tensor(st["pick"], rev4, wide(st["mx"], 2, [P, NT, GROUPS]), ALU.is_equal))
                link(V.tensor_scalar(st["pick"], st["pick"], BIG, -BIG, ALU.mult, ALU.add))
                dve.wait_ge(m["group_exp"], 1)
                link(V.tensor_reduce(st["gp"], st["ge"], AX, ALU.add))
                link(V.reciprocal(st["gp"], st["gp"]))
                link(V.tensor_tensor(ml.rearrange("q t (g e) -> q t g e", g=GROUPS),
                                     lg[:, :, GROUPS:].rearrange("q t (g e) -> q t g e", g=GROUPS),
                                     wide(st["pick"], 3, [P, NT, GROUPS, PER_GROUP]), ALU.add))

                rev32 = wide(rev, 1, [P, NT, EXPERTS])

                def first_of_max(mx, chosen):
                    link(V.tensor_reduce(mx, ml, AX, ALU.max))
                    link(V.tensor_tensor(chosen, ml, wide(mx, 2, [P, NT, EXPERTS]), ALU.is_equal))
                    link(V.tensor_tensor(chosen, chosen, rev32, ALU.mult))
                    link(V.tensor_reduce(st["mx"], chosen, AX, ALU.max))
                    link(V.tensor_tensor(chosen, rev32, wide(st["mx"], 2, [P, NT, EXPERTS]), ALU.is_equal))

                first_of_max(st["m1"], one)
                link(V.scalar_tensor_tensor(out=ml, in0=one, scalar=-3 * BIG, in1=ml, op0=ALU.mult, op1=ALU.add))
                first_of_max(st["m2"], two)
                V.tensor_tensor(st["dm"], st["m2"], st["m1"], ALU.subtract).then_inc(m["top_in"], 1)
                V.tensor_tensor(t32, one, two, ALU.add).then_inc(m["picked"], 1)
                V.memset(moe["posm"], -1.0)
                link(V.memset(moe["comb"], 0.0))
                dve.wait_ge(m["top_exp"], 1)
                link(V.tensor_scalar(st["m1"], st["e2"], 1.0, None, ALU.add))
                link(V.reciprocal(st["m1"], st["m1"]))
                link(V.tensor_tensor(st["m1"], st["m1"], st["gp"], ALU.mult))
                link(V.tensor_tensor(st["m2"], st["m1"], st["e2"], ALU.mult))
                link(V.tensor_tensor(one, one, wide(st["m1"], 2, [P, NT, EXPERTS]), ALU.mult))
                link(V.tensor_tensor(two, two, wide(st["m2"], 2, [P, NT, EXPERTS]), ALU.mult))
                comb = moe["comb"][:, :, FRONT:FRONT + EXPERTS]
                posm = moe["posm"][:, :, FRONT:FRONT + EXPERTS]
                link(V.tensor_tensor(comb, one, two, ALU.add))
                dve.wait_ge(m["pos"], 1)
                dve.wait_ge(m["picked"], 1)
                link(V.scalar_tensor_tensor(out=one, in0=psum[:, 5, 0:64].rearrange("q (a b) -> q a b", a=2), scalar=1.0,
                                            in1=t32, op0=ALU.add, op1=ALU.mult))
                link(V.tensor_scalar(posm, one, -1.0, None, ALU.add))
                link(V.tensor_reduce(st["mx"][:, 0:1], psum[:, 5, 64:96], AX, ALU.max))
                V.tensor_copy(flag_i[:, l:l + 1], st["mx"][:, 0:1]).then_inc(m["flag"], 1)
                link(V.tensor_scalar(two, posm, float(SLOTS), None, ALU.is_ge))
                link(V.tensor_tensor(moe["late"], two, comb, ALU.mult))

            def experts(l):
                m = M[l]
                norm(2 * l + 1)
                V.memset(zero, 0.0).then_inc(m["zero"], 1)
                route(l)

                def select(q, buf):
                    V.tensor_tensor(moe["sel"][:, :, buf, :].rearrange("q t (a b) -> q t a b", a=TRIO),
                                    iota.unsqueeze(1).unsqueeze(1).to_broadcast([P, NT, TRIO, SLOTS]),
                                    wide(moe["posm"][:, :, bass.ds(TRIO * q, TRIO)], 3, [P, NT, TRIO, SLOTS]),
                                    ALU.is_equal).then_inc(m["sel"], 1)

                def select_weighted(pair, at):
                    V.tensor_tensor(moe["selw"], iota.unsqueeze(1).unsqueeze(1).to_broadcast([P, NT, 2, SLOTS]),
                                    wide(moe["posm"][:, :, bass.ds(at, 2)], 3, [P, NT, 2, SLOTS]),
                                    ALU.is_equal).then_inc(m["pair"], 1)
                    dve.wait_ge(m["pair"], pair + 1)
                    V.tensor_tensor(moe["selw"], moe["selw"],
                                    wide(moe["comb"][:, :, bass.ds(at, 2)], 3, [P, NT, 2, SLOTS]),
                                    ALU.mult).then_inc(m["selw"], 1)

                def rows_in(q, buf, c):
                    dve.wait_ge(m["gathered"], 8 * q + (c - 15))
                    V.tensor_scalar(moe["xg"][:, c, buf, :], psum[:, 7, 0:TRIO * SLOTS],
                                    norm_gain[:, 2 * l + 1, c:c + 1], None, ALU.mult).then_inc(m["xg"], 1)

                def hidden(e):
                    dve.wait_ge(m["silu"], e + 1)
                    V.tensor_tensor(moe["hid"], moe["silu"], psum[:, 4, 256:512], ALU.mult).then_inc(m["hid"], 1)

                def combine_in(pair):
                    dve.wait_ge(m["comb_turned"], pair + 1)
                    V.tensor_copy(moe["combT"], psum[:, 6, 256:512]).then_inc(m["combT"], 1)

                for q in range(2):
                    select(q, q)
                def first_rows_in(k):
                    dve.wait_ge(m["first_gathered"], k + 1)
                    dst, bank = first_rows(k)
                    V.tensor_scalar(dst, bank, norm_gain[:, 2 * l + 1, k % KC:k % KC + 1], None, ALU.mult).then_inc(
                        m["first_dve" if k < 15 else "xg"], 1)

                for k in (0, 2, 4, 6, 8, 10):
                    first_rows_in(k)
                hidden(0)
                for k in (12, 14, 15):
                    first_rows_in(k)
                select(2, 0)
                with dve.Fori(0, 5) as i:
                    for k in range(6):
                        j = k % TRIO
                        q = 2 * i + (1 + k // TRIO)
                        buf = (1 + k // TRIO) % 2
                        rows_in(q + 1, 1 - buf, 3 * j)
                        hidden(6 * i + (k + 1))
                        rows_in(q + 1, 1 - buf, 3 * j + 1)
                        if k % 2 == 0:
                            select_weighted(3 * i + k // 2, 6 * i + (k + FRONT))
                        else:
                            combine_in(3 * i + k // 2)
                        if 3 * j + 2 < KC:
                            rows_in(q + 1, 1 - buf, 3 * j + 2)
                        if j == TRIO - 1:
                            select(q + 2, buf)
                hidden(EXPERTS - 1)
                select_weighted(EXPERTS // 2 - 1, EXPERTS - 2 + FRONT)
                combine_in(EXPERTS // 2 - 1)
                dve.wait_ge(m["combined"], EXPERTS // 2)
                for t in range(NT):
                    for hf in range(2):
                        cols = slice(hf * 512, (hf + 1) * 512)
                        ins = V.tensor_tensor(x[:, t, cols], x[:, t, cols], psum[:, 2 * hf + t, :], ALU.add)
                link(ins)

                late = dve.value_load(flag_i[0:1, l:l + 1], min_val=0, max_val=T)
                with dve.If(late > SLOTS):
                    V.memset(st["m1"], 0.0).then_inc(m["ov_freed"], 1)
                    V.memset(st["m2"], 0.0).then_inc(m["ov_added"], 1)
                    with dve.Fori(0, EXPERTS) as e:
                        for f in range(FC):
                            dve.wait_ge(m["ov_silu"], FC * e + f + 1)
                            V.tensor_tensor(ovf["hid"], ovf["silu"], psum[:, 5, 0:T], ALU.mult).then_inc(m["ov_hid"], 1)
                        dve.wait_ge(m["ov_freed"], FC * e + (FC + 1))
                        dve.wait_ge(m["ov_added"], 4 * e + 1)
                        for t in range(NT):
                            for n in range(2):
                                cols = slice(n * 512, (n + 1) * 512)
                                V.scalar_tensor_tensor(out=x[:, t, cols], in0=psum[:, 2 * t + n, :],
                                                       scalar=moe["late"][:, t, bass.ds(e, 1)], in1=x[:, t, cols],
                                                       op0=ALU.mult, op1=ALU.add).then_inc(m["ov_added"], 1)
                V.memset(st["gp"], 0.0).then_inc(x_ready[2 * l + 2], 4)

            attention()
            experts(0)
            convolution()
            experts(1)

        @block.gpsimd
        def _(pool):
            def overflow(l):
                m = M[l]
                pool.wait_ge(m["flag"], 1)
                late = pool.value_load(flag_i[0:1, l:l + 1], min_val=0, max_val=T)
                with pool.If(late > SLOTS):
                    with pool.Fori(0, EXPERTS) as e:
                        for f in range(FC):
                            pool.wait_ge(m["ov_freed"], FC * e + (f + 1))
                            cols = slice(f * P, (f + 1) * P)
                            for w, dst in (("moe_w_gate", "wg"), ("moe_w_up", "wu")):
                                pool.dma_start(ovf[dst], p[w][l, bass.ds(e, 1), :, cols].rearrange(
                                    "o (q c) f -> q (o c) f", c=KC)).then_inc(m["ov_loaded"], 16)
                            pool.dma_start(ovf["wd"], p["moe_w_down"][l, bass.ds(e, 1), cols, :].rearrange(
                                "o q f -> q (o f)")).then_inc(m["ov_loaded"], 16)

            pool.wait_ge(x_ready[1], 4)
            for name, row, n in (("conv_b_in", 0, 16), ("conv_dw_b", 16, 8), ("conv_ln_g", 24, 8),
                                 ("conv_ln_b", 32, 8)):
                pool.dma_start(conv["rows"][row:row + n, 0, :], p[name].rearrange(
                    "o (j k) -> (o j) k", k=P)).then_inc(conv_params_loaded, 16)
            taps = p["conv_dw_w"][0].rearrange("w (j k) -> (w j) k", k=P)
            pool.dma_start(conv["rows"][0:124, 1:3, :], taps.rearrange("(b r) k -> r b k", b=2)).then_inc(
                conv_params_loaded, 16)
            pool.dma_start(conv["b_out"], p["conv_b_out"][0].partition_broadcast(P)).then_inc(
                conv_params_loaded, 16)
            overflow(0)
            overflow(1)


_PARAMS = ["attn_norm", "diff_w_in", "diff_q_gain", "diff_k_gain", "diff_lambda_q1", "diff_lambda_k1", "diff_lambda_q2",
           "diff_lambda_k2", "diff_subln", "diff_w_out", "conv_norm", "conv_w_in", "conv_b_in", "conv_dw_w",
           "conv_dw_b", "conv_ln_g", "conv_ln_b", "conv_w_out", "conv_b_out", "ffn_norm", "router_group_w",
           "router_group_b", "router_expert_w", "router_expert_b", "moe_w_gate", "moe_w_up", "moe_w_down"]


def constants():
    import numpy as np

    con = np.zeros((P, C_END), np.float32)
    r = np.arange(P)
    con[:, C_IDENT:C_IDENT + P] = np.eye(P)
    con[:, C_BEFORE:C_BEFORE + P] = r[:, None] < r[None, :]
    con[:, C_ONES:C_ONES + P] = 1
    con[:, C_IOTA:C_IOTA + SLOTS] = np.arange(SLOTS)
    con[:, C_REV:C_REV + EXPERTS] = EXPERTS - np.arange(EXPERTS)
    con[[0, 64], C_EARLY:C_EARLY + 64] = 1
    con[[0, 64], C_HIDE:C_HIDE + 64] = -BIG
    inv_freq = np.float32(500000.0) ** (-np.arange(0, 2 * ROT, 2, dtype=np.float32) / np.float32(2 * ROT))
    ang = np.arange(T, dtype=np.float32)[:, None] * inv_freq[None, :]
    for t in range(NT):
        con[:, C_COS + ROT * t:C_COS + ROT * (t + 1)] = np.cos(ang[t * P:(t + 1) * P])
        con[:, C_SIN + ROT * t:C_SIN + ROT * (t + 1)] = np.sin(ang[t * P:(t + 1) * P])
    return con


def kernel(**inputs):
    import numpy as _np
    import concourse.bacc as _bacc
    from concourse import mybir as _mybir
    from concourse.bass_utils import run_bass_kernel_spmd as _run

    nc = _bacc.Bacc("TRN2", target_bir_lowering=False, num_devices=1)
    arrays = {"in_x": _np.ascontiguousarray(inputs["x"]), "in_constants": constants()}
    for name in _PARAMS:
        arrays["in_" + name] = _np.ascontiguousarray(inputs[name])
    aps = {k: nc.dram_tensor(k, a.shape, _mybir.dt.float32, kind="ExternalInput").ap() for k, a in arrays.items()}
    out = nc.dram_tensor("out", (1, T, D), _mybir.dt.float32, kind="ExternalOutput").ap()
    build(nc, aps["in_x"], aps["in_constants"], {n: aps["in_" + n] for n in _PARAMS}, out)
    r = _run(nc, [arrays], core_ids=[0])
    return r.results[0]["out"]
```

```python
from contextlib import ExitStack

import concourse.bass as bass
from concourse import mybir

P = 128
T = 256
NT = T // P
D = 1024
KC = D // P
BANK = 512
HEADS = 8
DH = 64
ROT = DH // 8
TAPS = 31
GROUPS = 4
PER_GROUP = 8
EXPERTS = GROUPS * PER_GROUP
CHOICES = GROUPS + EXPERTS
F = 512
FC = F // P
SLOTS = 64
FRONT = 2
PADDED = EXPERTS + 8
EPS = 1e-6
LAMBDA_INIT = 0.2
BIG = 1e30
TRIO = 3
POOL_CONV = (2, 5)
PE_CONV = ((6, 14), (7, TAPS))
PE_TAPS = tuple((j, tap) for j, n in PE_CONV for tap in range(n))

PRODUCTS = (TAPS + 1) // 2

SCRATCH = 8320
RING = 9
ATT_BASE = 0
MOE_PIECES = 3 * EXPERTS
MOE_BASE = (8, 8 + MOE_PIECES + 6)
CONV_BASE = 8 + MOE_PIECES

C_IDENT, C_BEFORE, C_ONES, C_IOTA, C_REV, C_EARLY, C_HIDE, C_COS, C_SIN, C_END = (
    0, 128, 256, 384, 448, 480, 608, 672, 688, 704)

IN_ORDER = (0, 2, 4, 1, 3, 5)
ROUNDS = {6: (0,), 7: (1, 2), 8: (3,), 9: (4, 5), 10: (6,), 11: (7,)}
UNITS = 16
LAG = 3
NORM_OUT = {8: 0, 10: 1, 15: 2}

PARAM_DMAS = 2 * 7
PHASES = ("att", "moe0", "conv", "moe1")


def build(nc, x_in, consts_in, p, out):
    fp32 = mybir.dt.float32
    i32 = mybir.dt.int32
    ALU = mybir.AluOpType
    ACT = mybir.ActivationFunctionType
    AX = mybir.AxisListType.X

    ctx = ExitStack()
    with ctx:
        def sb(name, shape, dt=fp32):
            return ctx.enter_context(nc.sbuf_tensor(name, shape, dt))

        def sem(name):
            return ctx.enter_context(nc.semaphore(name))

        ring = [sb(f"ring{i}", [P, 4096]) for i in range(RING)]
        x = sb("x", [P, NT, D])
        h = sb("h", [P, NT, KC, P])
        hT = sb("hT", [P, KC, T])
        con = sb("con", [P, C_END])
        norm_gain = sb("norm_gain", [P, 4, KC])
        router_w = sb("router_w", [P, 2, KC, GROUPS + EXPERTS])
        router_b = sb("router_b", [P, 2, GROUPS + EXPERTS])
        stat = sb("stat", [P, 144])
        flag_i = sb("flag_i", [P, 2], i32)
        scratch = sb("scratch", [P, SCRATCH])
        psum = ctx.enter_context(nc.psum_tensor("psum", [P, 8, BANK], fp32))

        ident = con[:, C_IDENT:C_IDENT + P]
        before = con[:, C_BEFORE:C_BEFORE + P]
        ones = con[:, C_ONES:C_ONES + P]
        iota = con[:, C_IOTA:C_IOTA + SLOTS]
        rev = con[:, C_REV:C_REV + EXPERTS]
        early = con[:, C_EARLY:C_EARLY + P]
        hide = con[:, C_HIDE:C_HIDE + 64]

        def carve(spec):
            at, views = 0, {}
            for name, *shape in spec:
                n = 1
                for s in shape:
                    n *= s
                v = scratch[:, at:at + n]
                at += n
                if len(shape) == 2:
                    v = v.rearrange("q (a b) -> q a b", a=shape[0])
                elif len(shape) == 3:
                    v = v.rearrange("q (a b c) -> q a b c", a=shape[0], b=shape[1])
                elif len(shape) == 4:
                    v = v.rearrange("q (a b c d) -> q a b c d", a=shape[0], b=shape[1], c=shape[2])
                views[name] = v
            assert at <= SCRATCH, at
            return views

        att = carve([("qk", NT, 2 * D), ("v", NT, D), ("probs", 3, 2, T),
                     ("pT", 2, P), ("junk", P), ("gains", 2, DH), ("subln", P)])
        o_rows = h[:].rearrange("q t c k -> q t (c k)")
        att["sq"] = o_rows[:, 0, 512:1024]
        att["tmp"] = o_rows[:, 1, 512:768].rearrange("q (a b) -> q a b", a=4)
        att["lam"] = att["probs"][:, 2].rearrange("q a b -> q (a b)")[:, 0:4 * DH].rearrange("q (a b) -> q a b", a=4)
        conv = carve([("u", KC, T + TAPS - 1), ("cv", KC, T), ("sig", 2, 2 * T), ("diag", 4, P),
                      ("cols", 40), ("taps", TAPS, KC), ("mean", T), ("rstd", T),
                      ("pad", 24), ("rows", 3, P), ("b_out", D)])
        conv["sq"] = h[:].rearrange("q t c k -> q (t c k)").rearrange("q (a b) -> q a b", a=KC)
        work = h[:].rearrange("q t c k -> q (t c k)")
        conv["acc"] = work[:, 0:2 * T].rearrange("q (a b) -> q a b", a=2)
        conv["prod"] = work[:, 2 * T:8 * T].rearrange("q (a b c) -> q a b c", a=3, b=2)
        moe = carve([("xg", KC, 2, TRIO * SLOTS), ("sel", NT, 2, TRIO * SLOTS), ("selw", NT, 2, SLOTS),
                     ("silu", T), ("hid", T), ("hidT", 2, P), ("combT", T), ("outs", D),
                     ("logit", NT, 36), ("ml", NT, EXPERTS), ("one", NT, EXPERTS), ("two", NT, EXPERTS),
                     ("t32", NT, EXPERTS), ("posm", NT, PADDED), ("comb", NT, PADDED),
                     ("late", NT, EXPERTS)])
        zero = moe["outs"][:, 0:BANK]
        logits_T = moe["combT"][0:CHOICES, :]
        ovf = carve([("wg", KC, P), ("wu", KC, P), ("wd", D), ("silu", T), ("hid", T)])

        st, at = {}, 0
        for name, n, cols in (("ss", 2, 0), ("ms", 2, 0), ("rstd", 2, 0), ("qms", 8, 0), ("qrstd", 8, 0),
                              ("nm", 6, 0), ("den", 6, 0), ("oss", 16, 0), ("oms", 16, 0), ("orstd", 16, 0),
                              ("lam_s", 2, 0), ("lam_e", 2, 0), ("neglam", 1, 0), ("mx", 2, 0), ("first", 2, 0), ("ge", 8, GROUPS),
                              ("pick", 8, GROUPS), ("gp", 2, 0), ("m1", 2, 0), ("m2", 2, 0), ("dm", 2, 0),
                              ("e2", 2, 0), ("spare", 10, 0)):
            st[name] = stat[:, at:at + n] if not cols else stat[:, at:at + n].rearrange("q (a b) -> q a b", b=cols)
            at += n

        arrived = [sem(f"arrived{i}") for i in range(RING)]
        piece_used = sem("piece_used")
        x_loaded = sem("x_loaded")
        consts_loaded = sem("consts_loaded")
        att_params_loaded = sem("att_params_loaded")
        lambda_params_loaded = sem("lambda_params_loaded")
        params_loaded = sem("params_loaded")
        conv_params_loaded = sem("conv_params_loaded")
        out_stored = sem("out_stored")
        dve_step = sem("dve_step")
        x_ready = [None] + [sem(f"x_ready_{n}") for n in PHASES[1:]] + [sem("x_final")]
        squares = sem("squares")
        inv_ms = sem("inv_ms")
        rstd_ready = sem("rstd_ready")
        rows_ready = [sem(f"rows_{n}") for n in PHASES]
        rows_turned = [sem(f"rows_turned_{n}") for n in PHASES]
        hT_ready = [sem(f"hT_ready_{n}") for n in PHASES]
        hT_other = [sem(f"hT_other_{n}") for n in PHASES]
        gains_loaded = sem("gains_loaded")
        A = {n: sem("att_" + n) for n in (
            "qkv", "qkv_out", "ms", "rstd", "rotated", "turned", "turned_out", "scores", "max", "neg_max",
            "exp", "mixed", "probs_turned", "pT_ready", "pv", "o_ready", "o_ms", "o_rstd", "o_normed", "o_turned",
            "oT_ready", "lam_sum", "lam_exp")}
        C = {n: sem("conv_" + n) for n in (
            "params_turned", "params", "glu", "sig", "u_ready", "diag", "diag_used",
            "pe_conv_out", "dve_conv", "products", "pool_step", "pool_conv", "sum", "centred", "squared", "var", "inv", "rstd", "scaled", "act")}
        M = [{n: sem(f"moe{l}_" + n) for n in (
            "logits", "logits_out", "group_in", "group_exp", "top_in", "top_exp", "picked", "pos", "sel", "pair", "selw", "flag",
            "first_gathered", "first_dve", "first_act",
            "gathered", "xg", "silu", "hid", "hid_turned", "hidT", "comb_turned", "combT", "outs",
            "combined", "zero", "ov_loaded", "ov_freed", "ov_gu", "ov_silu", "ov_hid",
            "ov_added")} for l in range(2)]

        block = ctx.enter_context(nc.Block())

        def unit(u):
            return u % 8 // 4, 4 * (u // 8) + u % 4

        def turned_product(n):
            return None if n // 2 % 3 == 2 else n - 2 * (n // 6)

        def first_rows(k):
            n, c = k // KC, k % KC
            at = (1 - n) * 2 * SLOTS
            return moe["xg"][:, c, n, at:TRIO * SLOTS], psum[:, 5 + k % 3, 0:TRIO * SLOTS - at]

        def gate_at(l, e):
            return MOE_BASE[l] if isinstance(e, int) and e == 0 else 3 * e + (MOE_BASE[l] - 1)

        def up_at(l, e):
            return gate_at(l, e) + 1

        def down_at(l, e):
            return 3 * e + (MOE_BASE[l] + 4) if not (isinstance(e, int) and e == EXPERTS - 1) else MOE_BASE[l] + 95

        @block.sync
        def _(sp):
            def load(place, src, slot=None, lap=None):
                slot = place % RING if slot is None else slot
                if not isinstance(place, int) or place >= RING:
                    sp.wait_ge(piece_used, place - RING + 1)
                sp.dma_start(ring[slot][:], src).then_inc(arrived[slot], 16)

            def columns(w, n):
                return w[:, n * 512:(n + 1) * 512].rearrange("(p c) f -> p c f", c=KC)

            def rows(w, half):
                return w[half * 512:(half + 1) * 512, :].rearrange("(c p) f -> p c f", p=P)

            def up_src(w, l, e):
                return w[l, bass.ds(e, 1)].rearrange("o (p c) f -> p (o c f)", c=KC)

            def down_src(l, e):
                return p["moe_w_down"][l, bass.ds(e, 1)].rearrange("o (c p) f -> p (o c) f", p=P)

            def load_moe(l):
                base = MOE_BASE[l]
                load(base, up_src(p["moe_w_gate"], l, 0))
                load(base + 1, up_src(p["moe_w_up"], l, 0))
                with sp.Fori(0, 5) as i:
                    for k in range(6):
                        at = base + 2 + 3 * k
                        load(18 * i + at, up_src(p["moe_w_gate"], l, 6 * i + k + 1), at % RING)
                        load(18 * i + at + 1, up_src(p["moe_w_up"], l, 6 * i + k + 1), (at + 1) % RING)
                        load(18 * i + at + 2, down_src(l, 6 * i + k), (at + 2) % RING)
                at = base + 92
                load(at, up_src(p["moe_w_gate"], l, EXPERTS - 1))
                load(at + 1, up_src(p["moe_w_up"], l, EXPERTS - 1))
                load(at + 2, down_src(l, EXPERTS - 2))
                load(at + 3, down_src(l, EXPERTS - 1))

            sp.dma_start(x[:], x_in[0].rearrange("(t p) d -> p t d", p=P)).then_inc(x_loaded, 16)
            sp.dma_start(norm_gain[:, 0, :], p["attn_norm"].rearrange("o (q c) -> q (o c)", c=KC)).then_inc(
                gains_loaded, 16)
            sp.dma_start(con[:], consts_in).then_inc(consts_loaded, 16)
            for n, name in enumerate(("diff_q_gain", "diff_k_gain")):
                sp.dma_start(att["gains"][:, n, :], p[name][0].partition_broadcast(P)).then_inc(att_params_loaded, 16)
            w = p["diff_w_in"][0]
            for n in range(6):
                load(ATT_BASE + n, columns(w, IN_ORDER[n]))
            sp.dma_start(att["subln"], p["diff_subln"][0].partition_broadcast(P)).then_inc(lambda_params_loaded, 16)
            for n, name in enumerate(("q1", "k1", "q2", "k2")):
                sp.dma_start(att["lam"][:, n, :], p["diff_lambda_" + name][0].partition_broadcast(P)).then_inc(
                    lambda_params_loaded, 16)
            for half in range(2):
                load(ATT_BASE + 6 + half, rows(p["diff_w_out"][0], half))
            sp.dma_start(norm_gain[:, 2, :], p["conv_norm"].rearrange("o (q c) -> q (o c)", c=KC)).then_inc(
                gains_loaded, 16)
            for l in range(2):
                sp.dma_start(norm_gain[:, 2 * l + 1, :], p["ffn_norm"][l].rearrange("(q c) -> q c", c=KC)).then_inc(
                    gains_loaded, 16)
                sp.dma_start(router_w[:, l, :, 0:GROUPS], p["router_group_w"][l].rearrange(
                    "(q c) g -> q c g", c=KC)).then_inc(params_loaded, 16)
                for g in range(GROUPS):
                    at = GROUPS + g * PER_GROUP
                    sp.dma_start(router_w[:, l, :, at:at + PER_GROUP], p["router_expert_w"][l, g].rearrange(
                        "(q c) e -> q c e", c=KC)).then_inc(params_loaded, 16)
                sp.dma_start(router_b[:, l, 0:GROUPS], p["router_group_b"][l].partition_broadcast(P)).then_inc(
                    params_loaded, 16)
                sp.dma_start(router_b[:, l, GROUPS:], p["router_expert_b"][l].rearrange(
                    "g e -> (g e)").partition_broadcast(P)).then_inc(params_loaded, 16)
            load_moe(0)
            for n, c in enumerate((0, 2, 1, 3)):
                load(CONV_BASE + n, columns(p["conv_w_in"][0], c))
            for half in range(2):
                load(CONV_BASE + 4 + half, rows(p["conv_w_out"][0], half))
            load_moe(1)
            sp.wait_ge(x_ready[4], 4)
            for t in range(NT):
                sp.dma_start(out[0, t * P:(t + 1) * P, :], x[:, t, :]).then_inc(out_stored, 16)
            sp.wait_ge(out_stored, 16 * NT)

        def has_arrived(eng, place, slot=None, lap=0):
            eng.wait_ge(arrived[place % RING], 16 * (place // RING + lap + 1))

        @block.tensor
        def _(pe):
            def turn_rows(ph):
                for r in range(4):
                    t, half = r // 2, r % 2
                    if half == 0:
                        pe.wait_ge(rows_ready[ph], t + 1)
                    for j in range(4):
                        mm = pe.transpose(psum[:, 4 + r, j * P:(j + 1) * P], h[:, t, 4 * half + j, :], ident)
                    mm.then_inc(rows_turned[ph], 1)

            def all_turned(ph, t):
                pe.wait_ge(hT_ready[ph], t + 1)
                pe.wait_ge(hT_other[ph], t + 1)

            def attention():
                turn_rows(0)

                bank6 = [hT_ready[0], 2]

                def turn(blocks, signal, reader, count):
                    pe.wait_ge(*bank6)
                    for j, block in enumerate(blocks):
                        mm = pe.transpose(psum[:, 6, j * P:(j + 1) * P], block, ident)
                    mm.then_inc(signal, 1)
                    bank6[:] = [reader, count]

                def turn_heads(n):
                    r, t, at = turned_product(n), n % 2, IN_ORDER[n // 2] * 512
                    pe.wait_ge(A["rotated"], r + 1)
                    turn([att["qk"][:, t, at + j * P:at + (j + 1) * P] for j in range(4)], A["turned"],
                         A["turned_out"], r + 1)

                def scores(u):
                    t, hd = unit(u)
                    pe.wait_ge(A["turned_out"], 4 + 4 * (u // 8))
                    if u >= 2:
                        pe.wait_ge(A["exp"], 2 * u - 2)
                    nk = (t + 1) * P
                    for c in range(2):
                        half, bank = slice(c * DH, (c + 1) * DH), 2 + 2 * (u % 2) + c
                        pe.matmul(psum[:, bank, 0:nk], att["qk"][half, t, hd * P:(hd + 1) * P],
                                  att["qk"][half, 0:t + 1, D + hd * P:D + (hd + 1) * P], start=True, stop=False)
                        mm = pe.matmul(psum[:, bank, nk - 64:nk], early[half, :], hide[half, :], start=False, stop=True)
                    mm.then_inc(A["scores"], 1)

                def turn_probs(u):
                    t, hd = unit(u)
                    pe.wait_ge(A["mixed"], u + 1)
                    turn([att["probs"][:, u % 3, 0, k * P:(k + 1) * P] for k in range(t + 1)], A["probs_turned"],
                         A["pT_ready"], u + 1)

                def values(u):
                    t, hd = unit(u)
                    pe.wait_ge(A["pT_ready"], u + 1)
                    pe.wait_ge(A["qkv_out"], 6 + 6 * (u // 8))
                    if u >= 1:
                        pe.wait_ge(A["o_ready"], 2 * u)
                    for k in range(t + 1):
                        mm = pe.matmul(psum[:, 7, 0:P], att["pT"][:, k, :], att["v"][:, k, hd * P:(hd + 1) * P],
                                       start=(k == 0), stop=(k == t))
                    mm.then_inc(A["pv"], 1)

                def turn_out(b):
                    pe.wait_ge(A["o_normed"], b + 1)
                    turn([o_rows[:, b % 2, (4 * (b // 2) + j) * P:(4 * (b // 2) + j + 1) * P] for j in range(4)],
                         A["o_turned"], A["oT_ready"], b + 1)

                def round_of(j):
                    if j < UNITS:
                        scores(j)
                    if LAG <= j < UNITS + LAG:
                        values(j - LAG)
                    if 2 <= j < UNITS + 2:
                        turn_probs(j - 2)
                    if j - 1 in NORM_OUT:
                        turn_out(NORM_OUT[j - 1])

                for n in range(12):
                    if n < 2:
                        all_turned(0, n)
                    if n % 2 == 0:
                        has_arrived(pe, ATT_BASE + n // 2)
                    if n >= 2:
                        pe.wait_ge(A["qkv_out"], n - 1)
                    w = ring[(ATT_BASE + n // 2) % RING][:].rearrange("q (c f) -> q c f", c=KC)
                    for c in range(KC):
                        mm = pe.matmul(psum[:, n % 2, :], hT[:, c, (n % 2) * P:(n % 2 + 1) * P], w[:, c, :],
                                       start=(c == 0), stop=(c == KC - 1))
                    mm.then_inc(A["qkv"] if n % 2 == 0 else piece_used, 1)
                    if n >= 2 and turned_product(n - 2) is not None:
                        turn_heads(n - 2)
                    for j in ROUNDS.get(n, ()):
                        round_of(j)
                for j in range(8, UNITS + LAG):
                    round_of(j)
                pe.wait_ge(A["exp"], 2 * UNITS)
                pe.wait_ge(A["qkv_out"], 12)
                for half in range(2):
                    has_arrived(pe, ATT_BASE + 6 + half)
                    if half == 1:
                        turn_out(3)
                    pe.wait_ge(A["oT_ready"], 2 * half + 2)
                    w = ring[(ATT_BASE + 6 + half) % RING][:].rearrange("q (c f) -> q c f", c=4)
                    for c in range(4):
                        for t in range(NT):
                            for n in range(2):
                                mm = pe.matmul(psum[:, 2 * t + n, :], att["qk"][:, t, (4 * half + c) * P:(4 * half + c + 1) * P],
                                               w[:, c, n * 512:(n + 1) * 512], start=(half + c == 0),
                                               stop=(half == 1 and c == 3))
                    mm.then_inc(piece_used, 1)

            def convolution():
                turn_rows(2)
                all_turned(2, 1)
                pe.wait_ge(conv_params_loaded, 16 * 6)
                pe.transpose(psum[:, 4, 0:40], conv["rows"][0:40, 0, :], ident[0:40, 0:40])
                for b in range(2):
                    mm = pe.transpose(psum[:, 4, 40 + 124 * b:164 + 124 * b], conv["rows"][0:124, 1 + b, :],
                                      ident[0:124, 0:124])
                mm.then_inc(C["params_turned"], 1)
                for b in range(4):
                    for gate in range(2):
                        n = 2 * (b // 2) + gate
                        has_arrived(pe, CONV_BASE + n)
                        w = ring[(CONV_BASE + n) % RING][:].rearrange("q (c f) -> q c f", c=KC)
                        bank = 4 * (b // 2) + 2 * gate + b % 2
                        if bank == 4:
                            pe.wait_ge(C["params"], 1)
                        for jj in range(2):
                            j = 2 * (b % 2) + jj
                            for c in range(KC):
                                mm = pe.matmul(psum[:, bank, jj * T:(jj + 1) * T], w[:, c, j * P:(j + 1) * P],
                                               hT[:, c, :], start=(c == 0), stop=(c == KC - 1))
                        if b % 2 == 1:
                            mm.then_inc(piece_used, 1)
                        elif gate:
                            mm.then_inc(C["glu"], 1)
                pe.wait_ge(C["u_ready"], 4)
                for n, (j, tap) in enumerate(PE_TAPS):
                    pe.wait_ge(C["diag"], n + 1)
                    pe.matmul(psum[:, j % 2, 0:T], conv["diag"][:, n % 4, :], conv["u"][:, j, tap:tap + T],
                              start=(tap == 0), stop=((j, tap + 1) not in PE_TAPS)).then_inc(C["diag_used"], 1)
                order = (0, 1, 2, 3, 4, 5, 7, 6)
                for j in order:
                    if j == 7:
                        pe.wait_ge(C["pe_conv_out"], 2)
                    elif j in POOL_CONV:
                        pe.wait_ge(C["pool_conv"], POOL_CONV.index(j) + 1)
                    else:
                        pe.wait_ge(C["dve_conv"], {0: 1, 1: 1, 3: 2, 4: 3, 6: 4}[j])
                    mm = pe.matmul(psum[:, 4, 0:T], ones, conv["cv"][:, j, :], start=(j == order[0]),
                                   stop=(j == order[-1]))
                mm.then_inc(C["sum"], 1)
                for j in range(KC):
                    pe.wait_ge(C["squared"], j + 1)
                    mm = pe.matmul(psum[:, 5, 0:T], ones, conv["sq"][:, j, :], start=(j == 0), stop=(j == KC - 1))
                mm.then_inc(C["var"], 1)
                for half in range(2):
                    has_arrived(pe, CONV_BASE + 4 + half)
                    w = ring[(CONV_BASE + 4 + half) % RING][:].rearrange("q (c f) -> q c f", c=4)
                    for c in range(4):
                        pe.wait_ge(C["act"], 4 * half + c + 1)
                        for t in range(NT):
                            for n in range(2):
                                mm = pe.matmul(psum[:, 2 * t + n, :], conv["sq"][:, 4 * half + c, t * P:(t + 1) * P],
                                               w[:, c, n * 512:(n + 1) * 512], start=(half + c == 0),
                                               stop=(half == 1 and c == 3))
                    mm.then_inc(piece_used, 1)

            def experts(l):
                m, base = M[l], MOE_BASE[l]
                turn_rows(2 * l + 1)
                if l == 0:
                    pe.wait_ge(params_loaded, PARAM_DMAS * 16)
                for t in range(NT):
                    all_turned(2 * l + 1, t)
                    for c in range(KC):
                        mm = pe.matmul(psum[0:CHOICES, 4 + 2 * t, 0:P], router_w[:, l, c, :],
                                       hT[:, c, t * P:(t + 1) * P], start=(c == 0), stop=(c == KC - 1))
                    mm.then_inc(m["logits"], 1)
                for t in range(NT):
                    pe.wait_ge(m["logits_out"], t + 1)
                    mm = pe.transpose(psum[:, 5, 64 * t:64 * t + CHOICES],
                                      logits_T[:, t * P:(t + 1) * P], ident[0:CHOICES, 0:CHOICES])
                mm.then_inc(m["logits"], 1)
                pe.wait_ge(m["zero"], 1)
                for b in range(4):
                    pe.matmul(psum[:, b, :], zero[:, 0:P], zero, start=True, stop=False,
                              skip_group_check=True)
                pe.wait_ge(m["picked"], 1)
                picked = moe["t32"]
                pe.matmul(psum[:, 6, 0:32], before, picked[:, 0, :], start=True, stop=True)
                pe.matmul(psum[:, 6, 32:64], ones, picked[:, 0, :], start=True, stop=False)
                pe.matmul(psum[:, 6, 32:64], before, picked[:, 1, :], start=False, stop=True).then_inc(m["pos"], 1)
                pe.matmul(psum[:, 4, 0:32], ones, picked[:, 0, :], start=True, stop=False)
                pe.matmul(psum[:, 4, 0:32], ones, picked[:, 1, :], start=False, stop=True).then_inc(m["pos"], 1)

                def gather(q, buf, c):
                    pe.wait_ge(m["xg"], 8 * q + (c - 15))
                    for t in range(NT):
                        mm = pe.matmul(psum[:, 7, 0:TRIO * SLOTS], h[:, t, c, :], moe["sel"][:, t, buf, :],
                                       start=(t == 0), stop=(t == NT - 1))
                    mm.then_inc(m["gathered"], 1)

                def up(place, lap, buf, j, bankcol):
                    has_arrived(pe, place, lap=lap)
                    w = ring[place % RING][:].rearrange("q (c f) -> q c f", c=KC)
                    for c in range(KC):
                        for hf in range(2):
                            mm = pe.matmul(psum[hf * SLOTS:(hf + 1) * SLOTS, 4, bankcol:bankcol + 256],
                                           moe["xg"][:, c, buf, j * SLOTS:(j + 1) * SLOTS],
                                           w[:, c, hf * 256:(hf + 1) * 256], start=(c == 0), stop=(c == KC - 1))
                    mm.then_inc(piece_used, 1)

                def turn_hidden(e):
                    pe.wait_ge(m["hid"], e + 1)
                    for j in range(2):
                        mm = pe.transpose(psum[:, 6, j * P:(j + 1) * P], moe["hid"][:, j * P:(j + 1) * P], ident)
                    mm.then_inc(m["hid_turned"], 1)

                def turn_combine(pair):
                    pe.wait_ge(m["selw"], pair + 1)
                    pe.wait_ge(m["hidT"], 2 * pair + 2)
                    for t in range(NT):
                        mm = pe.transpose(psum[:, 6, 256 + t * P:256 + (t + 1) * P],
                                          moe["selw"][:, t].rearrange("q a b -> q (a b)"), ident)
                    mm.then_inc(m["comb_turned"], 1)

                def down(e, odd, place, lap):
                    has_arrived(pe, place, lap=lap)
                    pe.wait_ge(m["hidT"], e + 1)
                    if odd:
                        pe.wait_ge(m["outs"], 2 * e)
                    w = ring[place % RING][:].rearrange("q (c f) -> q c f", c=FC)
                    for f in range(FC):
                        for hf in range(2):
                            mm = pe.matmul(psum[hf * SLOTS:(hf + 1) * SLOTS, 5, :],
                                           moe["hidT"][:, f % 2, (f // 2) * SLOTS:(f // 2 + 1) * SLOTS],
                                           w[:, f, hf * 512:(hf + 1) * 512], start=(f == 0), stop=(f == FC - 1))
                    mm.then_inc(piece_used, 1)

                def combine(pair, last=False):
                    pe.wait_ge(m["combT"], pair + 1)
                    pe.wait_ge(m["outs"], 4 * pair + 4)
                    for t in range(NT):
                        for hf in range(2):
                            mm = pe.matmul(psum[:, 2 * hf + t, :], moe["combT"][:, t * P:(t + 1) * P],
                                           moe["outs"][:, hf * 512:(hf + 1) * 512], start=False, stop=last,
                                           skip_group_check=True)
                    mm.then_inc(m["combined"], 1)

                def step(i, k):
                    e, q, buf, j = 6 * i + (k + 1), 2 * i + (1 + k // TRIO), (1 + k // TRIO) % 2, k % TRIO
                    at, lap = base + 2 + 3 * k, 2 * i
                    if j == 0:
                        pe.wait_ge(m["xg"], 8 * q - 7)
                        pe.wait_ge(m["sel"], q + 2)
                    pe.wait_ge(m["hid"], e)
                    up(at, lap, buf, j, 0)
                    gather(q + 1, 1 - buf, 3 * j)
                    turn_hidden(e - 1)
                    up(at + 1, lap, buf, j, 256)
                    gather(q + 1, 1 - buf, 3 * j + 1)
                    odd, pair = k % 2 == 1, 3 * i + k // 2
                    if odd:
                        turn_combine(pair)
                    down(e - 1, odd, at + 2, lap)
                    if 3 * j + 2 < KC:
                        gather(q + 1, 1 - buf, 3 * j + 2)
                    if odd:
                        combine(pair)

                def first_gather(n, c):
                    at, at_end = ((2 * SLOTS, TRIO * SLOTS), (0, TRIO * SLOTS))[n]
                    k = KC * n + c
                    if k >= 3:
                        pe.wait_ge(m["first_act" if k % 2 == 0 else "first_dve"], (k - 3) // 2 + 1)
                    for t in range(NT):
                        mm = pe.matmul(psum[:, 5 + k % 3, 0:at_end - at], h[:, t, c, :],
                                       moe["sel"][:, t, n, at:at_end], start=(t == 0), stop=(t == NT - 1))
                    mm.then_inc(m["first_gathered"], 1)

                pe.wait_ge(m["sel"], 1)
                for c in range(KC):
                    first_gather(0, c)
                pe.wait_ge(m["sel"], 2)
                pe.wait_ge(m["first_act"], 4)
                pe.wait_ge(m["first_dve"], 4)
                pe.wait_ge(m["flag"], 1)
                up(base, 0, 0, 2, 0)
                for c in range(4):
                    first_gather(1, c)
                up(base + 1, 0, 0, 2, 256)
                for c in range(4, KC):
                    first_gather(1, c)
                pe.wait_ge(m["first_act"], 7)
                with pe.Fori(0, 5) as i:
                    for k in range(6):
                        step(i, k)
                e, at = EXPERTS - 1, base + 92
                pe.wait_ge(m["xg"], 8 * 11 - 7)
                pe.wait_ge(m["hid"], e)
                up(at, 0, 1, 0, 0)
                turn_hidden(e - 1)
                up(at + 1, 0, 1, 0, 256)
                down(e - 1, False, at + 2, 0)
                turn_hidden(e)
                turn_combine(EXPERTS // 2 - 1)
                down(e, True, at + 3, 0)
                combine(EXPERTS // 2 - 1, last=True)

                pe.wait_ge(m["flag"], 1)
                late = pe.value_load(flag_i[0:1, l:l + 1], min_val=0, max_val=T)
                with pe.If(late > SLOTS):
                    with pe.Fori(0, EXPERTS) as e:
                        pe.wait_ge(m["ov_added"], 4 * e + 1)
                        for f in range(FC):
                            pe.wait_ge(m["ov_loaded"], 48 * (FC * e + f + 1))
                            for bank, wt in ((4, "wg"), (5, "wu")):
                                for c in range(KC):
                                    mm = pe.matmul(psum[:, bank, 0:T], ovf[wt][:, c, :], hT[:, c, :], start=(c == 0),
                                                   stop=(c == KC - 1))
                            mm.then_inc(m["ov_gu"], 1)
                            pe.wait_ge(m["ov_hid"], FC * e + f + 1)
                            for t in range(NT):
                                for n in range(2):
                                    mm = pe.matmul(psum[:, 2 * t + n, :], ovf["hid"][:, t * P:(t + 1) * P],
                                                   ovf["wd"][:, n * 512:(n + 1) * 512], start=(f == 0),
                                                   stop=(f == FC - 1))
                            mm.then_inc(m["ov_freed"], 1)

            pe.wait_ge(consts_loaded, 16)
            attention()
            experts(0)
            convolution()
            experts(1)

        @block.scalar
        def _(act):
            brought = [0]

            def bring_table(func):
                nc.scalar.activation(st["spare"][:, brought[0]:brought[0] + 1], ones[:, 0:1], func)
                brought[0] += 1

            def norm(ph):
                if ph > 0:
                    bring_table(ACT.Sqrt)
                for t in range(NT):
                    if ph > 0:
                        act.wait_ge(x_ready[ph], 2 * (t + 1))
                    elif t == 0:
                        act.wait_ge(x_loaded, 16)
                    nc.scalar.activation(h[:, t].rearrange("q c k -> q (c k)"), x[:, t, :], ACT.Square,
                                         accum_out=st["ss"][:, t:t + 1]).then_inc(squares, 1)
                    act.wait_ge(inv_ms, NT * ph + t + 1)
                    nc.scalar.activation(st["rstd"][:, t:t + 1], st["ms"][:, t:t + 1], ACT.Sqrt).then_inc(
                        rstd_ready, 1)
                for t in range(NT):
                    if t == 0:
                        act.wait_ge(gains_loaded, 16 * (1 if ph == 0 else 4))
                    act.wait_ge(rows_turned[ph], 2 * t + 2)
                    for j in range(4):
                        ins = nc.scalar.activation(hT[:, 4 + j, t * P:(t + 1) * P], psum[:, 5 + 2 * t, j * P:(j + 1) * P],
                                                   ACT.Copy, scale=norm_gain[:, ph, 4 + j:5 + j])
                    ins.then_inc(hT_other[ph], 1)

            def attention():
                norm(0)
                act.wait_ge(consts_loaded, 16)

                def exps(u):
                    t, hd = unit(u)
                    act.wait_ge(A["neg_max"], u + 1)
                    if u >= 3:
                        act.wait_ge(A["probs_turned"], u - 2)
                    nk = (t + 1) * P
                    for c in range(2):
                        at = 2 * (u % 3) + c
                        nc.scalar.activation(att["probs"][:, u % 3, c, 0:nk], psum[:, 2 + 2 * (u % 2) + c, 0:nk],
                                             ACT.Exp, bias=st["nm"][:, at:at + 1], scale=DH ** -0.5,
                                             accum_out=st["den"][:, at:at + 1]).then_inc(A["exp"], 1)

                def outputs(u):
                    t, hd = unit(u)
                    act.wait_ge(A["pv"], u + 1)
                    nc.scalar.activation(o_rows[:, t, hd * P:(hd + 1) * P], psum[:, 7, 0:P], ACT.Copy).then_inc(
                        A["o_ready"], 1)
                    if u >= 1:
                        act.wait_ge(A["o_ready"], 2 * u)
                    nc.scalar.activation(att["junk"], psum[:, 7, 0:P], ACT.Square,
                                         accum_out=st["oss"][:, u:u + 1]).then_inc(A["o_ready"], 1)

                def probs_out(u):
                    t, hd = unit(u)
                    act.wait_ge(A["probs_turned"], u + 1)
                    nc.scalar.activation(att["pT"][:, 0:t + 1, :].rearrange("q a b -> q (a b)"),
                                         psum[:, 6, 0:(t + 1) * P], ACT.Copy).then_inc(A["pT_ready"], 1)

                def norm_out(b):
                    act.wait_ge(A["o_ms"], b + 1)
                    sl = slice(4 * b, 4 * b + 4)
                    nc.scalar.activation(st["orstd"][:, sl], st["oms"][:, sl], ACT.Sqrt).then_inc(A["o_rstd"], 1)

                def turned_out(b):
                    act.wait_ge(A["o_turned"], b + 1)
                    nc.scalar.activation(att["qk"][:, b % 2, 512 * (b // 2):512 * (b // 2 + 1)], psum[:, 6, :],
                                         ACT.Copy).then_inc(A["oT_ready"], 1)

                def round_of(j):
                    if j < UNITS:
                        exps(j)
                    if LAG <= j < UNITS + LAG:
                        outputs(j - LAG)
                    if 2 <= j < UNITS + 2:
                        probs_out(j - 2)
                    if j in NORM_OUT:
                        norm_out(NORM_OUT[j])
                    if j - 1 in NORM_OUT:
                        turned_out(NORM_OUT[j - 1])

                for n in range(12):
                    if n % 2 == 0:
                        act.wait_ge(A["qkv"], n // 2 + 1)
                    else:
                        act.wait_ge(piece_used, ATT_BASE + n // 2 + 1)
                    at = IN_ORDER[n // 2] * 512
                    dst = att["qk"][:, n % 2, at:at + 512] if at < 2 * D else att["v"][:, n % 2, at - 2 * D:at - 2 * D + 512]
                    nc.scalar.activation(dst, psum[:, n % 2, :], ACT.Copy).then_inc(A["qkv_out"], 1)
                    if n >= 2 and turned_product(n - 2) is not None:
                        act.wait_ge(A["turned"], turned_product(n - 2) + 1)
                        at = IN_ORDER[(n - 2) // 2] * 512
                        nc.scalar.activation(att["qk"][:, n % 2, at:at + 512], psum[:, 6, :], ACT.Copy).then_inc(
                            A["turned_out"], 1)
                    for j in ROUNDS.get(n, ()):
                        round_of(j)
                    if turned_product(n) is not None:
                        act.wait_ge(A["ms"], turned_product(n) + 1)
                        nc.scalar.activation(st["qrstd"], st["qms"], ACT.Sqrt).then_inc(A["rstd"], 1)
                    if n == 5:
                        act.wait_ge(A["lam_sum"], 1)
                        nc.scalar.activation(st["lam_e"], st["lam_s"], ACT.Exp).then_inc(A["lam_exp"], 1)
                for j in range(8, UNITS + LAG):
                    round_of(j)
                norm_out(3)
                turned_out(3)

            def convolution():
                norm(2)
                act.wait_ge(C["params"], 1)
                bring_table(ACT.Sigmoid)

                def sigmoids(b):
                    if b % 2 == 0:
                        act.wait_ge(C["glu"], b // 2 + 1)
                    else:
                        act.wait_ge(piece_used, CONV_BASE + b + 1)
                    if b >= 2:
                        act.wait_ge(C["u_ready"], b - 1)
                    for jj in range(2):
                        j = 2 * b + jj
                        nc.scalar.activation(conv["sig"][:, b % 2, jj * T:(jj + 1) * T],
                                             psum[:, 4 * (b // 2) + 2 + b % 2, jj * T:(jj + 1) * T], ACT.Sigmoid,
                                             bias=conv["cols"][:, 8 + j:9 + j]).then_inc(C["sig"], 1)

                def products(i, n):
                    j = POOL_CONV[i]
                    if n == 0:
                        act.wait_ge(C["u_ready"], j // 2 + 1)
                        if i > 0:
                            act.wait_ge(C["pool_conv"], i)
                    if n >= 4:
                        act.wait_ge(C["pool_step"], (PRODUCTS - 1) * i + n - 3)
                    for k in range(min(2, TAPS - 2 * n)):
                        tap = 2 * n + k
                        src, weight = conv["u"][:, j, tap:tap + T], conv["taps"][:, tap, j:j + 1]
                        if tap == 0:
                            ins = nc.scalar.activation(conv["acc"][:, 0, :], src, ACT.Identity, scale=weight,
                                                       bias=conv["cols"][:, 16 + j:17 + j])
                        else:
                            dst = conv["acc"][:, 1, :] if tap == 1 else conv["prod"][:, n % 3, k, :]
                            ins = nc.scalar.activation(dst, src, ACT.Copy, scale=weight)
                    ins.then_inc(C["products"], 1)

                def diagonal(n):
                    j, tap = PE_TAPS[n]
                    if n >= 4:
                        act.wait_ge(C["diag_used"], n - 3)
                    nc.scalar.activation(conv["diag"][:, n % 4, :], ident, ACT.Copy,
                                         scale=conv["taps"][:, tap, j:j + 1]).then_inc(C["diag"], 1)

                def taps_out(i):
                    j, n = PE_CONV[i]
                    act.wait_ge(C["diag_used"], PE_CONV[0][1] * i + n)
                    nc.scalar.activation(conv["cv"][:, j, :], psum[:, j % 2, 0:T], ACT.Identity,
                                         bias=conv["cols"][:, 16 + j:17 + j]).then_inc(C["pe_conv_out"], 1)

                sigmoids(0)
                sigmoids(1)
                for n in range(10):
                    products(0, n)
                sigmoids(2)
                for n in range(10, PRODUCTS):
                    products(0, n)
                products(1, 0)
                products(1, 1)
                sigmoids(3)
                for n in range(2, PRODUCTS):
                    for k in range(3 * (n - 2), 3 * (n - 1)):
                        diagonal(k)
                        if k == PE_CONV[0][1] + 3:
                            taps_out(0)
                    products(1, n)
                for k in range(3 * (PRODUCTS - 2), len(PE_TAPS)):
                    diagonal(k)
                taps_out(1)
                bring_table(ACT.Sqrt)
                for j in range(KC):
                    act.wait_ge(C["centred"], j + 1)
                    nc.scalar.activation(conv["sq"][:, j, :], conv["cv"][:, j, :], ACT.Square).then_inc(C["squared"], 1)
                act.wait_ge(C["inv"], 1)
                nc.scalar.activation(conv["rstd"], conv["mean"], ACT.Sqrt).then_inc(C["rstd"], 1)
                bring_table(ACT.Silu)
                for j in range(KC):
                    act.wait_ge(C["scaled"], j + 1)
                    nc.scalar.activation(conv["sq"][:, j, :], conv["cv"][:, j, :], ACT.Silu,
                                         scale=conv["cols"][:, 24 + j:25 + j],
                                         bias=conv["cols"][:, 32 + j:33 + j]).then_inc(C["act"], 1)

            def experts(l):
                m = M[l]
                norm(2 * l + 1)
                for t in range(NT):
                    act.wait_ge(m["logits"], t + 1)
                    nc.scalar.activation(logits_T[:, t * P:(t + 1) * P], psum[0:CHOICES, 4 + 2 * t, 0:P],
                                         ACT.Copy).then_inc(m["logits_out"], 1)
                bring_table(ACT.Exp)
                act.wait_ge(m["group_in"], 1)
                nc.scalar.activation(st["ge"], st["ge"], ACT.Exp).then_inc(m["group_exp"], 1)
                act.wait_ge(m["top_in"], 1)
                nc.scalar.activation(st["e2"], st["dm"], ACT.Exp).then_inc(m["top_exp"], 1)
                bring_table(ACT.Silu)

                def silu(e):
                    act.wait_ge(piece_used, up_at(l, e) + 1)
                    nc.scalar.activation(moe["silu"], psum[:, 4, 0:256], ACT.Silu).then_inc(m["silu"], 1)

                def hidden_out(e):
                    act.wait_ge(m["hid_turned"], e + 1)
                    nc.scalar.activation(moe["hidT"].rearrange("q a b -> q (a b)"), psum[:, 6, 0:256],
                                         ACT.Copy).then_inc(m["hidT"], 1)

                def down_out(e, odd):
                    act.wait_ge(piece_used, down_at(l, e) + 1)
                    for hf in range(2):
                        nc.scalar.activation(moe["outs"][odd * SLOTS:(odd + 1) * SLOTS, hf * 512:(hf + 1) * 512],
                                             psum[hf * SLOTS:(hf + 1) * SLOTS, 5, :], ACT.Copy).then_inc(m["outs"], 1)

                def first_rows_in(k):
                    act.wait_ge(m["first_gathered"], k + 1)
                    dst, bank = first_rows(k)
                    nc.scalar.activation(dst, bank, ACT.Copy, scale=norm_gain[:, 2 * l + 1, k % KC:k % KC + 1]).then_inc(
                        m["first_act"], 1)

                for k in (1, 3, 5, 7, 9, 11):
                    first_rows_in(k)
                silu(0)
                first_rows_in(13)
                with act.Fori(0, 5) as i:
                    for k in range(6):
                        hidden_out(6 * i + k)
                        silu(6 * i + (k + 1))
                        down_out(6 * i + k, k % 2)
                hidden_out(EXPERTS - 2)
                silu(EXPERTS - 1)
                down_out(EXPERTS - 2, 0)
                hidden_out(EXPERTS - 1)
                down_out(EXPERTS - 1, 1)

                act.wait_ge(m["flag"], 1)
                late = act.value_load(flag_i[0:1, l:l + 1], min_val=0, max_val=T)
                with act.If(late > SLOTS):
                    with act.Fori(0, EXPERTS) as e:
                        for f in range(FC):
                            act.wait_ge(m["ov_gu"], FC * e + f + 1)
                            nc.scalar.activation(ovf["silu"], psum[:, 4, 0:T], ACT.Silu).then_inc(m["ov_silu"], 1)

            attention()
            experts(0)
            convolution()
            experts(1)

        @block.vector
        def _(dve):
            done = [0]
            V = nc.vector

            def link(ins):
                done[0] += 1
                ins.then_inc(dve_step, 1)
                dve.wait_ge(dve_step, done[0])

            def wide(ap, axis, shape):
                return ap.unsqueeze(axis).to_broadcast(shape)

            def norm(ph):
                for t in range(NT):
                    ms = st["ms"][:, t:t + 1]
                    dve.wait_ge(squares, NT * ph + t + 1)
                    link(V.tensor_scalar(ms, st["ss"][:, t:t + 1], 1.0 / D, EPS, ALU.mult, ALU.add))
                    V.reciprocal(ms, ms).then_inc(inv_ms, 1)
                    dve.wait_ge(rstd_ready, NT * ph + t + 1)
                    V.tensor_scalar(h[:, t].rearrange("q c k -> q k c"), x[:, t, :].rearrange("q (k c) -> q k c", c=KC),
                                    st["rstd"][:, t:t + 1], None, ALU.mult).then_inc(rows_ready[ph], 1)
                dve.wait_ge(gains_loaded, 16 * (1 if ph == 0 else 4))
                for t in range(NT):
                    dve.wait_ge(rows_turned[ph], 2 * t + 1)
                    V.tensor_tensor(hT[:, 0:4, t * P:(t + 1) * P],
                                    psum[:, 4 + 2 * t, :].rearrange("q (a b) -> q a b", a=4),
                                    wide(norm_gain[:, ph, 0:4], 2, [P, 4, P]), ALU.mult).then_inc(hT_ready[ph], 1)

            def attention():
                norm(0)
                tmp = att["tmp"]
                dve.wait_ge(consts_loaded, 16)
                dve.wait_ge(att_params_loaded, 16 * 2)

                def norm_heads(n):
                    r, t, at = turned_product(n), n % 2, IN_ORDER[n // 2] * 512
                    q = att["qk"][:, t, at:at + 512]
                    q3 = q.rearrange("q (a b) -> q a b", a=8)
                    dve.wait_ge(A["qkv_out"], n + 1)
                    link(V.tensor_tensor(att["sq"], q, q, ALU.mult))
                    link(V.tensor_reduce(st["qms"], att["sq"].rearrange("q (a b) -> q a b", a=8), AX, ALU.add))
                    link(V.tensor_scalar(st["qms"], st["qms"], 1.0 / DH, EPS, ALU.mult, ALU.add))
                    V.reciprocal(st["qms"], st["qms"]).then_inc(A["ms"], 1)
                    link(V.tensor_tensor(q3, q3, wide(att["gains"][:, at // D, :], 1, [P, 8, DH]), ALU.mult))
                    dve.wait_ge(A["rstd"], r + 1)
                    link(V.tensor_tensor(q3, q3, wide(st["qrstd"], 2, [P, 8, DH]), ALU.mult))
                    x1, x2 = q3[:, :, 0:ROT], q3[:, :, ROT:2 * ROT]
                    cos = wide(con[:, C_COS + ROT * t:C_COS + ROT * (t + 1)], 1, [P, 8, ROT])
                    sin = wide(con[:, C_SIN + ROT * t:C_SIN + ROT * (t + 1)], 1, [P, 8, ROT])
                    a = [tmp[:, k, :].rearrange("q (a b) -> q a b", a=8) for k in range(4)]
                    V.tensor_tensor(a[0], x1, cos, ALU.mult)
                    V.tensor_tensor(a[1], x2, sin, ALU.mult)
                    V.tensor_tensor(a[2], x2, cos, ALU.mult)
                    link(V.tensor_tensor(a[3], x1, sin, ALU.mult))
                    V.tensor_tensor(x1, a[0], a[1], ALU.subtract)
                    V.tensor_tensor(x2, a[2], a[3], ALU.add).then_inc(A["rotated"], 1)
                    dve.wait_ge(A["rotated"], r + 1)

                def biggest(u):
                    t, hd = unit(u)
                    dve.wait_ge(A["scores"], u + 1)
                    nm = st["nm"][:, 2 * (u % 3):2 * (u % 3) + 2]
                    bank = 2 + 2 * (u % 2)
                    V.tensor_reduce(nm, psum[:, bank:bank + 2, 0:(t + 1) * P], AX, ALU.max).then_inc(A["max"], 1)
                    dve.wait_ge(A["max"], u + 1)
                    V.tensor_scalar(nm, nm, -DH ** -0.5, None, ALU.mult).then_inc(A["neg_max"], 1)

                def mix(u):
                    t, hd = unit(u)
                    nk = (t + 1) * P
                    den = st["den"][:, 2 * (u % 3):2 * (u % 3) + 2]
                    one, other = att["probs"][:, u % 3, 0, 0:nk], att["probs"][:, u % 3, 1, 0:nk]
                    dve.wait_ge(A["exp"], 2 * u + 2)
                    link(V.reciprocal(den, den))
                    link(V.tensor_scalar(other, other, den[:, 1:2], st["neglam"], ALU.mult, ALU.mult))
                    V.scalar_tensor_tensor(out=one, in0=one, scalar=den[:, 0:1], in1=other, op0=ALU.mult,
                                           op1=ALU.add).then_inc(A["mixed"], 1)

                def norm_out(b):
                    dve.wait_ge(A["o_ready"], 8 * (b + 1))
                    sl = slice(4 * b, 4 * b + 4)
                    link(V.tensor_scalar(st["oms"][:, sl], st["oss"][:, sl], 1.0 / P, EPS, ALU.mult, ALU.add))
                    V.reciprocal(st["oms"][:, sl], st["oms"][:, sl]).then_inc(A["o_ms"], 1)
                    o3 = o_rows[:, b % 2, 512 * (b // 2):512 * (b // 2 + 1)].rearrange("q (a b) -> q a b", a=4)
                    link(V.scalar_tensor_tensor(out=o3, in0=o3, scalar=1.0 - LAMBDA_INIT,
                                                in1=wide(att["subln"], 1, [P, 4, P]), op0=ALU.mult, op1=ALU.mult))
                    dve.wait_ge(A["o_rstd"], b + 1)
                    V.tensor_tensor(o3, o3, wide(st["orstd"][:, sl], 2, [P, 4, P]), ALU.mult).then_inc(A["o_normed"], 1)

                def round_of(j):
                    if j < UNITS:
                        biggest(j)
                    if 1 <= j < UNITS + 1:
                        mix(j - 1)
                    if j in NORM_OUT:
                        norm_out(NORM_OUT[j])

                for n in range(12):
                    for j in ROUNDS.get(n, ()):
                        round_of(j)
                    if turned_product(n) is not None:
                        norm_heads(n)
                    if n == 4:
                        dve.wait_ge(lambda_params_loaded, 16 * 5)
                        for c in range(2):
                            link(V.tensor_tensor(tmp[:, c, :], att["lam"][:, 2 * c, :], att["lam"][:, 2 * c + 1, :],
                                                 ALU.mult))
                        V.tensor_reduce(st["lam_s"], tmp[:, 0:2, :], AX, ALU.add).then_inc(A["lam_sum"], 1)
                        dve.wait_ge(A["lam_exp"], 1)
                        link(V.tensor_tensor(st["neglam"], st["lam_e"][:, 1:2], st["lam_e"][:, 0:1], ALU.subtract))
                        link(V.tensor_scalar(st["neglam"], st["neglam"], -LAMBDA_INIT, None, ALU.add))
                for j in range(8, UNITS + LAG):
                    round_of(j)
                norm_out(3)
                dve.wait_ge(piece_used, ATT_BASE + 8)
                for t in range(NT):
                    for n in range(2):
                        cols = slice(n * 512, (n + 1) * 512)
                        V.tensor_tensor(x[:, t, cols], x[:, t, cols], psum[:, 2 * t + n, :], ALU.add).then_inc(
                            x_ready[1], 1)

            def convolution():
                link(V.memset(conv["u"][:, :, 0:TAPS - 1], 0.0))
                norm(2)
                dve.wait_ge(C["params_turned"], 1)
                V.tensor_copy(conv["cols"], psum[:, 4, 0:40])
                V.tensor_copy(conv["taps"].rearrange("q a b -> q (a b)"), psum[:, 4, 40:288]).then_inc(C["params"], 1)
                dve.wait_ge(C["params"], 1)
                for t in range(NT):
                    V.tensor_tensor(x[:, t, :], x[:, t, :], conv["b_out"], ALU.add)

                def glu(b):
                    dve.wait_ge(C["sig"], 2 * b + 2)
                    for jj in range(2):
                        j = 2 * b + jj
                        ins = V.scalar_tensor_tensor(
                            out=conv["u"][:, j, TAPS - 1:], in0=psum[:, 4 * (b // 2) + b % 2, jj * T:(jj + 1) * T],
                            scalar=conv["cols"][:, j:j + 1], in1=conv["sig"][:, b % 2, jj * T:(jj + 1) * T],
                            op0=ALU.add, op1=ALU.mult)
                    ins.then_inc(C["u_ready"], 1)
                    dve.wait_ge(C["u_ready"], b + 1)

                def taps(tiles, n):
                    for k in range(n):
                        for j, first in tiles:
                            src, tap = conv["u"][:, j, first + k:first + k + T], first + k
                            weight = conv["taps"][:, tap, j:j + 1]
                            if tap == 0:
                                ins = V.tensor_scalar(conv["cv"][:, j, :], src, weight, conv["cols"][:, 16 + j:17 + j],
                                                      ALU.mult, ALU.add)
                            else:
                                ins = V.scalar_tensor_tensor(out=conv["cv"][:, j, :], in0=src, scalar=weight,
                                                             in1=conv["cv"][:, j, :], op0=ALU.mult, op1=ALU.add)
                            done[0] += 1
                            ins.then_inc(dve_step, 1)
                            dve.wait_ge(dve_step, done[0] + 1 - len(tiles))
                    dve.wait_ge(dve_step, done[0])

                def tiles_done():
                    V.memset(st["mx"], 0.0).then_inc(C["dve_conv"], 1)

                glu(0)
                taps(((0, 0), (1, 0)), 14)
                glu(1)
                taps(((0, 14), (1, 14)), 17)
                tiles_done()
                taps(((3, 0),), 4)
                glu(2)
                taps(((3, 4), (4, 0)), 13)
                glu(3)
                taps(((3, 17), (4, 13)), 14)
                tiles_done()
                dve.wait_ge(C["pe_conv_out"], 1)
                taps(((4, 27), (6, PE_CONV[0][1])), 4)
                tiles_done()
                taps(((6, PE_CONV[0][1] + 4),), TAPS - 4 - PE_CONV[0][1])
                tiles_done()
                dve.wait_ge(C["sum"], 1)
                link(V.tensor_scalar(conv["mean"], psum[:, 4, 0:T], 1.0 / D, None, ALU.mult))
                dve.wait_ge(C["dve_conv"], 4)
                dve.wait_ge(C["pool_conv"], len(POOL_CONV))
                dve.wait_ge(C["pe_conv_out"], 2)
                for j in range(KC):
                    V.tensor_tensor(conv["cv"][:, j, :], conv["cv"][:, j, :], conv["mean"], ALU.subtract).then_inc(
                        C["centred"], 1)
                dve.wait_ge(C["var"], 1)
                dve.wait_ge(C["centred"], KC)
                link(V.tensor_scalar(conv["mean"], psum[:, 5, 0:T], 1.0 / D, EPS, ALU.mult, ALU.add))
                V.reciprocal(conv["mean"], conv["mean"]).then_inc(C["inv"], 1)
                dve.wait_ge(C["rstd"], 1)
                for j in range(KC):
                    V.tensor_tensor(conv["cv"][:, j, :], conv["cv"][:, j, :], conv["rstd"], ALU.mult).then_inc(
                        C["scaled"], 1)
                dve.wait_ge(piece_used, CONV_BASE + 6)
                for t in range(NT):
                    for n in range(2):
                        cols = slice(n * 512, (n + 1) * 512)
                        V.tensor_tensor(x[:, t, cols], x[:, t, cols], psum[:, 2 * t + n, :], ALU.add).then_inc(
                            x_ready[3], 1)

            def route(l, select):
                m = M[l]
                if l == 0:
                    dve.wait_ge(params_loaded, 16 * PARAM_DMAS)
                lg, ml, one, two, t32 = (moe[n] for n in ("logit", "ml", "one", "two", "t32"))
                dve.wait_ge(m["logits"], 3)
                link(V.tensor_tensor(lg, psum[:, 5, 0:128].rearrange("q (a b) -> q a b", a=2)[:, :, 0:CHOICES],
                                     wide(router_b[:, l, :], 1, [P, NT, CHOICES]), ALU.add))
                gl, pick = lg[:, :, 0:GROUPS], st["pick"]
                link(V.tensor_reduce(st["mx"], gl, AX, ALU.max))
                rev4 = wide(rev[:, EXPERTS - GROUPS:EXPERTS], 1, [P, NT, GROUPS])
                for t in range(NT):
                    ins = V.scalar_tensor_tensor(out=pick[:, t, :], in0=gl[:, t, :],
                                                 scalar=st["mx"][:, t:t + 1], in1=rev4[:, t, :], op0=ALU.is_equal,
                                                 op1=ALU.mult)
                V.tensor_tensor(st["ge"], gl, wide(st["mx"], 2, [P, NT, GROUPS]), ALU.subtract).then_inc(
                    m["group_in"], 1)
                dve.wait_ge(m["group_in"], 1)
                link(V.tensor_reduce(st["first"], pick, AX, ALU.max))
                link(V.tensor_tensor(pick, rev4, wide(st["first"], 2, [P, NT, GROUPS]), ALU.is_equal))
                link(V.tensor_scalar(pick, pick, BIG, -BIG, ALU.mult, ALU.add))
                link(V.tensor_tensor(ml.rearrange("q t (g e) -> q t g e", g=GROUPS),
                                     lg[:, :, GROUPS:].rearrange("q t (g e) -> q t g e", g=GROUPS),
                                     wide(pick, 3, [P, NT, GROUPS, PER_GROUP]), ALU.add))

                rev32 = wide(rev, 1, [P, NT, EXPERTS])
                def first_of_max(mx, chosen):
                    link(V.tensor_reduce(mx, ml, AX, ALU.max))
                    for t in range(NT):
                        ins = V.scalar_tensor_tensor(out=chosen[:, t, :], in0=ml[:, t, :], scalar=mx[:, t:t + 1],
                                                     in1=rev, op0=ALU.is_equal, op1=ALU.mult)
                    link(ins)
                    link(V.tensor_reduce(st["first"], chosen, AX, ALU.max))
                    link(V.tensor_tensor(chosen, rev32, wide(st["first"], 2, [P, NT, EXPERTS]), ALU.is_equal))

                first_of_max(st["m1"], one)
                link(V.scalar_tensor_tensor(out=ml, in0=one, scalar=-3 * BIG, in1=ml, op0=ALU.mult, op1=ALU.add))
                first_of_max(st["m2"], two)
                V.tensor_tensor(t32, one, two, ALU.add).then_inc(m["picked"], 1)
                V.tensor_tensor(st["dm"], st["m2"], st["m1"], ALU.subtract).then_inc(m["top_in"], 1)
                dve.wait_ge(m["group_exp"], 1)
                link(V.tensor_reduce(st["gp"], st["ge"], AX, ALU.add))
                link(V.reciprocal(st["gp"], st["gp"]))
                comb = moe["comb"][:, :, FRONT:FRONT + EXPERTS]
                posm = moe["posm"][:, :, FRONT:FRONT + EXPERTS]
                dve.wait_ge(m["pos"], 1)
                dve.wait_ge(m["picked"], 1)
                link(V.scalar_tensor_tensor(out=ml, in0=psum[:, 6, 0:64].rearrange("q (a b) -> q a b", a=2), scalar=1.0,
                                            in1=t32, op0=ALU.add, op1=ALU.mult))
                link(V.tensor_scalar(posm, ml, -1.0, None, ALU.add))
                for q in range(2):
                    select(q, q)
                dve.wait_ge(m["top_exp"], 1)
                link(V.tensor_scalar(st["m1"], st["e2"], 1.0, None, ALU.add))
                link(V.reciprocal(st["m1"], st["m1"]))
                link(V.tensor_tensor(st["m1"], st["m1"], st["gp"], ALU.mult))
                link(V.tensor_tensor(st["m2"], st["m1"], st["e2"], ALU.mult))
                V.tensor_tensor(one, one, wide(st["m1"], 2, [P, NT, EXPERTS]), ALU.mult)
                link(V.tensor_tensor(two, two, wide(st["m2"], 2, [P, NT, EXPERTS]), ALU.mult))
                link(V.tensor_tensor(comb, one, two, ALU.add))
                dve.wait_ge(m["pos"], 2)
                link(V.tensor_reduce(st["mx"][:, 0:1], psum[:, 4, 0:32], AX, ALU.max))
                V.tensor_copy(flag_i[:, l:l + 1], st["mx"][:, 0:1]).then_inc(m["flag"], 1)
                link(V.tensor_scalar(two, posm, float(SLOTS), None, ALU.is_ge))
                link(V.tensor_tensor(moe["late"], two, comb, ALU.mult))

            def experts(l):
                m = M[l]
                def select(q, buf):
                    V.tensor_tensor(moe["sel"][:, :, buf, :].rearrange("q t (a b) -> q t a b", a=TRIO),
                                    iota.unsqueeze(1).unsqueeze(1).to_broadcast([P, NT, TRIO, SLOTS]),
                                    wide(moe["posm"][:, :, bass.ds(TRIO * q, TRIO)], 3, [P, NT, TRIO, SLOTS]),
                                    ALU.is_equal).then_inc(m["sel"], 1)

                norm(2 * l + 1)
                V.memset(zero, 0.0).then_inc(m["zero"], 1)
                V.memset(moe["posm"], -1.0)
                link(V.memset(moe["comb"], 0.0))
                route(l, select)

                def select_weighted(pair, at):
                    V.tensor_tensor(moe["selw"], iota.unsqueeze(1).unsqueeze(1).to_broadcast([P, NT, 2, SLOTS]),
                                    wide(moe["posm"][:, :, bass.ds(at, 2)], 3, [P, NT, 2, SLOTS]),
                                    ALU.is_equal).then_inc(m["pair"], 1)
                    dve.wait_ge(m["pair"], pair + 1)
                    V.tensor_tensor(moe["selw"], moe["selw"],
                                    wide(moe["comb"][:, :, bass.ds(at, 2)], 3, [P, NT, 2, SLOTS]),
                                    ALU.mult).then_inc(m["selw"], 1)

                def rows_in(q, buf, c):
                    dve.wait_ge(m["gathered"], 8 * q + (c - 15))
                    V.tensor_scalar(moe["xg"][:, c, buf, :], psum[:, 7, 0:TRIO * SLOTS],
                                    norm_gain[:, 2 * l + 1, c:c + 1], None, ALU.mult).then_inc(m["xg"], 1)

                def hidden(e):
                    dve.wait_ge(m["silu"], e + 1)
                    V.tensor_tensor(moe["hid"], moe["silu"], psum[:, 4, 256:512], ALU.mult).then_inc(m["hid"], 1)

                def combine_in(pair):
                    dve.wait_ge(m["comb_turned"], pair + 1)
                    V.tensor_copy(moe["combT"], psum[:, 6, 256:512]).then_inc(m["combT"], 1)

                def first_rows_in(k):
                    dve.wait_ge(m["first_gathered"], k + 1)
                    dst, bank = first_rows(k)
                    V.tensor_scalar(dst, bank, norm_gain[:, 2 * l + 1, k % KC:k % KC + 1], None, ALU.mult).then_inc(
                        m["first_dve" if k < 15 else "xg"], 1)

                for k in (0, 2, 4, 6, 8, 10):
                    first_rows_in(k)
                hidden(0)
                for k in (12, 14, 15):
                    first_rows_in(k)
                select(2, 0)
                with dve.Fori(0, 5) as i:
                    for k in range(6):
                        j = k % TRIO
                        q = 2 * i + (1 + k // TRIO)
                        buf = (1 + k // TRIO) % 2
                        rows_in(q + 1, 1 - buf, 3 * j)
                        hidden(6 * i + (k + 1))
                        rows_in(q + 1, 1 - buf, 3 * j + 1)
                        if k % 2 == 0:
                            select_weighted(3 * i + k // 2, 6 * i + (k + FRONT))
                        else:
                            combine_in(3 * i + k // 2)
                        if 3 * j + 2 < KC:
                            rows_in(q + 1, 1 - buf, 3 * j + 2)
                        if j == TRIO - 1:
                            select(q + 2, buf)
                hidden(EXPERTS - 1)
                select_weighted(EXPERTS // 2 - 1, EXPERTS - 2 + FRONT)
                combine_in(EXPERTS // 2 - 1)
                late = dve.value_load(flag_i[0:1, l:l + 1], min_val=0, max_val=T)
                dve.wait_ge(m["combined"], EXPERTS // 2)
                for t in range(NT):
                    for hf in range(2):
                        cols = slice(hf * 512, (hf + 1) * 512)
                        ins = V.tensor_tensor(x[:, t, cols], x[:, t, cols], psum[:, 2 * hf + t, :], ALU.add)
                link(ins)

                with dve.If(late > SLOTS):
                    V.memset(st["m1"], 0.0).then_inc(m["ov_freed"], 1)
                    V.memset(st["m2"], 0.0).then_inc(m["ov_added"], 1)
                    with dve.Fori(0, EXPERTS) as e:
                        for f in range(FC):
                            dve.wait_ge(m["ov_silu"], FC * e + f + 1)
                            V.tensor_tensor(ovf["hid"], ovf["silu"], psum[:, 5, 0:T], ALU.mult).then_inc(m["ov_hid"], 1)
                        dve.wait_ge(m["ov_freed"], FC * e + (FC + 1))
                        dve.wait_ge(m["ov_added"], 4 * e + 1)
                        for t in range(NT):
                            for n in range(2):
                                cols = slice(n * 512, (n + 1) * 512)
                                V.scalar_tensor_tensor(out=x[:, t, cols], in0=psum[:, 2 * t + n, :],
                                                       scalar=moe["late"][:, t, bass.ds(e, 1)], in1=x[:, t, cols],
                                                       op0=ALU.mult, op1=ALU.add).then_inc(m["ov_added"], 1)
                V.memset(st["gp"], 0.0).then_inc(x_ready[2 * l + 2], 4)

            attention()
            experts(0)
            convolution()
            experts(1)

        @block.gpsimd
        def _(pool):
            def overflow(l):
                m = M[l]
                pool.wait_ge(m["flag"], 1)
                late = pool.value_load(flag_i[0:1, l:l + 1], min_val=0, max_val=T)
                with pool.If(late > SLOTS):
                    with pool.Fori(0, EXPERTS) as e:
                        for f in range(FC):
                            pool.wait_ge(m["ov_freed"], FC * e + (f + 1))
                            cols = slice(f * P, (f + 1) * P)
                            for w, dst in (("moe_w_gate", "wg"), ("moe_w_up", "wu")):
                                pool.dma_start(ovf[dst], p[w][l, bass.ds(e, 1), :, cols].rearrange(
                                    "o (q c) f -> q (o c) f", c=KC)).then_inc(m["ov_loaded"], 16)
                            pool.dma_start(ovf["wd"], p["moe_w_down"][l, bass.ds(e, 1), cols, :].rearrange(
                                "o q f -> q (o f)")).then_inc(m["ov_loaded"], 16)

            def convolution():
                for i, j in enumerate(POOL_CONV):
                    for n in range(1, PRODUCTS):
                        pool.wait_ge(C["products"], PRODUCTS * i + n + 1)
                        if n >= 2:
                            pool.wait_ge(C["pool_step"], (PRODUCTS - 1) * i + n - 1)
                        both = slice(0, 2 if n < PRODUCTS - 1 else 1)
                        nc.gpsimd.tensor_tensor(conv["acc"][:, both, :], conv["acc"][:, both, :],
                                                conv["prod"][:, n % 3, both, :], ALU.add).then_inc(C["pool_step"], 1)
                    pool.wait_ge(C["pool_step"], (PRODUCTS - 1) * (i + 1))
                    nc.gpsimd.tensor_tensor(conv["cv"][:, j, :], conv["acc"][:, 0, :], conv["acc"][:, 1, :],
                                            ALU.add).then_inc(C["pool_conv"], 1)

            pool.wait_ge(x_ready[1], 4)
            for name, row, n in (("conv_b_in", 0, 16), ("conv_dw_b", 16, 8), ("conv_ln_g", 24, 8),
                                 ("conv_ln_b", 32, 8)):
                pool.dma_start(conv["rows"][row:row + n, 0, :], p[name].rearrange(
                    "o (j k) -> (o j) k", k=P)).then_inc(conv_params_loaded, 16)
            taps = p["conv_dw_w"][0].rearrange("w (j k) -> (w j) k", k=P)
            pool.dma_start(conv["rows"][0:124, 1:3, :], taps.rearrange("(b r) k -> r b k", b=2)).then_inc(
                conv_params_loaded, 16)
            pool.dma_start(conv["b_out"], p["conv_b_out"][0].partition_broadcast(P)).then_inc(
                conv_params_loaded, 16)
            overflow(0)
            convolution()
            overflow(1)


_PARAMS = ["attn_norm", "diff_w_in", "diff_q_gain", "diff_k_gain", "diff_lambda_q1", "diff_lambda_k1", "diff_lambda_q2",
           "diff_lambda_k2", "diff_subln", "diff_w_out", "conv_norm", "conv_w_in", "conv_b_in", "conv_dw_w",
           "conv_dw_b", "conv_ln_g", "conv_ln_b", "conv_w_out", "conv_b_out", "ffn_norm", "router_group_w",
           "router_group_b", "router_expert_w", "router_expert_b", "moe_w_gate", "moe_w_up", "moe_w_down"]


def constants():
    import numpy as np

    con = np.zeros((P, C_END), np.float32)
    r = np.arange(P)
    con[:, C_IDENT:C_IDENT + P] = np.eye(P)
    con[:, C_BEFORE:C_BEFORE + P] = r[:, None] < r[None, :]
    con[:, C_ONES:C_ONES + P] = 1
    con[:, C_IOTA:C_IOTA + SLOTS] = np.arange(SLOTS)
    con[:, C_REV:C_REV + EXPERTS] = EXPERTS - np.arange(EXPERTS)
    con[[0, 64], C_EARLY:C_EARLY + 64] = 1
    con[[0, 64], C_HIDE:C_HIDE + 64] = -BIG
    inv_freq = np.float32(500000.0) ** (-np.arange(0, 2 * ROT, 2, dtype=np.float32) / np.float32(2 * ROT))
    ang = np.arange(T, dtype=np.float32)[:, None] * inv_freq[None, :]
    for t in range(NT):
        con[:, C_COS + ROT * t:C_COS + ROT * (t + 1)] = np.cos(ang[t * P:(t + 1) * P])
        con[:, C_SIN + ROT * t:C_SIN + ROT * (t + 1)] = np.sin(ang[t * P:(t + 1) * P])
    return con


def kernel(**inputs):
    import numpy as _np
    import concourse.bacc as _bacc
    from concourse import mybir as _mybir
    from concourse.bass_utils import run_bass_kernel_spmd as _run

    nc = _bacc.Bacc("TRN2", target_bir_lowering=False, num_devices=1)
    arrays = {"in_x": _np.ascontiguousarray(inputs["x"]), "in_constants": constants()}
    for name in _PARAMS:
        arrays["in_" + name] = _np.ascontiguousarray(inputs[name])
    aps = {k: nc.dram_tensor(k, a.shape, _mybir.dt.float32, kind="ExternalInput").ap() for k, a in arrays.items()}
    out = nc.dram_tensor("out", (1, T, D), _mybir.dt.float32, kind="ExternalOutput").ap()
    build(nc, aps["in_x"], aps["in_constants"], {n: aps["in_" + n] for n in _PARAMS}, out)
    r = _run(nc, [arrays], core_ids=[0])
    return r.results[0]["out"]
```

```python
from contextlib import ExitStack

import concourse.bass as bass
from concourse import mybir

P = 128
T = 256
NT = T // P
D = 1024
KC = D // P
BANK = 512
HEADS = 8
DH = 64
ROT = DH // 8
TAPS = 31
GROUPS = 4
PER_GROUP = 8
EXPERTS = GROUPS * PER_GROUP
CHOICES = GROUPS + EXPERTS
F = 512
FC = F // P
SLOTS = 64
FRONT = 2
PADDED = EXPERTS + 8
EPS = 1e-6
LAMBDA_INIT = 0.2
BIG = 1e30
TRIO = 3
POOL_CONV = (2, 5)
PE_CONV = ((6, 10), (7, TAPS))
MEAN_ORDER = (0, 1, 2, 3, 4, 7, 6, 5)
PE_TAPS = tuple((j, tap) for j, n in PE_CONV for tap in range(n))

PRODUCTS = (TAPS + 1) // 2

SCRATCH = 8320
RING = 9
ATT_BASE = 0
MOE_PIECES = 3 * EXPERTS
CONV_BASE = 8 + MOE_PIECES
MOE_BASE = (8, CONV_BASE + 6)

C_IDENT, C_EPS = 0, P
C_BEFORE = C_EPS + 1
C_ONES = C_BEFORE + P
C_IOTA = C_ONES + P
C_REV = C_IOTA + SLOTS
C_EARLY = C_REV + EXPERTS
C_HIDE = C_EARLY + P
C_COS = C_HIDE + 64
C_SIN = C_COS + NT * ROT
C_END = C_SIN + NT * ROT

IN_ORDER = (0, 2, 4, 1, 3, 5)
ROUNDS = {(6, 1): 0, (7, 0): 1, (7, 1): 2, (8, 1): 3, (9, 0): 4, (9, 1): 5, (10, 0): 6, (10, 1): 7,
          (11, 0): 8, (11, 1): 9}
UNITS = 16
LAG = 3
NORM_OUT = {8: 0, 10: 1, 15: 2}

OUT_PRODUCTS = {11: ((0, 0, (0,)),), 12: ((0, 0, (1,)),), 13: ((0, 0, (2,)),), 16: ((0, 0, (3,)),),
                17: ((0, 1, (0, 1)),), 18: ((0, 1, (2, 3)),)}

PARAM_DMAS = 2 * 7
PHASES = ("att", "moe0", "conv", "moe1")


def build(nc, x_in, consts_in, p, out):
    fp32 = mybir.dt.float32
    i32 = mybir.dt.int32
    ALU = mybir.AluOpType
    ACT = mybir.ActivationFunctionType
    AX = mybir.AxisListType.X

    ctx = ExitStack()
    with ctx:
        def sb(name, shape, dt=fp32):
            return ctx.enter_context(nc.sbuf_tensor(name, shape, dt))

        def sem(name):
            return ctx.enter_context(nc.semaphore(name))

        ring = [sb(f"ring{i}", [P, 4096]) for i in range(RING)]
        x = sb("x", [P, NT, D])
        h = sb("h", [P, NT, KC, P])
        hT = sb("hT", [P, KC, T])
        con = sb("con", [P, C_END])
        norm_gain = sb("norm_gain", [P, 4, KC])
        router_w = sb("router_w", [P, 2, KC, GROUPS + EXPERTS])
        router_b = sb("router_b", [P, 2, GROUPS + EXPERTS])
        stat = sb("stat", [P, 144])
        flag_i = sb("flag_i", [P, 2], i32)
        scratch = sb("scratch", [P, SCRATCH])
        psum = ctx.enter_context(nc.psum_tensor("psum", [P, 8, BANK], fp32))

        ident = con[:, C_IDENT:C_IDENT + P]
        before = con[:, C_BEFORE:C_BEFORE + P]
        eps = con[:, C_EPS:C_EPS + 1]
        ones = con[:, C_ONES:C_ONES + P]
        iota = con[:, C_IOTA:C_IOTA + SLOTS]
        rev = con[:, C_REV:C_REV + EXPERTS]
        early = con[:, C_EARLY:C_EARLY + P]
        hide = con[:, C_HIDE:C_HIDE + 64]

        def carve(spec):
            at, views = 0, {}
            for name, *shape in spec:
                n = 1
                for s in shape:
                    n *= s
                v = scratch[:, at:at + n]
                at += n
                if len(shape) == 2:
                    v = v.rearrange("q (a b) -> q a b", a=shape[0])
                elif len(shape) == 3:
                    v = v.rearrange("q (a b c) -> q a b c", a=shape[0], b=shape[1])
                elif len(shape) == 4:
                    v = v.rearrange("q (a b c d) -> q a b c d", a=shape[0], b=shape[1], c=shape[2])
                views[name] = v
            assert at <= SCRATCH, at
            return views

        att = carve([("qk", NT, 2 * D), ("v", NT, D), ("probs", 3, 2, T),
                     ("pT", 2, P), ("junk", P), ("gains", 2, DH), ("subln", P)])
        o_rows = h[:].rearrange("q t c k -> q t (c k)")
        att["sq"] = o_rows[:, 0, 512:1024]
        att["tmp"] = o_rows[:, 1, 512:768].rearrange("q (a b) -> q a b", a=4)
        att["lam"] = att["probs"][:, 2].rearrange("q a b -> q (a b)")[:, 0:4 * DH].rearrange("q (a b) -> q a b", a=4)
        conv = carve([("u", KC, T + TAPS - 1), ("cv", KC, T), ("sig", 2, 2 * T), ("diag", 4, P),
                      ("cols", 40), ("taps", TAPS, KC), ("mean", T), ("rstd", T),
                      ("beyond_experts", 24), ("rows", 3, P), ("b_out", D)])
        conv["std"] = conv["mean"]
        conv["sq"] = h[:].rearrange("q t c k -> q (t c k)").rearrange("q (a b) -> q a b", a=KC)
        work = h[:].rearrange("q t c k -> q (t c k)")
        conv["acc"] = work[:, 0:2 * T].rearrange("q (a b) -> q a b", a=2)
        conv["prod"] = work[:, 2 * T:8 * T].rearrange("q (a b c) -> q a b c", a=3, b=2)
        moe = carve([("xg", KC, 2, TRIO * SLOTS), ("sel", NT, 2, TRIO * SLOTS), ("selw", NT, 2, SLOTS),
                     ("silu", T), ("hid", T), ("hidT", 2, P), ("combT", T), ("outs", D),
                     ("logit", NT, CHOICES), ("ml", NT, EXPERTS), ("one", NT, EXPERTS), ("two", NT, EXPERTS),
                     ("t32", NT, EXPERTS), ("posm", NT, PADDED), ("comb", NT, PADDED),
                     ("late", NT, EXPERTS)])
        zero = moe["outs"][:, 0:BANK]
        logits_T = moe["combT"][0:CHOICES, :]
        ovf = carve([("wg", KC, P), ("wu", KC, P), ("wd", D), ("silu", T), ("hid", T)])

        st, at = {}, 0
        for name, n, cols in (("ss", 2, 0), ("rms", 2, 0), ("rstd", 2, 0), ("qms", 8, 0), ("qrstd", 8, 0),
                              ("nm", 6, 0), ("den", 6, 0), ("oss", 16, 0), ("oms", 16, 0), ("orstd", 16, 0),
                              ("lam_s", 2, 0), ("lam_e", 2, 0), ("neglam", 1, 0), ("mx", 2, 0), ("first", 2, 0),
                              ("ge", 8, GROUPS),
                              ("pick", 8, GROUPS), ("gp", 2, 0), ("m1", 2, 0), ("m2", 2, 0), ("dm", 2, 0),
                              ("e2", 2, 0), ("spare", 11, 0)):
            st[name] = stat[:, at:at + n] if not cols else stat[:, at:at + n].rearrange("q (a b) -> q a b", b=cols)
            at += n

        arrived = [sem(f"arrived{i}") for i in range(RING)]
        piece_used = sem("piece_used")
        x_loaded = [sem(f"x_loaded{t}") for t in range(NT)]
        identity_loaded = sem("identity_loaded")
        consts_loaded = sem("consts_loaded")
        att_params_loaded = sem("att_params_loaded")
        lambda_params_loaded = sem("lambda_params_loaded")
        params_loaded = sem("params_loaded")
        conv_params_loaded = sem("conv_params_loaded")
        out_stored = sem("out_stored")
        dve_step = sem("dve_step")
        x_ready = [None] + [sem(f"x_ready_{n}") for n in PHASES[1:]] + [sem("x_final")]
        squares = sem("squares")
        rms_ready = sem("rms_ready")
        rows_ready = [sem(f"rows_{n}") for n in PHASES]
        rows_turned = [sem(f"rows_turned_{n}") for n in PHASES]
        hT_ready = [sem(f"hT_ready_{n}") for n in PHASES]
        hT_other = [sem(f"hT_other_{n}") for n in PHASES]
        first_gain_loaded = sem("first_gain_loaded")
        gains_loaded = sem("gains_loaded")
        A = {n: sem("att_" + n) for n in (
            "qkv", "qkv_out", "ms", "rstd", "rotated", "turned", "turned_out", "scores", "max", "neg_max",
            "exp", "mixed", "probs_turned", "pT_ready", "pv", "o_ready", "o_ms", "o_rstd", "o_normed", "o_turned",
            "oT_ready", "first_tile", "lam_sum", "lam_exp")}
        C = {n: sem("conv_" + n) for n in (
            "params_turned", "params", "glu", "sig", "u_ready", "diag", "diag_used",
            "pe_conv_out", "dve_conv", "products", "pool_step", "pool_conv", "sum", "centred",
            "squared", "var", "std", "scaled", "act", "first_tile")}
        M = [{n: sem(f"moe{l}_" + n) for n in (
            "logits", "logits_out", "group_in", "group_exp", "top_in", "top_exp", "picked", "pos", "sel", "pair",
            "selw", "flag",
            "first_gathered", "first_dve", "first_act",
            "gathered", "xg", "silu", "hid", "hid_turned", "hidT", "comb_turned", "combT", "outs",
            "combined", "zero", "ov_loaded", "ov_freed", "ov_gu", "ov_silu", "ov_hid",
            "ov_added")} for l in range(2)]

        block = ctx.enter_context(nc.Block())

        def unit(u):
            return u % 8 // 4, 4 * (u // 8) + u % 4

        def turned_product(n):
            return None if n // 2 % 3 == 2 else n - 2 * (n // 6)

        def turned_beside(n):
            ready = {10: (8, 9), 11: ()}.get(n, (n - 2,))
            return [k for k in ready if k >= 0 and turned_product(k) is not None]

        def first_rows(k):
            n, c = k // KC, k % KC
            at = (1 - n) * 2 * SLOTS
            return moe["xg"][:, c, n, at:TRIO * SLOTS], psum[:, 5 + k % 3, 0:TRIO * SLOTS - at]

        def gate_at(l, e):
            return MOE_BASE[l] if isinstance(e, int) and e == 0 else 3 * e + (MOE_BASE[l] - 1)

        def up_at(l, e):
            return gate_at(l, e) + 1

        def down_at(l, e):
            return 3 * e + (MOE_BASE[l] + 4) if not (isinstance(e, int) and e == EXPERTS - 1) else MOE_BASE[l] + 95

        @block.sync
        def _(sp):
            def load(place, src, slot=None, lap=None):
                slot = place % RING if slot is None else slot
                if not isinstance(place, int) or place >= RING:
                    sp.wait_ge(piece_used, place - RING + 1)
                sp.dma_start(ring[slot][:], src).then_inc(arrived[slot], 16)

            def columns(w, n):
                return w[:, n * 512:(n + 1) * 512].rearrange("(p c) f -> p c f", c=KC)

            def rows(w, half):
                return w[half * 512:(half + 1) * 512, :].rearrange("(c p) f -> p c f", p=P)

            def up_src(w, l, e):
                return w[l, bass.ds(e, 1)].rearrange("o (p c) f -> p (o c f)", c=KC)

            def down_src(l, e):
                return p["moe_w_down"][l, bass.ds(e, 1)].rearrange("o (c p) f -> p (o c) f", p=P)

            def load_moe(l):
                base = MOE_BASE[l]
                load(base, up_src(p["moe_w_gate"], l, 0))
                load(base + 1, up_src(p["moe_w_up"], l, 0))
                with sp.Fori(0, 5) as i:
                    for k in range(6):
                        at = base + 2 + 3 * k
                        load(18 * i + at, up_src(p["moe_w_gate"], l, 6 * i + k + 1), at % RING)
                        load(18 * i + at + 1, up_src(p["moe_w_up"], l, 6 * i + k + 1), (at + 1) % RING)
                        load(18 * i + at + 2, down_src(l, 6 * i + k), (at + 2) % RING)
                at = base + 92
                load(at, up_src(p["moe_w_gate"], l, EXPERTS - 1))
                load(at + 1, up_src(p["moe_w_up"], l, EXPERTS - 1))
                load(at + 2, down_src(l, EXPERTS - 2))
                load(at + 3, down_src(l, EXPERTS - 1))

            sp.dma_start(con[:, 0:C_BEFORE], consts_in[:, 0:C_BEFORE]).then_inc(identity_loaded, 16)
            for t in range(NT):
                sp.dma_start(x[:, t, :], x_in[0, t * P:(t + 1) * P, :]).then_inc(x_loaded[t], 16)
            sp.dma_start(norm_gain[:, 0, :], p["attn_norm"].rearrange("o (q c) -> q (o c)", c=KC)).then_inc(
                first_gain_loaded, 16)
            w = p["diff_w_in"][0]
            load(ATT_BASE, columns(w, IN_ORDER[0]))
            sp.dma_start(con[:, C_BEFORE:], consts_in[:, C_BEFORE:]).then_inc(consts_loaded, 16)
            for n, name in enumerate(("diff_q_gain", "diff_k_gain")):
                sp.dma_start(att["gains"][:, n, :], p[name][0].partition_broadcast(P)).then_inc(att_params_loaded, 16)
            for n in range(1, 6):
                load(ATT_BASE + n, columns(w, IN_ORDER[n]))
            sp.dma_start(att["subln"], p["diff_subln"][0].partition_broadcast(P)).then_inc(lambda_params_loaded, 16)
            for n, name in enumerate(("q1", "k1", "q2", "k2")):
                sp.dma_start(att["lam"][:, n, :], p["diff_lambda_" + name][0].partition_broadcast(P)).then_inc(
                    lambda_params_loaded, 16)
            for half in range(2):
                load(ATT_BASE + 6 + half, rows(p["diff_w_out"][0], half))
            sp.dma_start(norm_gain[:, 2, :], p["conv_norm"].rearrange("o (q c) -> q (o c)", c=KC)).then_inc(
                gains_loaded, 16)
            for l in range(2):
                sp.dma_start(norm_gain[:, 2 * l + 1, :], p["ffn_norm"][l].rearrange("(q c) -> q c", c=KC)).then_inc(
                    gains_loaded, 16)
                sp.dma_start(router_w[:, l, :, 0:GROUPS], p["router_group_w"][l].rearrange(
                    "(q c) g -> q c g", c=KC)).then_inc(params_loaded, 16)
                for g in range(GROUPS):
                    at = GROUPS + g * PER_GROUP
                    sp.dma_start(router_w[:, l, :, at:at + PER_GROUP], p["router_expert_w"][l, g].rearrange(
                        "(q c) e -> q c e", c=KC)).then_inc(params_loaded, 16)
                sp.dma_start(router_b[:, l, 0:GROUPS], p["router_group_b"][l].partition_broadcast(P)).then_inc(
                    params_loaded, 16)
                sp.dma_start(router_b[:, l, GROUPS:], p["router_expert_b"][l].rearrange(
                    "g e -> (g e)").partition_broadcast(P)).then_inc(params_loaded, 16)
            load_moe(0)
            for n, c in enumerate((0, 2, 1, 3)):
                load(CONV_BASE + n, columns(p["conv_w_in"][0], c))
            for half in range(2):
                load(CONV_BASE + 4 + half, rows(p["conv_w_out"][0], half))
            load_moe(1)
            sp.wait_ge(x_ready[4], 4)
            for t in range(NT):
                sp.dma_start(out[0, t * P:(t + 1) * P, :], x[:, t, :]).then_inc(out_stored, 16)
            sp.wait_ge(out_stored, 16 * NT)

        def has_arrived(eng, place, slot=None, lap=0):
            eng.wait_ge(arrived[place % RING], 16 * (place // RING + lap + 1))

        @block.tensor
        def _(pe):
            def turn_rows(ph, between=None):
                for r in range(4):
                    t, half = r // 2, r % 2
                    if r == 2 and between:
                        between()
                    if half == 0:
                        pe.wait_ge(rows_ready[ph], t + 1)
                    for j in range(4):
                        mm = pe.transpose(psum[:, 4 + r, j * P:(j + 1) * P], h[:, t, 4 * half + j, :], ident)
                    mm.then_inc(rows_turned[ph], 1)

            def keep_awake(n):
                for _ in range(n):
                    pe.matmul(psum[:, 7, 0:T], ones, con[:, 0:T], start=True, stop=True)

            def all_turned(ph, t):
                pe.wait_ge(hT_ready[ph], t + 1)
                if t == NT - 1:
                    pe.wait_ge(hT_other[ph], 1)

            def attention():
                turn_rows(0)

                bank6 = [hT_ready[0], 2]

                def turn(blocks, signal, reader, count):
                    pe.wait_ge(*bank6)
                    for j, block in enumerate(blocks):
                        mm = pe.transpose(psum[:, 6, j * P:(j + 1) * P], block, ident)
                    mm.then_inc(signal, 1)
                    bank6[:] = [reader, count]

                def turn_heads(n):
                    r, t, at = turned_product(n), n % 2, IN_ORDER[n // 2] * 512
                    pe.wait_ge(A["rotated"], r + 1)
                    turn([att["qk"][:, t, at + j * P:at + (j + 1) * P] for j in range(4)], A["turned"],
                         A["turned_out"], r + 1)

                def scores(u):
                    t, hd = unit(u)
                    pe.wait_ge(A["turned_out"], 4 + 4 * (u // 8))
                    if u >= 2:
                        pe.wait_ge(A["exp"], 2 * u - 2)
                    else:
                        pe.wait_ge(consts_loaded, 16)
                    nk = (t + 1) * P
                    for c in range(2):
                        half, bank = slice(c * DH, (c + 1) * DH), 2 + 2 * (u % 2) + c
                        pe.matmul(psum[:, bank, 0:nk], att["qk"][half, t, hd * P:(hd + 1) * P],
                                  att["qk"][half, 0:t + 1, D + hd * P:D + (hd + 1) * P], start=True, stop=False)
                        mm = pe.matmul(psum[:, bank, nk - 64:nk], early[half, :], hide[half, :], start=False, stop=True)
                    mm.then_inc(A["scores"], 1)

                def turn_probs(u):
                    t, hd = unit(u)
                    pe.wait_ge(A["mixed"], u + 1)
                    turn([att["probs"][:, u % 3, 0, k * P:(k + 1) * P] for k in range(t + 1)], A["probs_turned"],
                         A["pT_ready"], u + 1)

                def values(u):
                    t, hd = unit(u)
                    pe.wait_ge(A["pT_ready"], u + 1)
                    pe.wait_ge(A["qkv_out"], 6 + 6 * (u // 8))
                    if u >= 1:
                        pe.wait_ge(A["o_ready"], 2 * u)
                    for k in range(t + 1):
                        mm = pe.matmul(psum[:, 7, 0:P], att["pT"][:, k, :], att["v"][:, k, hd * P:(hd + 1) * P],
                                       start=(k == 0), stop=(k == t))
                    mm.then_inc(A["pv"], 1)

                def turn_out(b):
                    pe.wait_ge(A["o_normed"], b + 1)
                    turn([o_rows[:, b % 2, (4 * (b // 2) + j) * P:(4 * (b // 2) + j + 1) * P] for j in range(4)],
                         A["o_turned"], A["oT_ready"], b + 1)

                def round_of(j):
                    if j < UNITS:
                        scores(j)
                    for args in OUT_PRODUCTS.get(j, ()):
                        out_product(*args)
                    if LAG <= j < UNITS + LAG:
                        values(j - LAG)
                    if 2 <= j < UNITS + 2:
                        turn_probs(j - 2)
                    if j - 2 in NORM_OUT:
                        turn_out(NORM_OUT[j - 2])

                for n in range(12):
                    if n < 2:
                        all_turned(0, n)
                    if n % 2 == 0:
                        has_arrived(pe, ATT_BASE + n // 2)
                    if n >= 2:
                        pe.wait_ge(A["qkv_out"], n - 1)
                    w = ring[(ATT_BASE + n // 2) % RING][:].rearrange("q (c f) -> q c f", c=KC)
                    for c in range(KC):
                        if c == KC // 2 and (n, 0) in ROUNDS:
                            round_of(ROUNDS[n, 0])
                        mm = pe.matmul(psum[:, n % 2, :], hT[:, c, (n % 2) * P:(n % 2 + 1) * P], w[:, c, :],
                                       start=(c == 0), stop=(c == KC - 1))
                    mm.then_inc(A["qkv"] if n % 2 == 0 else piece_used, 1)
                    for k in turned_beside(n):
                        turn_heads(k)
                    if (n, 1) in ROUNDS:
                        round_of(ROUNDS[n, 1])

                def out_product(half, t, pieces):
                    w = ring[(ATT_BASE + 6 + half) % RING][:].rearrange("q (c f) -> q c f", c=4)
                    if 0 in pieces:
                        has_arrived(pe, ATT_BASE + 6 + half)
                        pe.wait_ge(A["oT_ready"], 2 * half + t + 1)
                        if half == 0:
                            pe.wait_ge(*((A["qkv_out"], 12) if t == 0 else (A["exp"], 2 * UNITS - 2)))
                    for c in pieces:
                        for n in range(2):
                            mm = pe.matmul(psum[:, 2 * t + n, :],
                                           att["qk"][:, t, (4 * half + c) * P:(4 * half + c + 1) * P],
                                           w[:, c, n * 512:(n + 1) * 512], start=(half + c == 0),
                                           stop=(half == 1 and c == 3))
                    if 3 in pieces and (half, t) != (0, 0):
                        mm.then_inc(piece_used if t == 1 else A["first_tile"], 1)

                for j in range(len(ROUNDS), UNITS + LAG):
                    round_of(j)
                out_product(1, 0, range(4))
                turn_out(3)
                out_product(1, 1, range(4))

            def convolution():
                keep_awake(8)
                turn_rows(2)
                all_turned(2, 1)
                pe.wait_ge(conv_params_loaded, 16 * 6)
                pe.transpose(psum[:, 4, 0:40], conv["rows"][0:40, 0, :], ident[0:40, 0:40])
                for b in range(2):
                    mm = pe.transpose(psum[:, 4, 40 + 124 * b:164 + 124 * b], conv["rows"][0:124, 1 + b, :],
                                      ident[0:124, 0:124])
                mm.then_inc(C["params_turned"], 1)
                for b in range(4):
                    for gate in range(2):
                        n = 2 * (b // 2) + gate
                        has_arrived(pe, CONV_BASE + n)
                        w = ring[(CONV_BASE + n) % RING][:].rearrange("q (c f) -> q c f", c=KC)
                        bank = 4 * (b // 2) + 2 * gate + b % 2
                        if bank == 4:
                            pe.wait_ge(C["params"], 1)
                        for jj in range(2):
                            j = 2 * (b % 2) + jj
                            for c in range(KC):
                                mm = pe.matmul(psum[:, bank, jj * T:(jj + 1) * T], w[:, c, j * P:(j + 1) * P],
                                               hT[:, c, :], start=(c == 0), stop=(c == KC - 1))
                        if b % 2 == 1:
                            mm.then_inc(piece_used, 1)
                        elif gate:
                            mm.then_inc(C["glu"], 1)

                def add_to_mean(j):
                    if j == PE_CONV[-1][0]:
                        pe.wait_ge(C["pe_conv_out"], 2)
                    elif j in POOL_CONV:
                        pe.wait_ge(C["pool_conv"], POOL_CONV.index(j) + 1)
                    else:
                        pe.wait_ge(C["dve_conv"], {0: 1, 1: 1, 3: 2, 4: 3, 6: 4}[j])
                    return pe.matmul(psum[:, 4, 0:T], ones, conv["cv"][:, j, :], start=(j == MEAN_ORDER[0]),
                                     stop=(j == MEAN_ORDER[-1]))

                pe.wait_ge(C["u_ready"], 3)
                for j in MEAN_ORDER[:3]:
                    add_to_mean(j)
                pe.wait_ge(C["u_ready"], 4)
                for n, (j, tap) in enumerate(PE_TAPS):
                    pe.wait_ge(C["diag"], n + 1)
                    pe.matmul(psum[:, j % 2, 0:T], conv["diag"][:, n % 4, :], conv["u"][:, j, tap:tap + T],
                              start=(tap == 0), stop=((j, tap + 1) not in PE_TAPS)).then_inc(C["diag_used"], 1)
                for j in MEAN_ORDER[3:]:
                    mm = add_to_mean(j)
                mm.then_inc(C["sum"], 1)
                for j in range(KC):
                    pe.wait_ge(C["squared"], j + 1)
                    mm = pe.matmul(psum[:, 5, 0:T], ones, conv["sq"][:, j, :], start=(j == 0), stop=(j == KC - 1))
                mm.then_inc(C["var"], 1)
                keep_awake(5)
                for t in range(NT):
                    for half in range(2):
                        if t == 0:
                            has_arrived(pe, CONV_BASE + 4 + half)
                        w = ring[(CONV_BASE + 4 + half) % RING][:].rearrange("q (c f) -> q c f", c=4)
                        for c in range(4):
                            pe.wait_ge(C["act"], KC * t + 4 * half + c + 1)
                            for n in range(2):
                                mm = pe.matmul(psum[:, 2 * t + n, :], conv["cv"][:, 4 * half + c, t * P:(t + 1) * P],
                                               w[:, c, n * 512:(n + 1) * 512], start=(half + c == 0),
                                               stop=(half == 1 and c == 3))
                        if t == 1:
                            mm.then_inc(piece_used, 1)
                        elif half == 1:
                            mm.then_inc(C["first_tile"], 1)

            def experts(l):
                m, base = M[l], MOE_BASE[l]

                def start_from_zero(banks):
                    for b in banks:
                        pe.matmul(psum[:, b, :], zero[:, 0:P], zero, start=True, stop=False,
                                  skip_group_check=True)

                def start_first_tile():
                    pe.wait_ge(m["zero"], 1)
                    start_from_zero((0, 1))

                turn_rows(2 * l + 1, start_first_tile)
                if l == 0:
                    pe.wait_ge(params_loaded, PARAM_DMAS * 16)
                for t in range(NT):
                    all_turned(2 * l + 1, t)
                    for c in range(KC):
                        mm = pe.matmul(psum[0:CHOICES, 4 + 2 * t, 0:P], router_w[:, l, c, :],
                                       hT[:, c, t * P:(t + 1) * P], start=(c == 0), stop=(c == KC - 1))
                    mm.then_inc(m["logits"], 1)
                for t in range(NT):
                    pe.wait_ge(m["logits_out"], t + 1)
                    mm = pe.transpose(psum[:, 5, 64 * t:64 * t + CHOICES],
                                      logits_T[:, t * P:(t + 1) * P], ident[0:CHOICES, 0:CHOICES])
                mm.then_inc(m["logits"], 1)
                start_from_zero((2, 3))
                keep_awake(6)
                pe.wait_ge(m["picked"], 1)
                picked = moe["t32"]
                pe.matmul(psum[:, 6, 0:32], before, picked[:, 0, :], start=True, stop=True)
                pe.matmul(psum[:, 6, 32:64], ones, picked[:, 0, :], start=True, stop=False)
                pe.matmul(psum[:, 6, 32:64], before, picked[:, 1, :], start=False, stop=True).then_inc(m["pos"], 1)
                pe.matmul(psum[:, 4, 0:32], ones, picked[:, 0, :], start=True, stop=False)
                pe.matmul(psum[:, 4, 0:32], ones, picked[:, 1, :], start=False, stop=True).then_inc(m["pos"], 1)

                def gather(q, buf, c):
                    pe.wait_ge(m["xg"], 8 * q + (c - 15))
                    for t in range(NT):
                        mm = pe.matmul(psum[:, 7, 0:TRIO * SLOTS], h[:, t, c, :], moe["sel"][:, t, buf, :],
                                       start=(t == 0), stop=(t == NT - 1))
                    mm.then_inc(m["gathered"], 1)

                def up(place, lap, buf, j, bankcol):
                    has_arrived(pe, place, lap=lap)
                    w = ring[place % RING][:].rearrange("q (c f) -> q c f", c=KC)
                    for c in range(KC):
                        for hf in range(2):
                            mm = pe.matmul(psum[hf * SLOTS:(hf + 1) * SLOTS, 4, bankcol:bankcol + 256],
                                           moe["xg"][:, c, buf, j * SLOTS:(j + 1) * SLOTS],
                                           w[:, c, hf * 256:(hf + 1) * 256], start=(c == 0), stop=(c == KC - 1))
                    mm.then_inc(piece_used, 1)

                def turn_hidden(e):
                    pe.wait_ge(m["hid"], e + 1)
                    for j in range(2):
                        mm = pe.transpose(psum[:, 6, j * P:(j + 1) * P], moe["hid"][:, j * P:(j + 1) * P], ident)
                    mm.then_inc(m["hid_turned"], 1)

                def turn_combine(pair, last=False):
                    pe.wait_ge(m["selw"], pair + 1)
                    if not last:
                        pe.wait_ge(m["hidT"], 2 * pair + 2)
                    for t in range(NT):
                        mm = pe.transpose(psum[:, 7 if last else 6, 256 + t * P:256 + (t + 1) * P],
                                          moe["selw"][:, t].rearrange("q a b -> q (a b)"), ident)
                    mm.then_inc(m["comb_turned"], 1)

                def down(e, odd, place, lap):
                    has_arrived(pe, place, lap=lap)
                    pe.wait_ge(m["hidT"], e + 1)
                    if odd:
                        pe.wait_ge(m["outs"], 2 * e)
                    w = ring[place % RING][:].rearrange("q (c f) -> q c f", c=FC)
                    for f in range(FC):
                        for hf in range(2):
                            mm = pe.matmul(psum[hf * SLOTS:(hf + 1) * SLOTS, 5, :],
                                           moe["hidT"][:, f % 2, (f // 2) * SLOTS:(f // 2 + 1) * SLOTS],
                                           w[:, f, hf * 512:(hf + 1) * 512], start=(f == 0), stop=(f == FC - 1))
                    mm.then_inc(piece_used, 1)

                def combine(pair, last=False):
                    pe.wait_ge(m["combT"], pair + 1)
                    pe.wait_ge(m["outs"], 4 * pair + 4)
                    for t in range(NT):
                        for hf in range(2):
                            mm = pe.matmul(psum[:, 2 * hf + t, :], moe["combT"][:, t * P:(t + 1) * P],
                                           moe["outs"][:, hf * 512:(hf + 1) * 512], start=False, stop=last,
                                           skip_group_check=True)
                        if last or t == NT - 1:
                            mm.then_inc(m["combined"], 1)

                def step(i, k):
                    e, q, buf, j = 6 * i + (k + 1), 2 * i + (1 + k // TRIO), (1 + k // TRIO) % 2, k % TRIO
                    at, lap = base + 2 + 3 * k, 2 * i
                    if j == 0:
                        pe.wait_ge(m["xg"], 8 * q - 7)
                        pe.wait_ge(m["sel"], q + 2)
                    pe.wait_ge(m["hid"], e)
                    up(at, lap, buf, j, 0)
                    gather(q + 1, 1 - buf, 3 * j)
                    turn_hidden(e - 1)
                    up(at + 1, lap, buf, j, 256)
                    gather(q + 1, 1 - buf, 3 * j + 1)
                    odd, pair = k % 2 == 1, 3 * i + k // 2
                    if odd:
                        turn_combine(pair)
                    down(e - 1, odd, at + 2, lap)
                    if 3 * j + 2 < KC:
                        gather(q + 1, 1 - buf, 3 * j + 2)
                    if odd:
                        combine(pair)

                def first_gather(n, c):
                    at, at_end = ((2 * SLOTS, TRIO * SLOTS), (0, TRIO * SLOTS))[n]
                    k = KC * n + c
                    if k >= 3:
                        pe.wait_ge(m["first_act" if k % 2 == 0 else "first_dve"], (k - 3) // 2 + 1)
                    for t in range(NT):
                        mm = pe.matmul(psum[:, 5 + k % 3, 0:at_end - at], h[:, t, c, :],
                                       moe["sel"][:, t, n, at:at_end], start=(t == 0), stop=(t == NT - 1))
                    mm.then_inc(m["first_gathered"], 1)

                keep_awake(3)
                pe.wait_ge(m["sel"], 1)
                for c in range(KC):
                    first_gather(0, c)
                pe.wait_ge(m["sel"], 2)
                pe.wait_ge(m["first_act"], 4)
                pe.wait_ge(m["first_dve"], 4)
                pe.wait_ge(m["flag"], 1)
                up(base, 0, 0, 2, 0)
                for c in range(4):
                    first_gather(1, c)
                up(base + 1, 0, 0, 2, 256)
                for c in range(4, KC):
                    first_gather(1, c)
                pe.wait_ge(m["first_act"], 7)
                with pe.Fori(0, 5) as i:
                    for k in range(6):
                        step(i, k)
                e, at = EXPERTS - 1, base + 92
                pe.wait_ge(m["xg"], 8 * 11 - 7)
                pe.wait_ge(m["hid"], e)
                up(at, 0, 1, 0, 0)
                turn_hidden(e - 1)
                up(at + 1, 0, 1, 0, 256)
                turn_combine(EXPERTS // 2 - 1, last=True)
                down(e - 1, False, at + 2, 0)
                turn_hidden(e)
                down(e, True, at + 3, 0)
                combine(EXPERTS // 2 - 1, last=True)

                pe.wait_ge(m["flag"], 1)
                late = pe.value_load(flag_i[0:1, l:l + 1], min_val=0, max_val=T)
                with pe.If(late > SLOTS):
                    with pe.Fori(0, EXPERTS) as e:
                        pe.wait_ge(m["ov_added"], 4 * e + 1)
                        for f in range(FC):
                            pe.wait_ge(m["ov_loaded"], 48 * (FC * e + f + 1))
                            for bank, wt in ((4, "wg"), (5, "wu")):
                                for c in range(KC):
                                    mm = pe.matmul(psum[:, bank, 0:T], ovf[wt][:, c, :], hT[:, c, :], start=(c == 0),
                                                   stop=(c == KC - 1))
                            mm.then_inc(m["ov_gu"], 1)
                            pe.wait_ge(m["ov_hid"], FC * e + f + 1)
                            for t in range(NT):
                                for n in range(2):
                                    mm = pe.matmul(psum[:, 2 * t + n, :], ovf["hid"][:, t * P:(t + 1) * P],
                                                   ovf["wd"][:, n * 512:(n + 1) * 512], start=(f == 0),
                                                   stop=(f == FC - 1))
                            mm.then_inc(m["ov_freed"], 1)

            pe.wait_ge(identity_loaded, 16)
            attention()
            experts(0)
            convolution()
            experts(1)

        @block.scalar
        def _(act):
            brought = [0]

            def bring_table(func):
                nc.scalar.activation(st["spare"][:, brought[0]:brought[0] + 1], ident[:, 0:1], func)
                brought[0] += 1

            def norm(ph):
                if ph == 0:
                    act.wait_ge(identity_loaded, 16)
                bring_table(ACT.Sqrt)
                for t in range(NT):
                    if ph > 0:
                        act.wait_ge(x_ready[ph], 2 * (t + 1))
                    else:
                        act.wait_ge(x_loaded[t], 16)
                    nc.scalar.activation(h[:, t].rearrange("q c k -> q (c k)"), x[:, t, :], ACT.Square,
                                         accum_out=st["ss"][:, t:t + 1]).then_inc(squares, 1)
                    act.wait_ge(squares, NT * ph + t + 1)
                    nc.scalar.activation(st["rms"][:, t:t + 1], st["ss"][:, t:t + 1], ACT.Sqrt, scale=1.0 / D,
                                         bias=eps).then_inc(rms_ready, 1)
                act.wait_ge(*((first_gain_loaded, 16) if ph == 0 else (gains_loaded, 16 * 3)))
                act.wait_ge(rows_turned[ph], 4)
                for j in range(4):
                    ins = nc.scalar.activation(hT[:, 4 + j, P:], psum[:, 7, j * P:(j + 1) * P], ACT.Copy,
                                               scale=norm_gain[:, ph, 4 + j:5 + j])
                ins.then_inc(hT_other[ph], 1)

            def attention():
                norm(0)

                def exps(u):
                    t, hd = unit(u)
                    act.wait_ge(A["neg_max"], u + 1)
                    if u >= 3:
                        act.wait_ge(A["probs_turned"], u - 2)
                    nk = (t + 1) * P
                    for c in range(2):
                        at = 2 * (u % 3) + c
                        nc.scalar.activation(att["probs"][:, u % 3, c, 0:nk], psum[:, 2 + 2 * (u % 2) + c, 0:nk],
                                             ACT.Exp, bias=st["nm"][:, at:at + 1], scale=DH ** -0.5,
                                             accum_out=st["den"][:, at:at + 1]).then_inc(A["exp"], 1)

                def outputs(u):
                    t, hd = unit(u)
                    act.wait_ge(A["pv"], u + 1)
                    nc.scalar.activation(o_rows[:, t, hd * P:(hd + 1) * P], psum[:, 7, 0:P], ACT.Copy).then_inc(
                        A["o_ready"], 1)
                    if u >= 1:
                        act.wait_ge(A["o_ready"], 2 * u)
                    nc.scalar.activation(att["junk"], psum[:, 7, 0:P], ACT.Square,
                                         accum_out=st["oss"][:, u:u + 1]).then_inc(A["o_ready"], 1)

                def probs_out(u):
                    t, hd = unit(u)
                    act.wait_ge(A["probs_turned"], u + 1)
                    nc.scalar.activation(att["pT"][:, 0:t + 1, :].rearrange("q a b -> q (a b)"),
                                         psum[:, 6, 0:(t + 1) * P], ACT.Copy).then_inc(A["pT_ready"], 1)

                def norm_out(b):
                    act.wait_ge(A["o_ms"], b + 1)
                    sl = slice(4 * b, 4 * b + 4)
                    nc.scalar.activation(st["orstd"][:, sl], st["oms"][:, sl], ACT.Sqrt).then_inc(A["o_rstd"], 1)

                def turned_out(b):
                    act.wait_ge(A["o_turned"], b + 1)
                    nc.scalar.activation(att["qk"][:, b % 2, 512 * (b // 2):512 * (b // 2 + 1)], psum[:, 6, :],
                                         ACT.Copy).then_inc(A["oT_ready"], 1)

                def round_of(j):
                    if j < UNITS:
                        exps(j)
                    if LAG <= j < UNITS + LAG:
                        outputs(j - LAG)
                    if 2 <= j < UNITS + 2:
                        probs_out(j - 2)
                    if j in NORM_OUT:
                        norm_out(NORM_OUT[j])
                    if j - 2 in NORM_OUT:
                        turned_out(NORM_OUT[j - 2])

                for n in range(12):
                    if (n, 0) in ROUNDS:
                        round_of(ROUNDS[n, 0])
                    if n % 2 == 0:
                        act.wait_ge(A["qkv"], n // 2 + 1)
                    else:
                        act.wait_ge(piece_used, ATT_BASE + n // 2 + 1)
                    at = IN_ORDER[n // 2] * 512
                    if at < 2 * D:
                        dst = att["qk"][:, n % 2, at:at + 512]
                    else:
                        dst = att["v"][:, n % 2, at - 2 * D:at - 2 * D + 512]
                    nc.scalar.activation(dst, psum[:, n % 2, :], ACT.Copy).then_inc(A["qkv_out"], 1)
                    for k in turned_beside(n):
                        act.wait_ge(A["turned"], turned_product(k) + 1)
                        at = IN_ORDER[k // 2] * 512
                        nc.scalar.activation(att["qk"][:, k % 2, at:at + 512], psum[:, 6, :], ACT.Copy).then_inc(
                            A["turned_out"], 1)
                    if (n, 1) in ROUNDS:
                        round_of(ROUNDS[n, 1])
                    if turned_product(n) is not None:
                        act.wait_ge(A["ms"], turned_product(n) + 1)
                        nc.scalar.activation(st["qrstd"], st["qms"], ACT.Sqrt).then_inc(A["rstd"], 1)
                    if n == 5:
                        act.wait_ge(A["lam_sum"], 1)
                        nc.scalar.activation(st["lam_e"], st["lam_s"], ACT.Exp).then_inc(A["lam_exp"], 1)
                for j in range(len(ROUNDS), UNITS + LAG):
                    round_of(j)
                norm_out(3)
                turned_out(3)

            def convolution():
                norm(2)
                act.wait_ge(C["params"], 1)
                bring_table(ACT.Sigmoid)

                def sigmoids(b):
                    if b % 2 == 0:
                        act.wait_ge(C["glu"], b // 2 + 1)
                    else:
                        act.wait_ge(piece_used, CONV_BASE + b + 1)
                    if b >= 2:
                        act.wait_ge(C["u_ready"], b - 1)
                    for jj in range(2):
                        j = 2 * b + jj
                        nc.scalar.activation(conv["sig"][:, b % 2, jj * T:(jj + 1) * T],
                                             psum[:, 4 * (b // 2) + 2 + b % 2, jj * T:(jj + 1) * T], ACT.Sigmoid,
                                             bias=conv["cols"][:, 8 + j:9 + j]).then_inc(C["sig"], 1)

                def products(i, n):
                    j = POOL_CONV[i]
                    if n == 0:
                        act.wait_ge(C["u_ready"], j // 2 + 1)
                        if i > 0:
                            act.wait_ge(C["pool_conv"], i)
                    if n >= 4:
                        act.wait_ge(C["pool_step"], (PRODUCTS - 1) * i + n - 3)
                    for k in range(min(2, TAPS - 2 * n)):
                        tap = 2 * n + k
                        src, weight = conv["u"][:, j, tap:tap + T], conv["taps"][:, tap, j:j + 1]
                        if tap == 0:
                            ins = nc.scalar.activation(conv["acc"][:, 0, :], src, ACT.Identity, scale=weight,
                                                       bias=conv["cols"][:, 16 + j:17 + j])
                        else:
                            dst = conv["acc"][:, 1, :] if tap == 1 else conv["prod"][:, n % 3, k, :]
                            ins = nc.scalar.activation(dst, src, ACT.Copy, scale=weight)
                    ins.then_inc(C["products"], 1)

                def diagonal(n):
                    j, tap = PE_TAPS[n]
                    if n >= 4:
                        act.wait_ge(C["diag_used"], n - 3)
                    nc.scalar.activation(conv["diag"][:, n % 4, :], ident, ACT.Copy,
                                         scale=conv["taps"][:, tap, j:j + 1]).then_inc(C["diag"], 1)

                def taps_out(i):
                    j, n = PE_CONV[i]
                    act.wait_ge(C["diag_used"], PE_CONV[0][1] * i + n)
                    nc.scalar.activation(conv["cv"][:, j, :], psum[:, j % 2, 0:T], ACT.Identity,
                                         bias=conv["cols"][:, 16 + j:17 + j]).then_inc(C["pe_conv_out"], 1)

                sigmoids(0)
                sigmoids(1)
                for n in range(10):
                    products(0, n)
                sigmoids(2)
                for n in range(10, PRODUCTS):
                    products(0, n)
                products(1, 0)
                products(1, 1)
                sigmoids(3)
                for n in range(2, PRODUCTS):
                    for k in range(3 * (n - 2), min(3 * (n - 1), len(PE_TAPS))):
                        diagonal(k)
                        if k == PE_CONV[0][1] + 3:
                            taps_out(0)
                    products(1, n)
                for k in range(3 * (PRODUCTS - 2), len(PE_TAPS)):
                    diagonal(k)
                taps_out(1)
                bring_table(ACT.Sqrt)
                for j in range(KC):
                    act.wait_ge(C["centred"], j + 1)
                    nc.scalar.activation(conv["sq"][:, j, :], conv["cv"][:, j, :], ACT.Square).then_inc(C["squared"], 1)
                act.wait_ge(C["var"], 1)
                nc.scalar.activation(conv["std"], psum[:, 5, 0:T], ACT.Sqrt, scale=1.0 / D, bias=eps).then_inc(
                    C["std"], 1)
                bring_table(ACT.Silu)
                for t in range(NT):
                    tokens = slice(t * P, (t + 1) * P)
                    for j in range(KC):
                        act.wait_ge(C["scaled"], KC * t + j + 1)
                        nc.scalar.activation(conv["cv"][:, j, tokens], conv["cv"][:, j, tokens], ACT.Silu,
                                             scale=conv["cols"][:, 24 + j:25 + j],
                                             bias=conv["cols"][:, 32 + j:33 + j]).then_inc(C["act"], 1)

            def experts(l):
                m = M[l]
                norm(2 * l + 1)
                for t in range(NT):
                    act.wait_ge(m["logits"], t + 1)
                    nc.scalar.activation(logits_T[:, t * P:(t + 1) * P], psum[0:CHOICES, 4 + 2 * t, 0:P],
                                         ACT.Copy).then_inc(m["logits_out"], 1)
                bring_table(ACT.Exp)
                act.wait_ge(m["group_in"], 1)
                nc.scalar.activation(st["ge"], st["ge"], ACT.Exp).then_inc(m["group_exp"], 1)
                act.wait_ge(m["top_in"], 1)
                nc.scalar.activation(st["e2"], st["dm"], ACT.Exp).then_inc(m["top_exp"], 1)
                bring_table(ACT.Silu)

                def silu(e):
                    act.wait_ge(piece_used, up_at(l, e) + 1)
                    nc.scalar.activation(moe["silu"], psum[:, 4, 0:256], ACT.Silu).then_inc(m["silu"], 1)

                def hidden_out(e):
                    act.wait_ge(m["hid_turned"], e + 1)
                    nc.scalar.activation(moe["hidT"].rearrange("q a b -> q (a b)"), psum[:, 6, 0:256],
                                         ACT.Copy).then_inc(m["hidT"], 1)

                def down_out(e, odd):
                    act.wait_ge(piece_used, down_at(l, e) + 1)
                    for hf in range(2):
                        nc.scalar.activation(moe["outs"][odd * SLOTS:(odd + 1) * SLOTS, hf * 512:(hf + 1) * 512],
                                             psum[hf * SLOTS:(hf + 1) * SLOTS, 5, :], ACT.Copy).then_inc(m["outs"], 1)

                def first_rows_in(k):
                    act.wait_ge(m["first_gathered"], k + 1)
                    dst, bank = first_rows(k)
                    nc.scalar.activation(dst, bank, ACT.Copy, scale=norm_gain[:, 2 * l + 1, k % KC:k % KC + 1]).then_inc(
                        m["first_act"], 1)

                for k in (1, 3, 5, 7, 9, 11):
                    first_rows_in(k)
                silu(0)
                first_rows_in(13)
                with act.Fori(0, 5) as i:
                    for k in range(6):
                        hidden_out(6 * i + k)
                        silu(6 * i + (k + 1))
                        down_out(6 * i + k, k % 2)
                hidden_out(EXPERTS - 2)
                silu(EXPERTS - 1)
                down_out(EXPERTS - 2, 0)
                hidden_out(EXPERTS - 1)
                down_out(EXPERTS - 1, 1)

                act.wait_ge(m["flag"], 1)
                late = act.value_load(flag_i[0:1, l:l + 1], min_val=0, max_val=T)
                with act.If(late > SLOTS):
                    with act.Fori(0, EXPERTS) as e:
                        for f in range(FC):
                            act.wait_ge(m["ov_gu"], FC * e + f + 1)
                            nc.scalar.activation(ovf["silu"], psum[:, 4, 0:T], ACT.Silu).then_inc(m["ov_silu"], 1)

            attention()
            experts(0)
            convolution()
            experts(1)

        @block.vector
        def _(dve):
            done = [0]
            V = nc.vector

            def link(ins):
                done[0] += 1
                ins.then_inc(dve_step, 1)
                dve.wait_ge(dve_step, done[0])

            def wide(ap, axis, shape):
                return ap.unsqueeze(axis).to_broadcast(shape)

            def normalise(ph, t):
                dve.wait_ge(rms_ready, NT * ph + t + 1)
                link(V.reciprocal(st["rstd"][:, t:t + 1], st["rms"][:, t:t + 1]))
                V.tensor_scalar(h[:, t].rearrange("q c k -> q k c"), x[:, t, :].rearrange("q (k c) -> q k c", c=KC),
                                st["rstd"][:, t:t + 1], None, ALU.mult).then_inc(rows_ready[ph], 1)

            def turned_in(ph, t):
                dve.wait_ge(*((first_gain_loaded, 16) if ph == 0 else (gains_loaded, 16 * 3)))
                for half in range(2 - t):
                    dve.wait_ge(rows_turned[ph], 2 * t + half + 1)
                    ins = V.tensor_tensor(hT[:, 4 * half:4 * half + 4, t * P:(t + 1) * P],
                                          psum[:, 4 + 2 * t + half, :].rearrange("q (a b) -> q a b", a=4),
                                          wide(norm_gain[:, ph, 4 * half:4 * half + 4], 2, [P, 4, P]), ALU.mult)
                ins.then_inc(hT_ready[ph], 1)

            def norm(ph):
                for t in range(NT):
                    normalise(ph, t)
                for t in range(NT):
                    turned_in(ph, t)

            def join(ph, first_tile, pieces):
                for t in range(NT):
                    if t == 0:
                        dve.wait_ge(first_tile, 1)
                    else:
                        dve.wait_ge(piece_used, pieces)
                    for n in range(2):
                        cols = slice(n * 512, (n + 1) * 512)
                        V.tensor_tensor(x[:, t, cols], x[:, t, cols], psum[:, 2 * t + n, :], ALU.add).then_inc(
                            x_ready[ph], 1)
                    if t == 1:
                        turned_in(ph, 0)
                    normalise(ph, t)
                    if t == 0:
                        V.memset(zero, 0.0).then_inc(M[ph // 2]["zero"], 1)
                turned_in(ph, 1)

            def attention():
                norm(0)
                tmp = att["tmp"]
                dve.wait_ge(consts_loaded, 16)
                dve.wait_ge(att_params_loaded, 16 * 2)

                def norm_heads(n):
                    r, t, at = turned_product(n), n % 2, IN_ORDER[n // 2] * 512
                    q = att["qk"][:, t, at:at + 512]
                    q3 = q.rearrange("q (a b) -> q a b", a=8)
                    dve.wait_ge(A["qkv_out"], n + 1)
                    link(V.tensor_tensor(att["sq"], q, q, ALU.mult))
                    link(V.tensor_reduce(st["qms"], att["sq"].rearrange("q (a b) -> q a b", a=8), AX, ALU.add))
                    link(V.tensor_scalar(st["qms"], st["qms"], 1.0 / DH, EPS, ALU.mult, ALU.add))
                    V.reciprocal(st["qms"], st["qms"]).then_inc(A["ms"], 1)
                    link(V.tensor_tensor(q3, q3, wide(att["gains"][:, at // D, :], 1, [P, 8, DH]), ALU.mult))
                    dve.wait_ge(A["rstd"], r + 1)
                    link(V.tensor_tensor(q3, q3, wide(st["qrstd"], 2, [P, 8, DH]), ALU.mult))
                    x1, x2 = q3[:, :, 0:ROT], q3[:, :, ROT:2 * ROT]
                    cos = wide(con[:, C_COS + ROT * t:C_COS + ROT * (t + 1)], 1, [P, 8, ROT])
                    sin = wide(con[:, C_SIN + ROT * t:C_SIN + ROT * (t + 1)], 1, [P, 8, ROT])
                    a = [tmp[:, k, :].rearrange("q (a b) -> q a b", a=8) for k in range(4)]
                    V.tensor_tensor(a[0], x1, cos, ALU.mult)
                    V.tensor_tensor(a[1], x2, sin, ALU.mult)
                    V.tensor_tensor(a[2], x2, cos, ALU.mult)
                    link(V.tensor_tensor(a[3], x1, sin, ALU.mult))
                    V.tensor_tensor(x1, a[0], a[1], ALU.subtract)
                    V.tensor_tensor(x2, a[2], a[3], ALU.add).then_inc(A["rotated"], 1)
                    dve.wait_ge(A["rotated"], r + 1)

                def biggest(u):
                    t, hd = unit(u)
                    dve.wait_ge(A["scores"], u + 1)
                    nm = st["nm"][:, 2 * (u % 3):2 * (u % 3) + 2]
                    bank = 2 + 2 * (u % 2)
                    V.tensor_reduce(nm, psum[:, bank:bank + 2, 0:(t + 1) * P], AX, ALU.max).then_inc(A["max"], 1)
                    dve.wait_ge(A["max"], u + 1)
                    V.tensor_scalar(nm, nm, -DH ** -0.5, None, ALU.mult).then_inc(A["neg_max"], 1)

                def mix(u):
                    t, hd = unit(u)
                    nk = (t + 1) * P
                    den = st["den"][:, 2 * (u % 3):2 * (u % 3) + 2]
                    one, other = att["probs"][:, u % 3, 0, 0:nk], att["probs"][:, u % 3, 1, 0:nk]
                    dve.wait_ge(A["exp"], 2 * u + 2)
                    link(V.reciprocal(den, den))
                    link(V.tensor_scalar(other, other, den[:, 1:2], st["neglam"], ALU.mult, ALU.mult))
                    V.scalar_tensor_tensor(out=one, in0=one, scalar=den[:, 0:1], in1=other, op0=ALU.mult,
                                           op1=ALU.add).then_inc(A["mixed"], 1)

                def norm_out(b):
                    dve.wait_ge(A["o_ready"], 8 * (b + 1))
                    sl = slice(4 * b, 4 * b + 4)
                    link(V.tensor_scalar(st["oms"][:, sl], st["oss"][:, sl], 1.0 / P, EPS, ALU.mult, ALU.add))
                    V.reciprocal(st["oms"][:, sl], st["oms"][:, sl]).then_inc(A["o_ms"], 1)
                    o3 = o_rows[:, b % 2, 512 * (b // 2):512 * (b // 2 + 1)].rearrange("q (a b) -> q a b", a=4)
                    link(V.scalar_tensor_tensor(out=o3, in0=o3, scalar=1.0 - LAMBDA_INIT,
                                                in1=wide(att["subln"], 1, [P, 4, P]), op0=ALU.mult, op1=ALU.mult))
                    dve.wait_ge(A["o_rstd"], b + 1)
                    V.tensor_tensor(o3, o3, wide(st["orstd"][:, sl], 2, [P, 4, P]), ALU.mult).then_inc(A["o_normed"], 1)

                def round_of(j):
                    if j < UNITS:
                        biggest(j)
                    if 1 <= j < UNITS + 1:
                        mix(j - 1)
                    if j in NORM_OUT:
                        norm_out(NORM_OUT[j])

                for n in range(12):
                    for half in range(2):
                        if (n, half) in ROUNDS:
                            round_of(ROUNDS[n, half])
                    if turned_product(n) is not None:
                        norm_heads(n)
                    if n == 4:
                        dve.wait_ge(lambda_params_loaded, 16 * 5)
                        for c in range(2):
                            link(V.tensor_tensor(tmp[:, c, :], att["lam"][:, 2 * c, :], att["lam"][:, 2 * c + 1, :],
                                                 ALU.mult))
                        V.tensor_reduce(st["lam_s"], tmp[:, 0:2, :], AX, ALU.add).then_inc(A["lam_sum"], 1)
                        dve.wait_ge(A["lam_exp"], 1)
                        link(V.tensor_tensor(st["neglam"], st["lam_e"][:, 1:2], st["lam_e"][:, 0:1], ALU.subtract))
                        link(V.tensor_scalar(st["neglam"], st["neglam"], -LAMBDA_INIT, None, ALU.add))
                for j in range(len(ROUNDS), UNITS + LAG):
                    round_of(j)
                norm_out(3)
                join(1, A["first_tile"], ATT_BASE + 8)

            def convolution():
                link(V.memset(conv["u"][:, :, 0:TAPS - 1], 0.0))
                norm(2)
                dve.wait_ge(C["params_turned"], 1)
                V.tensor_copy(conv["cols"], psum[:, 4, 0:40])
                V.tensor_copy(conv["taps"].rearrange("q a b -> q (a b)"), psum[:, 4, 40:288]).then_inc(C["params"], 1)
                dve.wait_ge(C["params"], 1)
                for t in range(NT):
                    V.tensor_tensor(x[:, t, :], x[:, t, :], conv["b_out"], ALU.add)

                def glu(b):
                    dve.wait_ge(C["sig"], 2 * b + 2)
                    for jj in range(2):
                        j = 2 * b + jj
                        ins = V.scalar_tensor_tensor(
                            out=conv["u"][:, j, TAPS - 1:], in0=psum[:, 4 * (b // 2) + b % 2, jj * T:(jj + 1) * T],
                            scalar=conv["cols"][:, j:j + 1], in1=conv["sig"][:, b % 2, jj * T:(jj + 1) * T],
                            op0=ALU.add, op1=ALU.mult)
                    ins.then_inc(C["u_ready"], 1)
                    dve.wait_ge(C["u_ready"], b + 1)

                def taps(tiles, n):
                    for k in range(n):
                        for j, first in tiles:
                            src, tap = conv["u"][:, j, first + k:first + k + T], first + k
                            weight = conv["taps"][:, tap, j:j + 1]
                            if tap == 0:
                                ins = V.tensor_scalar(conv["cv"][:, j, :], src, weight, conv["cols"][:, 16 + j:17 + j],
                                                      ALU.mult, ALU.add)
                            else:
                                ins = V.scalar_tensor_tensor(out=conv["cv"][:, j, :], in0=src, scalar=weight,
                                                             in1=conv["cv"][:, j, :], op0=ALU.mult, op1=ALU.add)
                            done[0] += 1
                            ins.then_inc(dve_step, 1)
                            dve.wait_ge(dve_step, done[0] + 1 - len(tiles))
                    dve.wait_ge(dve_step, done[0])

                def tiles_done():
                    V.memset(st["mx"], 0.0).then_inc(C["dve_conv"], 1)

                glu(0)
                taps(((0, 0), (1, 0)), 14)
                glu(1)
                taps(((0, 14), (1, 14)), 17)
                tiles_done()
                taps(((3, 0),), 4)
                glu(2)
                taps(((3, 4), (4, 0)), 13)
                glu(3)
                taps(((3, 17), (4, 13)), 14)
                tiles_done()
                dve.wait_ge(C["pe_conv_out"], 1)
                taps(((4, 27), (6, PE_CONV[0][1])), 4)
                tiles_done()
                taps(((6, PE_CONV[0][1] + 4),), TAPS - 4 - PE_CONV[0][1])
                tiles_done()
                dve.wait_ge(C["sum"], 1)
                link(V.tensor_scalar(conv["mean"], psum[:, 4, 0:T], 1.0 / D, None, ALU.mult))
                dve.wait_ge(C["dve_conv"], 4)
                dve.wait_ge(C["pool_conv"], len(POOL_CONV))
                dve.wait_ge(C["pe_conv_out"], 2)
                for j in range(KC):
                    V.tensor_tensor(conv["cv"][:, j, :], conv["cv"][:, j, :], conv["mean"], ALU.subtract).then_inc(
                        C["centred"], 1)
                dve.wait_ge(C["centred"], KC)
                dve.wait_ge(C["std"], 1)
                for t in range(NT):
                    tokens = slice(t * P, (t + 1) * P)
                    link(V.reciprocal(conv["rstd"][:, tokens], conv["std"][:, tokens]))
                    for j in range(KC):
                        V.tensor_tensor(conv["cv"][:, j, tokens], conv["cv"][:, j, tokens], conv["rstd"][:, tokens],
                                        ALU.mult).then_inc(C["scaled"], 1)
                join(3, C["first_tile"], CONV_BASE + 6)

            def route(l, select):
                m = M[l]
                if l == 0:
                    dve.wait_ge(params_loaded, 16 * PARAM_DMAS)
                lg, ml, one, two, t32 = (moe[n] for n in ("logit", "ml", "one", "two", "t32"))
                dve.wait_ge(m["logits"], 3)
                link(V.tensor_tensor(lg, psum[:, 5, 0:128].rearrange("q (a b) -> q a b", a=2)[:, :, 0:CHOICES],
                                     wide(router_b[:, l, :], 1, [P, NT, CHOICES]), ALU.add))
                gl, pick = lg[:, :, 0:GROUPS], st["pick"]
                link(V.tensor_reduce(st["mx"], gl, AX, ALU.max))
                rev4 = wide(rev[:, EXPERTS - GROUPS:EXPERTS], 1, [P, NT, GROUPS])
                for t in range(NT):
                    ins = V.scalar_tensor_tensor(out=pick[:, t, :], in0=gl[:, t, :],
                                                 scalar=st["mx"][:, t:t + 1], in1=rev4[:, t, :], op0=ALU.is_equal,
                                                 op1=ALU.mult)
                V.tensor_tensor(st["ge"], gl, wide(st["mx"], 2, [P, NT, GROUPS]), ALU.subtract).then_inc(
                    m["group_in"], 1)
                dve.wait_ge(m["group_in"], 1)
                link(V.tensor_reduce(st["first"], pick, AX, ALU.max))
                link(V.tensor_tensor(pick, rev4, wide(st["first"], 2, [P, NT, GROUPS]), ALU.is_equal))
                link(V.tensor_scalar(pick, pick, BIG, -BIG, ALU.mult, ALU.add))
                link(V.tensor_tensor(ml.rearrange("q t (g e) -> q t g e", g=GROUPS),
                                     lg[:, :, GROUPS:].rearrange("q t (g e) -> q t g e", g=GROUPS),
                                     wide(pick, 3, [P, NT, GROUPS, PER_GROUP]), ALU.add))

                rev32 = wide(rev, 1, [P, NT, EXPERTS])
                def first_of_max(mx, chosen):
                    link(V.tensor_reduce(mx, ml, AX, ALU.max))
                    for t in range(NT):
                        ins = V.scalar_tensor_tensor(out=chosen[:, t, :], in0=ml[:, t, :], scalar=mx[:, t:t + 1],
                                                     in1=rev, op0=ALU.is_equal, op1=ALU.mult)
                    link(ins)
                    link(V.tensor_reduce(st["first"], chosen, AX, ALU.max))
                    link(V.tensor_tensor(chosen, rev32, wide(st["first"], 2, [P, NT, EXPERTS]), ALU.is_equal))

                first_of_max(st["m1"], one)
                link(V.scalar_tensor_tensor(out=ml, in0=one, scalar=-3 * BIG, in1=ml, op0=ALU.mult, op1=ALU.add))
                first_of_max(st["m2"], two)
                V.tensor_tensor(t32, one, two, ALU.add).then_inc(m["picked"], 1)
                V.tensor_tensor(st["dm"], st["m2"], st["m1"], ALU.subtract).then_inc(m["top_in"], 1)
                dve.wait_ge(m["group_exp"], 1)
                link(V.tensor_reduce(st["gp"], st["ge"], AX, ALU.add))
                link(V.reciprocal(st["gp"], st["gp"]))
                comb = moe["comb"][:, :, FRONT:FRONT + EXPERTS]
                posm = moe["posm"][:, :, FRONT:FRONT + EXPERTS]
                dve.wait_ge(m["pos"], 1)
                dve.wait_ge(m["picked"], 1)
                link(V.scalar_tensor_tensor(out=ml, in0=psum[:, 6, 0:64].rearrange("q (a b) -> q a b", a=2), scalar=1.0,
                                            in1=t32, op0=ALU.add, op1=ALU.mult))
                link(V.tensor_scalar(posm, ml, -1.0, None, ALU.add))
                for q in range(2):
                    select(q, q)

                def first_weight():
                    dve.wait_ge(m["top_exp"], 1)
                    link(V.tensor_scalar(st["m1"], st["e2"], 1.0, None, ALU.add))
                    link(V.reciprocal(st["m1"], st["m1"]))
                    link(V.tensor_tensor(st["m1"], st["m1"], st["gp"], ALU.mult))

                def weights():
                    link(V.tensor_tensor(st["m2"], st["m1"], st["e2"], ALU.mult))
                    V.tensor_tensor(one, one, wide(st["m1"], 2, [P, NT, EXPERTS]), ALU.mult)
                    link(V.tensor_tensor(two, two, wide(st["m2"], 2, [P, NT, EXPERTS]), ALU.mult))
                    link(V.tensor_tensor(comb, one, two, ALU.add))

                def count():
                    dve.wait_ge(m["pos"], 2)
                    link(V.tensor_reduce(st["mx"][:, 0:1], psum[:, 4, 0:32], AX, ALU.max))
                    V.tensor_copy(flag_i[:, l:l + 1], st["mx"][:, 0:1]).then_inc(m["flag"], 1)

                def late():
                    link(V.tensor_scalar(two, posm, float(SLOTS), None, ALU.is_ge))
                    link(V.tensor_tensor(moe["late"], two, comb, ALU.mult))

                return first_weight, weights, count, late

            def experts(l):
                m = M[l]
                def select(q, buf):
                    V.tensor_tensor(moe["sel"][:, :, buf, :].rearrange("q t (a b) -> q t a b", a=TRIO),
                                    iota.unsqueeze(1).unsqueeze(1).to_broadcast([P, NT, TRIO, SLOTS]),
                                    wide(moe["posm"][:, :, bass.ds(TRIO * q, TRIO)], 3, [P, NT, TRIO, SLOTS]),
                                    ALU.is_equal).then_inc(m["sel"], 1)

                V.memset(moe["posm"], -1.0)
                link(V.memset(moe["comb"], 0.0))
                small_steps = route(l, select)

                def select_weighted(pair, at):
                    V.tensor_tensor(moe["selw"], iota.unsqueeze(1).unsqueeze(1).to_broadcast([P, NT, 2, SLOTS]),
                                    wide(moe["posm"][:, :, bass.ds(at, 2)], 3, [P, NT, 2, SLOTS]),
                                    ALU.is_equal).then_inc(m["pair"], 1)
                    dve.wait_ge(m["pair"], pair + 1)
                    V.tensor_tensor(moe["selw"], moe["selw"],
                                    wide(moe["comb"][:, :, bass.ds(at, 2)], 3, [P, NT, 2, SLOTS]),
                                    ALU.mult).then_inc(m["selw"], 1)

                def rows_in(q, buf, c):
                    dve.wait_ge(m["gathered"], 8 * q + (c - 15))
                    V.tensor_scalar(moe["xg"][:, c, buf, :], psum[:, 7, 0:TRIO * SLOTS],
                                    norm_gain[:, 2 * l + 1, c:c + 1], None, ALU.mult).then_inc(m["xg"], 1)

                def hidden(e):
                    dve.wait_ge(m["silu"], e + 1)
                    V.tensor_tensor(moe["hid"], moe["silu"], psum[:, 4, 256:512], ALU.mult).then_inc(m["hid"], 1)

                def combine_in(pair, bank=6):
                    dve.wait_ge(m["comb_turned"], pair + 1)
                    V.tensor_copy(moe["combT"], psum[:, bank, 256:512]).then_inc(m["combT"], 1)

                def first_rows_in(k):
                    dve.wait_ge(m["first_gathered"], k + 1)
                    dst, bank = first_rows(k)
                    V.tensor_scalar(dst, bank, norm_gain[:, 2 * l + 1, k % KC:k % KC + 1], None, ALU.mult).then_inc(
                        m["first_dve" if k < 15 else "xg"], 1)

                for k in (0, 2, 4, 6, 8, 10):
                    first_rows_in(k)
                    if k < 8:
                        small_steps[k // 2]()
                hidden(0)
                for k in (12, 14, 15):
                    first_rows_in(k)
                select(2, 0)
                with dve.Fori(0, 5) as i:
                    for k in range(6):
                        j = k % TRIO
                        q = 2 * i + (1 + k // TRIO)
                        buf = (1 + k // TRIO) % 2
                        rows_in(q + 1, 1 - buf, 3 * j)
                        hidden(6 * i + (k + 1))
                        rows_in(q + 1, 1 - buf, 3 * j + 1)
                        if k % 2 == 0:
                            select_weighted(3 * i + k // 2, 6 * i + (k + FRONT))
                        else:
                            combine_in(3 * i + k // 2)
                        if 3 * j + 2 < KC:
                            rows_in(q + 1, 1 - buf, 3 * j + 2)
                        if j == TRIO - 1:
                            select(q + 2, buf)
                select_weighted(EXPERTS // 2 - 1, EXPERTS - 2 + FRONT)
                hidden(EXPERTS - 1)
                combine_in(EXPERTS // 2 - 1, 7)
                late = dve.value_load(flag_i[0:1, l:l + 1], min_val=0, max_val=T)
                for t in range(NT):
                    dve.wait_ge(m["combined"], EXPERTS // 2 + t)
                    for hf in range(2):
                        cols = slice(hf * 512, (hf + 1) * 512)
                        ins = V.tensor_tensor(x[:, t, cols], x[:, t, cols], psum[:, 2 * hf + t, :], ALU.add)
                link(ins)

                with dve.If(late > SLOTS):
                    V.memset(st["m1"], 0.0).then_inc(m["ov_freed"], 1)
                    V.memset(st["m2"], 0.0).then_inc(m["ov_added"], 1)
                    with dve.Fori(0, EXPERTS) as e:
                        for f in range(FC):
                            dve.wait_ge(m["ov_silu"], FC * e + f + 1)
                            V.tensor_tensor(ovf["hid"], ovf["silu"], psum[:, 5, 0:T], ALU.mult).then_inc(m["ov_hid"], 1)
                        dve.wait_ge(m["ov_freed"], FC * e + (FC + 1))
                        dve.wait_ge(m["ov_added"], 4 * e + 1)
                        for t in range(NT):
                            for n in range(2):
                                cols = slice(n * 512, (n + 1) * 512)
                                V.scalar_tensor_tensor(out=x[:, t, cols], in0=psum[:, 2 * t + n, :],
                                                       scalar=moe["late"][:, t, bass.ds(e, 1)], in1=x[:, t, cols],
                                                       op0=ALU.mult, op1=ALU.add).then_inc(m["ov_added"], 1)
                V.memset(st["gp"], 0.0).then_inc(x_ready[2 * l + 2], 4)

            attention()
            experts(0)
            convolution()
            experts(1)

        @block.gpsimd
        def _(pool):
            def overflow(l):
                m = M[l]
                pool.wait_ge(m["flag"], 1)
                late = pool.value_load(flag_i[0:1, l:l + 1], min_val=0, max_val=T)
                with pool.If(late > SLOTS):
                    with pool.Fori(0, EXPERTS) as e:
                        for f in range(FC):
                            pool.wait_ge(m["ov_freed"], FC * e + (f + 1))
                            cols = slice(f * P, (f + 1) * P)
                            for w, dst in (("moe_w_gate", "wg"), ("moe_w_up", "wu")):
                                pool.dma_start(ovf[dst], p[w][l, bass.ds(e, 1), :, cols].rearrange(
                                    "o (q c) f -> q (o c) f", c=KC)).then_inc(m["ov_loaded"], 16)
                            pool.dma_start(ovf["wd"], p["moe_w_down"][l, bass.ds(e, 1), cols, :].rearrange(
                                "o q f -> q (o f)")).then_inc(m["ov_loaded"], 16)

            def convolution():
                for i, j in enumerate(POOL_CONV):
                    for n in range(1, PRODUCTS):
                        pool.wait_ge(C["products"], PRODUCTS * i + n + 1)
                        if n >= 2:
                            pool.wait_ge(C["pool_step"], (PRODUCTS - 1) * i + n - 1)
                        both = slice(0, 2 if n < PRODUCTS - 1 else 1)
                        nc.gpsimd.tensor_tensor(conv["acc"][:, both, :], conv["acc"][:, both, :],
                                                conv["prod"][:, n % 3, both, :], ALU.add).then_inc(C["pool_step"], 1)
                    pool.wait_ge(C["pool_step"], (PRODUCTS - 1) * (i + 1))
                    nc.gpsimd.tensor_tensor(conv["cv"][:, j, :], conv["acc"][:, 0, :], conv["acc"][:, 1, :],
                                            ALU.add).then_inc(C["pool_conv"], 1)

            pool.wait_ge(x_ready[1], 4)
            for name, row, n in (("conv_b_in", 0, 16), ("conv_dw_b", 16, 8), ("conv_ln_g", 24, 8),
                                 ("conv_ln_b", 32, 8)):
                pool.dma_start(conv["rows"][row:row + n, 0, :], p[name].rearrange(
                    "o (j k) -> (o j) k", k=P)).then_inc(conv_params_loaded, 16)
            taps = p["conv_dw_w"][0].rearrange("w (j k) -> (w j) k", k=P)
            pool.dma_start(conv["rows"][0:124, 1:3, :], taps.rearrange("(b r) k -> r b k", b=2)).then_inc(
                conv_params_loaded, 16)
            pool.dma_start(conv["b_out"], p["conv_b_out"][0].partition_broadcast(P)).then_inc(
                conv_params_loaded, 16)
            overflow(0)
            convolution()
            overflow(1)


_PARAMS = ["attn_norm", "diff_w_in", "diff_q_gain", "diff_k_gain", "diff_lambda_q1", "diff_lambda_k1", "diff_lambda_q2",
           "diff_lambda_k2", "diff_subln", "diff_w_out", "conv_norm", "conv_w_in", "conv_b_in", "conv_dw_w",
           "conv_dw_b", "conv_ln_g", "conv_ln_b", "conv_w_out", "conv_b_out", "ffn_norm", "router_group_w",
           "router_group_b", "router_expert_w", "router_expert_b", "moe_w_gate", "moe_w_up", "moe_w_down"]


def constants():
    import numpy as np

    con = np.zeros((P, C_END), np.float32)
    r = np.arange(P)
    con[:, C_IDENT:C_IDENT + P] = np.eye(P)
    con[:, C_EPS] = EPS
    con[:, C_BEFORE:C_BEFORE + P] = r[:, None] < r[None, :]
    con[:, C_ONES:C_ONES + P] = 1
    con[:, C_IOTA:C_IOTA + SLOTS] = np.arange(SLOTS)
    con[:, C_REV:C_REV + EXPERTS] = EXPERTS - np.arange(EXPERTS)
    con[[0, 64], C_EARLY:C_EARLY + 64] = 1
    con[[0, 64], C_HIDE:C_HIDE + 64] = -BIG
    inv_freq = np.float32(500000.0) ** (-np.arange(0, 2 * ROT, 2, dtype=np.float32) / np.float32(2 * ROT))
    ang = np.arange(T, dtype=np.float32)[:, None] * inv_freq[None, :]
    for t in range(NT):
        con[:, C_COS + ROT * t:C_COS + ROT * (t + 1)] = np.cos(ang[t * P:(t + 1) * P])
        con[:, C_SIN + ROT * t:C_SIN + ROT * (t + 1)] = np.sin(ang[t * P:(t + 1) * P])
    return con


def kernel(**inputs):
    import numpy as _np
    import concourse.bacc as _bacc
    from concourse import mybir as _mybir
    from concourse.bass_utils import run_bass_kernel_spmd as _run

    nc = _bacc.Bacc("TRN2", target_bir_lowering=False, num_devices=1)
    arrays = {"in_x": _np.ascontiguousarray(inputs["x"]), "in_constants": constants()}
    for name in _PARAMS:
        arrays["in_" + name] = _np.ascontiguousarray(inputs[name])
    aps = {k: nc.dram_tensor(k, a.shape, _mybir.dt.float32, kind="ExternalInput").ap() for k, a in arrays.items()}
    out = nc.dram_tensor("out", (1, T, D), _mybir.dt.float32, kind="ExternalOutput").ap()
    build(nc, aps["in_x"], aps["in_constants"], {n: aps["in_" + n] for n in _PARAMS}, out)
    r = _run(nc, [arrays], core_ids=[0])
    return r.results[0]["out"]
```
